# Optimizing a Trainium2 kernel written in Bass

```python
import math
import jax, jax.numpy as jnp
from jax import lax
import numpy as np

D_MODEL = 1024
BATCH = 1
SEQ = 512
DEPTH = 1

D_PLE = 256
M_HEADS = 4
M_QK = 128
M_V = 256
M_WIDTH = M_HEADS * M_V
M_CHUNK = 64
CONV_W = 4
A_HEADS = 8
A_DH = 64
A_WIDTH = A_HEADS * A_DH
IDX_HEADS = 8
IDX_DH = 64
TOPK_MAX = 256
Q_BLOCK = 128
REL_BUCKETS = 32
REL_MAX_DIST = 128
D_MIX = M_WIDTH + A_WIDTH
EPS = 1e-6

PROJ_SIZES = [
    M_HEADS * M_QK,
    M_HEADS * M_QK,
    M_WIDTH,
    M_WIDTH,
    M_WIDTH,
    2 * M_HEADS,
    A_WIDTH,
    A_WIDTH,
    A_WIDTH,
    A_WIDTH,
    IDX_HEADS * IDX_DH,
    IDX_DH,
    IDX_HEADS,
]
PROJ_TOTAL = int(sum(PROJ_SIZES))
SPLIT_POINTS = [int(v) for v in np.cumsum(PROJ_SIZES)[:-1]]


def rmsnorm(x, g):
    xf = x.astype(jnp.float32)
    y = xf * lax.rsqrt(jnp.mean(xf * xf, axis=-1, keepdims=True) + EPS)
    return (y * g.astype(jnp.float32)).astype(x.dtype)

def causal_dwconv(x, w):
    S = x.shape[1]
    xp = jnp.pad(x, ((0, 0), (CONV_W - 1, 0), (0, 0)))
    y = xp[:, 0:S] * w[0]
    for j in range(1, CONV_W):
        y = y + xp[:, j:j + S] * w[j]
    return y

def mlstm_chunkwise(q, k, v, log_i, log_f):
    f32 = jnp.float32
    B, S, H, Dk = q.shape
    Dv = v.shape[-1]
    L = M_CHUNK
    NC = S // L

    def to_chunks(a):
        return a.reshape((B, NC, L) + a.shape[2:]).swapaxes(0, 1)

    qc = to_chunks(q.astype(f32))
    kc = to_chunks(k.astype(f32) * (Dk ** -0.5))
    vc = to_chunks(v.astype(f32))
    ic = to_chunks(log_i.astype(f32))
    fc = to_chunks(log_f.astype(f32))
    causal = jnp.tril(jnp.ones((L, L), dtype=bool))

    def step(carry, inp):
        C, n, m = carry
        q_, k_, v_, li, lf = inp
        b = jnp.cumsum(lf, axis=1).transpose(0, 2, 1)
        li_h = li.transpose(0, 2, 1)
        D = b[:, :, :, None] - b[:, :, None, :] + li_h[:, :, None, :]
        D = jnp.where(causal, D, -jnp.inf)
        inter = b + m[:, :, None]
        m_t = jnp.maximum(inter, D.max(-1))
        s = jnp.einsum('blhd,bshd->bhls', q_, k_) * jnp.exp(D - m_t[..., None])
        w_inter = jnp.exp(inter - m_t)
        num = (jnp.einsum('bhls,bshv->blhv', s, v_)
               + w_inter.transpose(0, 2, 1)[..., None] * jnp.einsum('blhd,bhdv->blhv', q_, C))
        den = s.sum(-1) + w_inter * jnp.einsum('blhd,bhd->bhl', q_, n)
        den = jnp.maximum(jnp.abs(den), jnp.exp(-m_t))
        h = num / den.transpose(0, 2, 1)[..., None]
        b_L = b[:, :, -1]
        g = b_L[:, :, None] - b + li_h
        m_new = jnp.maximum(b_L + m, g.max(-1))
        wk = jnp.exp(g - m_new[..., None])
        decay = jnp.exp(b_L + m - m_new)
        C_new = decay[..., None, None] * C + jnp.einsum('bhs,bshd,bshv->bhdv', wk, k_, v_)
        n_new = decay[..., None] * n + jnp.einsum('bhs,bshd->bhd', wk, k_)
        return (C_new, n_new, m_new), h

    init = (jnp.zeros((B, H, Dk, Dv), f32), jnp.zeros((B, H, Dk), f32), jnp.zeros((B, H), f32))
    _, hs = lax.scan(step, init, (qc, kc, vc, ic, fc))
    return hs.swapaxes(0, 1).reshape(B, S, H, Dv)

def t5_bucket(dist):
    max_exact = REL_BUCKETS // 2
    large = max_exact + (jnp.log(jnp.maximum(dist, 1).astype(jnp.float32) / max_exact)
                         / math.log(REL_MAX_DIST / max_exact) * (REL_BUCKETS - max_exact)).astype(jnp.int32)
    large = jnp.minimum(large, REL_BUCKETS - 1)
    return jnp.where(dist < max_exact, dist, large)

def dsa_attention(q, k, v, iq, ik, iw, rel_bias):
    B, S, H, dh = q.shape
    topk = min(TOPK_MAX, S // 4)
    NB = S // Q_BLOCK
    key_pos = jnp.arange(S)
    iq = iq * (IDX_DH ** -0.5)
    iw = iw * (IDX_HEADS ** -0.5)

    def blockify(a):
        return a.reshape((B, NB, Q_BLOCK) + a.shape[2:]).swapaxes(0, 1)

    def one_block(args):
        qb, iqb, iwb, bi = args
        t = bi * Q_BLOCK + jnp.arange(Q_BLOCK)
        sc = jax.nn.relu(jnp.einsum('bthd,bsd->bths', iqb, ik))
        score = jnp.einsum('bths,bth->bts', sc, iwb).astype(jnp.float32)
        causal = key_pos[None, :] <= t[:, None]
        score = jnp.where(causal[None], score, -jnp.inf)
        _, idx = lax.top_k(score, topk)
        k_sel = jax.vmap(lambda kb, ib: kb[ib])(k, idx)
        v_sel = jax.vmap(lambda vb, ib: vb[ib])(v, idx)
        valid = idx <= t[None, :, None]
        bucket = t5_bucket(jnp.maximum(t[None, :, None] - idx, 0))
        bias = rel_bias[bucket].astype(jnp.float32).transpose(0, 1, 3, 2)
        logits = jnp.einsum('bthd,btkhd->bthk', qb, k_sel).astype(jnp.float32) * (dh ** -0.5) + bias
        logits = jnp.where(valid[:, :, None, :], logits, -jnp.inf)
        probs = jax.nn.softmax(logits, axis=-1).astype(v.dtype)
        return jnp.einsum('bthk,btkhd->bthd', probs, v_sel)

    out = lax.map(one_block, (blockify(q), blockify(iq), blockify(iw), jnp.arange(NB)))
    return out.swapaxes(0, 1).reshape(B, S, H, dh)

def first_inputs(seed: int = 0) -> dict:
    key = jax.random.key(seed)
    ks = jax.random.split(key, 16)
    f32 = jnp.float32
    x = jax.random.normal(ks[0], (BATCH, SEQ, D_MODEL), f32)
    p = jax.random.normal(ks[1], (DEPTH, BATCH, SEQ, D_PLE), f32)
    w_in = jax.random.normal(ks[2], (DEPTH, D_MODEL, PROJ_TOTAL), f32) * D_MODEL ** -0.5
    i_bias = 0.1 * jax.random.normal(ks[3], (DEPTH, M_HEADS), f32)
    f_bias = jnp.linspace(3.0, 6.0, M_HEADS, dtype=f32)[None] + 0.1 * jax.random.normal(ks[4], (DEPTH, M_HEADS), f32)
    b_gate = jnp.concatenate([i_bias, f_bias], axis=-1)
    conv_w = jax.random.normal(ks[5], (DEPTH, CONV_W, 2 * M_HEADS * M_QK), f32) * CONV_W ** -0.5
    w_out = jax.random.normal(ks[6], (DEPTH, D_MIX, D_MODEL), f32) * D_MIX ** -0.5
    norm_in = 1.0 + 0.1 * jax.random.normal(ks[7], (DEPTH, D_MODEL), f32)
    m_norm = 1.0 + 0.1 * jax.random.normal(ks[8], (DEPTH, M_WIDTH), f32)
    rel_bias = 0.5 * jax.random.normal(ks[9], (REL_BUCKETS, A_HEADS), f32)
    w_ple = jax.random.normal(ks[10], (DEPTH, D_PLE, D_MODEL), f32) * D_PLE ** -0.5
    w_ple_gate = jax.random.normal(ks[11], (DEPTH, D_MODEL, D_MODEL), f32) * D_MODEL ** -0.5
    norm_final = 1.0 + 0.1 * jax.random.normal(ks[12], (D_MODEL,), f32)
    return {"x": x, "p": p, "w_in": w_in, "b_gate": b_gate, "conv_w": conv_w, "w_out": w_out,
            "norm_in": norm_in, "m_norm": m_norm, "rel_bias": rel_bias, "w_ple": w_ple,
            "w_ple_gate": w_ple_gate, "norm_final": norm_final}

def first_block(x, p, w_in, b_gate, conv_w, w_out, norm_in, m_norm, rel_bias, w_ple, w_ple_gate, norm_final):
    B, S, _ = x.shape
    h = x
    for i in range(DEPTH):
        u = rmsnorm(h, norm_in[i])
        proj = u @ w_in[i]
        (m_q, m_k, m_v, m_o, m_z, m_if, a_q, a_k, a_v, a_z,
         ix_q, ix_k, ix_w) = jnp.split(proj, SPLIT_POINTS, axis=-1)

        qk = jax.nn.silu(causal_dwconv(jnp.concatenate([m_q, m_k], axis=-1), conv_w[i]))
        mq, mk = jnp.split(qk, 2, axis=-1)
        gates = (m_if + b_gate[i]).astype(jnp.float32)
        log_i = gates[..., :M_HEADS]
        log_f = jax.nn.log_sigmoid(gates[..., M_HEADS:])
        hm = mlstm_chunkwise(mq.reshape(B, S, M_HEADS, M_QK), mk.reshape(B, S, M_HEADS, M_QK),
                             m_v.reshape(B, S, M_HEADS, M_V), log_i, log_f)
        hm = hm * lax.rsqrt(jnp.mean(hm * hm, axis=-1, keepdims=True) + EPS)
        hm = hm.reshape(B, S, M_WIDTH) * m_norm[i].astype(jnp.float32)
        hm = jax.nn.sigmoid(m_o) * hm.astype(x.dtype) * jax.nn.silu(m_z)

        ha = dsa_attention(a_q.reshape(B, S, A_HEADS, A_DH), a_k.reshape(B, S, A_HEADS, A_DH),
                           a_v.reshape(B, S, A_HEADS, A_DH), ix_q.reshape(B, S, IDX_HEADS, IDX_DH),
                           ix_k, ix_w, rel_bias)
        ha = ha.reshape(B, S, A_WIDTH) * jax.nn.silu(a_z)

        h = h + jnp.concatenate([hm, ha], axis=-1) @ w_out[i]

        h = h + (p[i] @ w_ple[i]) * jax.nn.sigmoid(h @ w_ple_gate[i])
    return rmsnorm(h, norm_final)


SSD_EXPAND = 2
D_INNER = SSD_EXPAND * D_MODEL
SSD_HEAD_DIM = 64
SSD_HEADS = D_INNER // SSD_HEAD_DIM
SSD_GROUPS = 4
SSD_HEADS_PER_GROUP = SSD_HEADS // SSD_GROUPS
SSD_STATE = 128
SSD_CONV = 4
SSD_CHUNK = 128
SSD_CONV_DIM = D_INNER + 2 * SSD_GROUPS * SSD_STATE
MLA_HEADS = 16
MLA_Q_LORA = 256
MLA_KV_LORA = 128
MLA_NOPE = 64
MLA_ROPE = 32
MLA_QK_DIM = MLA_NOPE + MLA_ROPE
MLA_V_DIM = 64
MLA_WIDTH = MLA_HEADS * MLA_V_DIM
ROPE_THETA = 10000.0
ATTN_Q_BLOCK = 128
D_FF = 2816
FFN_CONV = 3
NORM_EPS = 1e-6

OFF_Z = D_INNER
OFF_XBC = OFF_Z + SSD_CONV_DIM
OFF_DT = OFF_XBC + SSD_HEADS
OFF_QA = OFF_DT + MLA_Q_LORA
OFF_KVA = OFF_QA + MLA_KV_LORA
OFF_KR = OFF_KVA + MLA_ROPE
IN_COLS = OFF_KR + 2 * D_MODEL


def rms_norm(x, g):
    xf = x.astype(jnp.float32)
    xf = xf * lax.rsqrt(jnp.mean(xf * xf, axis=-1, keepdims=True) + NORM_EPS)
    return (xf * g.astype(jnp.float32)).astype(x.dtype)

def causal_depthwise_conv(x, w, b):
    k, c = w.shape
    y = lax.conv_general_dilated(x, w[:, None, :].astype(x.dtype), window_strides=(1,),
                                 padding=[(k - 1, 0)], dimension_numbers=('NWC', 'WIO', 'NWC'),
                                 feature_group_count=c)
    return y + b

def rope_tables(seq, dim):
    inv = 1.0 / (ROPE_THETA ** (jnp.arange(0, dim, 2, dtype=jnp.float32) / dim))
    ang = jnp.arange(seq, dtype=jnp.float32)[:, None] * inv[None, :]
    return jnp.cos(ang)[None, :, None, :], jnp.sin(ang)[None, :, None, :]

def apply_rope(x, cos, sin):
    x1, x2 = jnp.split(x.astype(jnp.float32), 2, axis=-1)
    return jnp.concatenate([x1 * cos - x2 * sin, x1 * sin + x2 * cos], axis=-1).astype(x.dtype)

def ssd_chunked_scan(xdt, a, bm, cm):
    b, l, h, p = xdt.shape
    nc = l // SSD_CHUNK
    f32 = jnp.float32
    xc = xdt.astype(f32).reshape(b, nc, SSD_CHUNK, SSD_GROUPS, SSD_HEADS_PER_GROUP, p)
    bc = bm.astype(f32).reshape(b, nc, SSD_CHUNK, SSD_GROUPS, SSD_STATE)
    cc = cm.astype(f32).reshape(b, nc, SSD_CHUNK, SSD_GROUPS, SSD_STATE)
    ac = a.astype(f32).reshape(b, nc, SSD_CHUNK, SSD_GROUPS, SSD_HEADS_PER_GROUP).transpose(0, 1, 3, 4, 2)
    a_cum = jnp.cumsum(ac, axis=-1)
    causal = jnp.tril(jnp.ones((SSD_CHUNK, SSD_CHUNK), dtype=bool))
    seg = a_cum[..., :, None] - a_cum[..., None, :]
    decay_in = jnp.exp(jnp.where(causal, seg, -jnp.inf))
    scores = jnp.einsum('bclgn,bcsgn->bcgls', cc, bc)
    y_diag = jnp.einsum('bcgls,bcgels,bcsgep->bclgep', scores, decay_in, xc)
    decay_to_end = jnp.exp(a_cum[..., -1:] - a_cum)
    chunk_states = jnp.einsum('bclgn,bcgel,bclgep->bcgepn', bc, decay_to_end, xc)
    chunk_decay = jnp.exp(a_cum[..., -1])

    def carry_state(state, inp):
        new_states, decay = inp
        return state * decay[..., None, None] + new_states, state

    init = jnp.zeros_like(chunk_states[:, 0])
    _, prev = lax.scan(carry_state, init,
                       (jnp.moveaxis(chunk_states, 1, 0), jnp.moveaxis(chunk_decay, 1, 0)))
    y_off = jnp.einsum('bclgn,cbgepn,bcgel->bclgep', cc, prev, jnp.exp(a_cum))
    return (y_diag + y_off).reshape(b, l, h, p).astype(xdt.dtype)

def ssd_mixer(z, xbc, dt_raw, conv_w, conv_b, dt_bias, a_log, d_skip, norm_g):
    b, l, _ = z.shape
    xbc = jax.nn.silu(causal_depthwise_conv(xbc, conv_w, conv_b))
    xs, bm, cm = jnp.split(xbc, [D_INNER, D_INNER + SSD_GROUPS * SSD_STATE], axis=-1)
    xs = xs.reshape(b, l, SSD_HEADS, SSD_HEAD_DIM)
    bm = bm.reshape(b, l, SSD_GROUPS, SSD_STATE)
    cm = cm.reshape(b, l, SSD_GROUPS, SSD_STATE)
    dt = jax.nn.softplus(dt_raw.astype(jnp.float32) + dt_bias.astype(jnp.float32))
    a = -jnp.exp(a_log.astype(jnp.float32))
    y = ssd_chunked_scan(xs * dt[..., None].astype(xs.dtype), dt * a, bm, cm)
    y = y + xs * d_skip[:, None]
    y = y.reshape(b, l, D_INNER) * jax.nn.silu(z)
    y = rms_norm(y.reshape(b, l, SSD_GROUPS, D_INNER // SSD_GROUPS),
                 norm_g.reshape(SSD_GROUPS, D_INNER // SSD_GROUPS))
    return y.reshape(b, l, D_INNER)

def blocked_causal_attention(q, k, v):
    b, l, h, dk = q.shape
    scale = dk ** -0.5
    key_pos = jnp.arange(l)

    def one_block(i):
        start = i * ATTN_Q_BLOCK
        qb = lax.dynamic_slice_in_dim(q, start, ATTN_Q_BLOCK, axis=1)
        s = jnp.einsum('bqhd,bkhd->bhqk', qb, k).astype(jnp.float32) * scale
        qpos = start + jnp.arange(ATTN_Q_BLOCK)
        s = jnp.where(qpos[:, None] >= key_pos[None, :], s, -jnp.inf)
        p = jax.nn.softmax(s, axis=-1).astype(v.dtype)
        return jnp.einsum('bhqk,bkhd->bqhd', p, v)

    out = lax.map(one_block, jnp.arange(l // ATTN_Q_BLOCK))
    return jnp.moveaxis(out, 0, 1).reshape(b, l, h * v.shape[-1])

def mla_mixer(q_a, kv_a, k_rope_raw, q_a_norm_g, w_uq, kv_a_norm_g, w_ukv, q_norm_g, k_norm_g, cos, sin):
    b, l, _ = q_a.shape
    q = (rms_norm(q_a, q_a_norm_g) @ w_uq).reshape(b, l, MLA_HEADS, MLA_QK_DIM)
    kv = (rms_norm(kv_a, kv_a_norm_g) @ w_ukv).reshape(b, l, MLA_HEADS, MLA_NOPE + MLA_V_DIM)
    k_nope, v = jnp.split(kv, [MLA_NOPE], axis=-1)
    k_rope = jnp.broadcast_to(k_rope_raw[:, :, None, :], (b, l, MLA_HEADS, MLA_ROPE))
    k = jnp.concatenate([k_nope, k_rope], axis=-1)
    q = rms_norm(q, q_norm_g)
    k = rms_norm(k, k_norm_g)
    q = jnp.concatenate([q[..., :MLA_NOPE], apply_rope(q[..., MLA_NOPE:], cos, sin)], axis=-1)
    k = jnp.concatenate([k[..., :MLA_NOPE], apply_rope(k[..., MLA_NOPE:], cos, sin)], axis=-1)
    return blocked_causal_attention(q, k, v)

def second_inputs(seed: int = 0) -> dict:
    key = jax.random.key(seed)
    ks = jax.random.split(key, 24)
    f32 = jnp.float32

    def dense(k, shape, fan_in):
        return jax.random.normal(k, (DEPTH,) + shape, f32) * fan_in ** -0.5

    def gain(k, n):
        return 1.0 + 0.02 * jax.random.normal(k, (DEPTH, n), f32)

    def bias(k, n):
        return 0.02 * jax.random.normal(k, (DEPTH, n), f32)

    dt0 = jnp.exp(jax.random.uniform(ks[5], (DEPTH, SSD_HEADS), f32, np.log(1e-3), np.log(1e-1)))
    return {
        "x": jax.random.normal(ks[0], (BATCH, SEQ, D_MODEL), f32),
        "norm_mix_g": gain(ks[1], D_MODEL),
        "w_in": dense(ks[2], (D_MODEL, IN_COLS), D_MODEL),
        "conv_ssd_w": dense(ks[3], (SSD_CONV, SSD_CONV_DIM), SSD_CONV),
        "conv_ssd_b": bias(ks[4], SSD_CONV_DIM),
        "dt_bias": dt0 + jnp.log(-jnp.expm1(-dt0)),
        "a_log": jnp.log(jax.random.uniform(ks[6], (DEPTH, SSD_HEADS), f32, 1.0, 16.0)),
        "d_skip": 1.0 + 0.1 * jax.random.normal(ks[7], (DEPTH, SSD_HEADS), f32),
        "ssd_norm_g": gain(ks[8], D_INNER),
        "w_ssd_proj": dense(ks[9], (D_INNER, D_MODEL), D_INNER),
        "q_a_norm_g": gain(ks[10], MLA_Q_LORA),
        "w_uq": dense(ks[11], (MLA_Q_LORA, MLA_HEADS * MLA_QK_DIM), MLA_Q_LORA),
        "kv_a_norm_g": gain(ks[12], MLA_KV_LORA),
        "w_ukv": dense(ks[13], (MLA_KV_LORA, MLA_HEADS * (MLA_NOPE + MLA_V_DIM)), MLA_KV_LORA),
        "q_norm_g": gain(ks[14], MLA_QK_DIM),
        "k_norm_g": gain(ks[15], MLA_QK_DIM),
        "w_mla_proj": dense(ks[16], (MLA_WIDTH, D_MODEL), MLA_WIDTH),
        "gate_b": bias(ks[17], 2 * D_MODEL),
        "w_o": dense(ks[18], (D_MODEL, D_MODEL), D_MODEL),
        "norm_ffn_g": gain(ks[19], D_MODEL),
        "w_up": dense(ks[20], (D_MODEL, 2 * D_FF), D_MODEL),
        "conv_ffn_w": dense(ks[21], (FFN_CONV, 2 * D_FF), FFN_CONV),
        "conv_ffn_b": bias(ks[22], 2 * D_FF),
        "w_down": dense(ks[23], (D_FF, D_MODEL), D_FF),
    }

def second_block(x, norm_mix_g, w_in, conv_ssd_w, conv_ssd_b, dt_bias, a_log, d_skip, ssd_norm_g,
              w_ssd_proj, q_a_norm_g, w_uq, kv_a_norm_g, w_ukv, q_norm_g, k_norm_g, w_mla_proj,
              gate_b, w_o, norm_ffn_g, w_up, conv_ffn_w, conv_ffn_b, w_down):
    cos, sin = rope_tables(x.shape[1], MLA_ROPE)
    for i in range(DEPTH):
        h = rms_norm(x, norm_mix_g[i])
        proj = h @ w_in[i]
        z, xbc, dt_raw, q_a, kv_a, k_rope_raw, gates = jnp.split(
            proj, [OFF_Z, OFF_XBC, OFF_DT, OFF_QA, OFF_KVA, OFF_KR], axis=-1)
        y_ssd = ssd_mixer(z, xbc, dt_raw, conv_ssd_w[i], conv_ssd_b[i], dt_bias[i], a_log[i],
                          d_skip[i], ssd_norm_g[i]) @ w_ssd_proj[i]
        y_mla = mla_mixer(q_a, kv_a, k_rope_raw, q_a_norm_g[i], w_uq[i], kv_a_norm_g[i], w_ukv[i],
                          q_norm_g[i], k_norm_g[i], cos, sin) @ w_mla_proj[i]
        g_ssd, g_mla = jnp.split(jax.nn.sigmoid(gates + gate_b[i]), 2, axis=-1)
        x = x + (g_ssd * y_ssd + g_mla * y_mla) @ w_o[i]
        h = rms_norm(x, norm_ffn_g[i])
        u = causal_depthwise_conv(h @ w_up[i], conv_ffn_w[i], conv_ffn_b[i])
        u_gate, u_val = jnp.split(u, 2, axis=-1)
        x = x + (jax.nn.silu(u_gate) * u_val) @ w_down[i]
    return x


def setup_inputs(seed=0):
    out = dict(first_inputs(seed))
    for name, value in second_inputs(seed + 1).items():
        if name != "x":
            out[name + "_2"] = value
    return out


def reference(
    x, p, w_in, b_gate, conv_w, w_out, norm_in, m_norm, rel_bias, w_ple, w_ple_gate, norm_final,
    norm_mix_g_2, w_in_2, conv_ssd_w_2, conv_ssd_b_2, dt_bias_2, a_log_2, d_skip_2,
    ssd_norm_g_2, w_ssd_proj_2, q_a_norm_g_2, w_uq_2, kv_a_norm_g_2, w_ukv_2, q_norm_g_2,
    k_norm_g_2, w_mla_proj_2, gate_b_2, w_o_2, norm_ffn_g_2, w_up_2, conv_ffn_w_2, conv_ffn_b_2,
    w_down_2,
):
    x = first_block(
        x, p, w_in, b_gate, conv_w, w_out, norm_in, m_norm, rel_bias, w_ple, w_ple_gate,
        norm_final,
    )
    return second_block(
        x, norm_mix_g_2, w_in_2, conv_ssd_w_2, conv_ssd_b_2, dt_bias_2, a_log_2, d_skip_2,
        ssd_norm_g_2, w_ssd_proj_2, q_a_norm_g_2, w_uq_2, kv_a_norm_g_2, w_ukv_2, q_norm_g_2,
        k_norm_g_2, w_mla_proj_2, gate_b_2, w_o_2, norm_ffn_g_2, w_up_2, conv_ffn_w_2,
        conv_ffn_b_2, w_down_2,
    )


_drawn_inputs = setup_inputs


def setup_inputs(seed=0):
    import zlib

    import numpy as np

    out = dict(_drawn_inputs(seed))
    spreads = {}
    factors = {'norm_mix_g_2': 3.398,
     'conv_ssd_b_2': 10.887,
     'ssd_norm_g_2': 19.447,
     'q_a_norm_g_2': 8.0,
     'kv_a_norm_g_2': 8.0,
     'q_norm_g_2': 8.0,
     'k_norm_g_2': 8.0,
     'gate_b_2': 8.0,
     'norm_ffn_g_2': 11.264,
     'conv_ffn_b_2': 12.658,
     'd_skip_2': 61.916}
    for name, (base, spread) in spreads.items():
        noise = np.random.default_rng([zlib.crc32(name.encode()), seed]).standard_normal(out[name].shape)
        drawn = base * np.exp(spread * noise) if base else spread * noise
        out[name] = __import__('jax').numpy.asarray(drawn.astype(out[name].dtype))
    for name, factor in factors.items():
        out[name] = (out[name] * factor).astype(out[name].dtype)
    return out
```

```python
from contextlib import ExitStack

import numpy as np

import concourse.bass as bass
from concourse import mybir
from concourse.alu_op_type import AluOpType as ALU

F32 = mybir.dt.float32
F32R = mybir.dt.float32r
BF16 = mybir.dt.bfloat16
ACT = mybir.ActivationFunctionType
AX_X = mybir.AxisListType.X

P = 128
S = 512
NT = S // P
D = 1024
KD = D // P
EPS = 1e-6
NEG = -1e30

MH, MQK, MV = 4, 128, 256
AH, ADH = 8, 64
IH, IDH = 8, 64
TOPK = S // 4
BUCKETS = 32
HANK = S + P
SSD_H, SSD_P, SSD_G = 32, 64, 4
XH, QK, NOPE, ROPE, VD = 16, 96, 64, 32, 64
D_FF = 2816
FT = D_FF // P

CH = 8
RING = 4

VEC = {}
_n = 0
for _name, _w in (("norm_in", KD), ("conv_w", 8 * 4), ("m_norm", KD), ("gate_bias", 1), ("gate_scale", 1),
                  ("norm_final", KD), ("norm_mix", KD), ("ssd_conv_w", 24 * 4), ("ssd_conv_b", 24),
                  ("dt_bias", 1), ("a_log", 1), ("d_skip", 16), ("ssd_g", 16), ("qa_g", 2), ("kva_g", 1),
                  ("q_g", 1), ("k_g", 1), ("gate_b", 16), ("norm_ffn", KD), ("ffn_conv_w", 2 * FT * 3),
                  ("ffn_conv_b", 2 * FT), ("eps", 1), ("eps_q", 1), ("eps2", 1)):
    VEC[_name] = (_n, _w)
    _n += _w
NVEC = _n


class Plan:

    def __init__(self):
        self.chunks = self.events = self.turn = 0
        self.banks, self.last = [0, 1, 2, 3], {}
        self.stage, self.used_at, self.count = {}, {}, {"A": 0, "D": 0}
        self.upto = -1

    def use_banks(self, *banks):
        self.banks, self.turn = list(banks), 0

    def chunk(self):
        self.chunks += 1
        return self.chunks - 1

    def event(self, c=None):
        self.events += 1
        if c is not None:
            self.used_at[c] = self.events
            while self.upto + 1 in self.used_at:
                self.upto += 1

    def open(self, name, parts, ends):
        bank = self.banks[self.turn % len(self.banks)]
        self.turn += 1
        t = dict(parts=parts, ends=ends, bank=bank, before=self.last.get(bank))
        self.stage.setdefault(name, []).append(t)
        return t

    def close(self, t, reader):
        t.update(full=self.events, upto=self.upto)
        self.count[reader] += 1
        t["freed"] = self.last[t["bank"]] = (reader, self.count[reader])

    def tile(self, name, parts, reader, last=None):
        t = self.open(name, parts, [])
        self.fill(t, reader, last)

    def fill(self, t, reader, last=None):
        parts, ends = t["parts"], t["ends"]
        for i, (c, s) in enumerate(parts):
            done = c in last if last is not None else s == CH - 1
            if i == len(parts) - 1 or (parts[i + 1][0] != c and done):
                self.event(c if done else None)
                ends.append(i)
        self.close(t, reader)

    def columns(self, name, n, kt, readers):
        c0 = self.chunks
        self.chunks += -(-n * kt // CH)
        for t in range(n):
            parts = [(c0 + f // CH, f % CH) for f in range(t * kt, (t + 1) * kt)]
            last = {c for c, s in parts if s == CH - 1 or (c, s) == (c0 + (n * kt - 1) // CH, (n * kt - 1) % CH)}
            self.tile(name, parts, readers[t % len(readers)], last)

    def rows(self, name, halves, kt, readers):
        per = CH * P // S
        flat = [(self.chunks + f // per, f % per) for f in range(halves * kt)]
        self.chunks = flat[-1][0] + 1
        for h in range(halves):
            self.use_banks(0, 1, 2, 3)
            parts = flat[h * kt:(h + 1) * kt]
            ends = [i for i, (c, s) in enumerate(parts) if s == per - 1 or i == kt - 1]
            for i in ends:
                c, s = parts[i]
                self.event(c if s == per - 1 or (h, i) == (halves - 1, kt - 1) else None)
            for t in range(NT):
                self.close(self.open(name, parts, ends), readers[t % len(readers)])


def make_plan():
    plan = Plan()
    for name, n, kt, reader in (("idx_q", 4, KD, "A"), ("idx_k", 1, KD, "A"), ("small", 1, KD, "A"),
                                ("att_q", 4, KD, "A"), ("att_k", 4, KD, "A")):
        plan.columns(name, n, kt, reader)
    plan.rows("att_v", 1, KD, "AD")
    plan.rows("mem_v", 2, KD, "AD")
    for name, n, kt, reader in (("att_z", 4, KD, "D"), ("mem_qk", 8, KD, "D"), ("mem_oz", 16, KD, "AD"),
                                ("out", 8, 12, "D"), ("ple", 8, 2, "A"), ("gate", 8, KD, "A"),
                                ("small2", 1, KD, "A"), ("ssd_b", 4, KD, "D"), ("ssd_c", 4, KD, "D"),
                                ("ssd_x", 16, KD, "D")):
        plan.columns(name, n, kt, reader)
    plan.use_banks(0, 1)
    for name, n, reader in (("z", 16, "D"), ("qa", 2, "A"), ("kva", 1, "A")):
        plan.columns(name, n, KD, reader)
    plan.use_banks(0, 1, 2, 3)
    plan.columns("ssd_out", 8, 16, "A")
    plan.rows("v", 2, 1, "AD")
    plan.use_banks(1, 2)
    pairs = {}

    def project(h):
        if h % 2 == 0:
            pairs[h // 2] = plan.chunk()
        c, s = pairs[h // 2], 3 * (h % 2)
        plan.tile("head_q", [(c, s), (c, s + 1)], "D", ())
        plan.tile("head_k", [(c, s + 2)], "D", (c,) if h % 2 else ())

    project(0)
    for h in range(XH):
        plan.use_banks(3 * (h % 2))
        c = plan.chunk()
        t = plan.open("mix_gate", [(c, s) for s in range(KD)], [])
        plan.use_banks(1, 2)
        if h == 0:
            project(1)
            plan.fill(t, "A")
        if h + 2 < XH:
            project(h + 2)
        if h:
            plan.fill(t, "A")
    plan.use_banks(0, 1, 2, 3)
    for name, n, kt in (("mla_out", 8, KD), ("mix_out", 8, KD), ("up", 2 * FT, KD), ("down", 8, FT)):
        plan.columns(name, n, kt, "D")
    return plan


def build(nc, a, out):
    plan = make_plan()
    st = plan.stage
    N_CHUNK = plan.chunks
    ctx = ExitStack()
    with ctx:
        base = (nc.sbuf_base + 63) // 64 * 64

        def at(name, kb, shape, dt=F32):
            return nc.alloc_sbuf_tensor_at(name, shape, dt, offset=base + int(kb * 1024))

        def sem(name):
            return ctx.enter_context(nc.semaphore(name))

        bank = [ctx.enter_context(nc.psum_tensor(f"bank{i}", [P, 512], F32)) for i in range(8)]

        w_raw = at("w_raw", 0, [P, RING, CH * P])
        w_hi = at("w_hi", 16, [P, RING, CH * P], F32R)
        w_lo = at("w_lo", 32, [P, RING, CH * P], F32R)
        ones = at("ones", 48, [P, 512])
        ident = at("ident", 50, [P, P])
        flip = at("flip", 50.5, [P, P])
        tri = at("tri", 51, [P, P])
        ident_b = at("ident_b", 51.5, [P, P], BF16)
        later4_b = at("later4_b", 51.75, [P, 4 * P], BF16)
        vecs = at("vecs", 52.75, [P, NVEC])
        sel_m = at("sel_m", 54.5, [96, MH * P], BF16)
        u_hi = at("u_hi", 56, [P, KD, S], F32R)
        u_lo = at("u_lo", 72, [P, KD, S], F32R)
        iq = at("iq", 88, [P, 4, S])
        ik = at("ik", 96, [P, S])
        relu = at("relu", 98, [P, 2, S])
        score = at("score", 102, [P, 3, S])
        work = at("work", 108, [P, 2, S])
        work2 = at("work2", 200, [P, S])
        small = at("small", 202, [P, S])
        top8 = at("top8", 204, [P, 3, 8])
        tk = at("tk", 204.25, [P, 3, 4])
        iw = at("iw", 204.5, [P, 3, IH])
        acol = at("acol", 205, [P, NT * MH])
        da_cols = at("da_cols", 205.5, [P, 4, AH * NT])
        chosen = at("chosen", 112, [P, NT, S])
        xt = at("xt", 120, [P, KD, S])
        sq = at("sq", 136, [P, 2, S])
        rms_std = at("rms_std", 140, [P, S])
        rms_inv = at("rms_inv", 142, [P, S])
        u_val = at("u_val", 144, [P, 2, S])
        mem_qk = at("mem_qk", 120, [P, 8, S])
        mem_v = at("mem_v", 136, [P, NT, MH * MV])
        mem_o = at("mem_o", 152, [P, 8, S])
        att_q = at("att_q", 168, [P, 4, S])
        att_k = at("att_k", 176, [P, 4, S])
        att_v = at("att_v", 184, [P, NT, AH * ADH])
        att_z = at("att_z", 192, [P, 4, S])
        ev = at("ev", 108, [P, 2, S])
        sg = at("sg", 200, [P, S])
        bias_row = at("bias_row", 192, [AH, HANK])
        rel = at("rel", 194.5, [BUCKETS, AH])
        buckets = at("buckets", 195, [BUCKETS, HANK])
        r_f = at("r_f", 152, [MH, S])
        r_t = at("r_t", 154, [MH, S])
        r_lf = at("r_lf", 156, [MH, S])
        r_b = at("r_b", 158, [MH, S])
        r_a = at("r_a", 160, [MH, S])
        r_m = at("r_m", 162, [MH, S])
        r_n = at("r_n", 164, [MH, S])
        r_p = at("r_p", 166, [MH, 2, S], BF16)
        stack_m = at("stack_m", 206, [96, S], BF16)
        stack_f = at("stack_f", 204, [96, S], BF16)
        decay = at("decay", 176, [P, 2, 1280])
        h_val = at("h_val", 186, [P, 2, S])
        floor = at("floor", 190, [P, S])
        den = at("den", 88, [P, S])
        inv_den = at("inv_den", 90, [P, S])
        sq_m = at("sq_m", 96, [P, 2, S])
        std_m = at("std_m", 92, [P, S])
        inv_m = at("inv_m", 94, [P, S])
        val_m = at("val_m", 112, [P, 2, S])
        mix_hi = at("mix_hi", 152, [P, 8, S], F32R)
        mix_lo = at("mix_lo", 120, [P, 8, S], F32R)
        hank = at("hank", 88, [P, 2, S])
        probs = at("probs", 92, [P, 2, S])
        turned = at("turned", 96, [P, 2, S])
        att_o = at("att_o", 100, [P, NT, S])
        mixa_hi = at("mixa_hi", 192, [P, 4, S], F32R)
        mixa_lo = at("mixa_lo", 168, [P, 4, S], F32R)
        xt2 = at("xt2", 72, [P, KD, S])
        h_res = at("h_res", 56, [P, KD, S])
        h_hi = at("h_hi", 72, [P, KD, S], F32R)
        h_lo = at("h_lo", 88, [P, KD, S], F32R)
        p_val = at("p_val", 136, [P, 2, S])
        p_hi = at("p_hi", 140, [P, 2, S], F32R)
        p_lo = at("p_lo", 144, [P, 2, S], F32R)
        ple = at("ple", 168, [P, KD, S])
        gate = at("gate", 184, [P, 2, S])
        sq_f = at("sq_f", 136, [P, 4, S])
        std_f = at("std_f", 192, [P, S])
        inv_f = at("inv_f", 194, [P, S])
        std_g = at("std_g", 144, [P, S])
        inv_g = at("inv_g", 146, [P, S])
        gain2 = at("gain2", 206.75, [P, KD])
        val_f = at("val_f", 196, [P, 2, S])
        u2_hi = at("u2_hi", 72, [P, KD, S], F32R)
        u2_lo = at("u2_lo", 88, [P, KD, S], F32R)
        bias_dram = nc.dram_tensor("bias_dram", (AH, HANK), F32).ap()

        def vec(name, i=0):
            return vecs[:, VEC[name][0] + i:VEC[name][0] + i + 1]

        def e_t(h, j):
            o = sum(S - i * P for i in range(j))
            return decay[:, h % 2, o:o + S - j * P]

        units = [(h, ti) for h in range(AH) for ti in range(NT)]
        n_lo = {}
        for name, n in (("u", KD), ("mixa", 4), ("mix", 8), ("p", 2), ("h", KD), ("u2", KD)):
            n_lo[name] = n + (max(n_lo.values()) if n_lo else 0)

        w_landed = [sem(f"w_landed{i}") for i in range(RING)]
        w_hi_ready = sem("w_hi_ready")
        w_lo_ready = sem("w_lo_ready")
        dense_done = sem("dense_done")
        act_freed = sem("act_freed")
        dve_freed = sem("dve_freed")
        freed = {"A": act_freed, "D": dve_freed}
        consts_in = sem("consts_in")
        x_in = [sem(f"x_in{i}") for i in range(KD)]
        sq_ready = sem("sq_ready")
        sq_used = sem("sq_used")
        std_ready = sem("std_ready")
        inv_ready = sem("inv_ready")
        val_ready = sem("val_ready")
        hi_ready = sem("hi_ready")
        lo_ready = sem("lo_ready")
        dve_step = sem("dve_step")
        act_step = sem("act_step")
        ones_ready = sem("ones_ready")
        iw_turned = sem("iw_turned")
        iw_ready = sem("iw_ready")
        idx_dot = sem("idx_dot")
        idx_relu = sem("idx_relu")
        idx_added = sem("idx_added")
        top_found = sem("top_found")
        top_gone = sem("top_gone")
        chosen_ready = sem("chosen_ready")
        ev_ready = sem("ev_ready")
        ev_used = sem("ev_used")
        taps_ready = sem("taps_ready")
        sg_ready = sem("sg_ready")
        mem_qk_ready = sem("mem_qk_ready")
        ml_f = sem("ml_f")
        ml_log = sem("ml_log")
        rows_ready = sem("rows_ready")
        stack_ready = sem("stack_ready")
        acol_turned = sem("acol_turned")
        acol_ready = sem("acol_ready")
        ml_spread = sem("ml_spread")
        ml_decay = sem("ml_decay")
        ml_score = sem("ml_score")
        ml_weight = sem("ml_weight")
        ml_sums = sem("ml_sums")
        ml_values = sem("ml_values")
        ml_floor = sem("ml_floor")
        ml_h = sem("ml_h")
        bias_dot = sem("bias_dot")
        bias_ready = sem("bias_ready")
        bias_out = sem("bias_out")
        hank_in = [sem("hank_in0"), sem("hank_in1")]
        da_logits = sem("da_logits")
        da_max = sem("da_max")
        da_probs = sem("da_probs")
        da_turn = sem("da_turn")
        da_turned = sem("da_turned")
        da_sum = sem("da_sum")
        da_out = sem("da_out")
        da_back = sem("da_back")
        x2_in = sem("x2_in")
        p_in = sem("p_in")
        h_res_ready = sem("h_res_ready")
        ple_added = sem("ple_added")
        x2_ready = sem("x2_ready")
        v_tok_ready = sem("v_tok_ready")
        norm_sums_in = sem("norm_sums_in")
        stored = sem("stored")
        tri_b = at("tri_b", 55.5, [P, P], BF16)
        y = at("y", 104, [P, 16, S])
        y_lo = at("y_lo", 104, [P, 16, S], F32R)
        one_hot = at("one_hot", 206.5, [96, SSD_H], BF16)
        trig = at("trig", 148, [P, S])
        b_t = at("b_t", 150, [P, SSD_G, S])
        c_t = at("c_t", 158, [P, SSD_G, S])
        small2 = at("small2", 166, [P, S])
        stack_a = at("stack_a", 168, [96, S], BF16)
        cols = at("cols", 169, [P, 3 * NT, SSD_H])
        rate = at("rate", 170.5, [SSD_H, 1])
        chunk_decay = at("chunk_decay", 171, [P, 2 * SSD_H])
        ends_diag = at("ends_diag", 171.75, [SSD_H, 2 * SSD_H])
        r_dt = at("r_dt", 172.5, [SSD_H, S])
        r_ac = at("r_ac", 174.5, [SSD_H, S])
        r_dte = at("r_dte", 176.5, [SSD_H, S])
        r_t2 = at("r_t2", 178.5, [SSD_H, S])
        r_p2 = at("r_p2", 188.5, [SSD_H, 2, S], BF16)
        r_n2 = at("r_n2", 190.5, [SSD_H, S])
        taps = at("taps", 180.5, [P, 2, S])
        taps_sg = at("taps_sg", 184.5, [P, 2, S])
        states = at("states", 172.5, [P, 3, S])
        scores = at("scores", 178.5, [P, S])
        xdt = at("xdt", 180.5, [P, NT, S])
        xdec = at("xdec", 188.5, [P, 3, S])
        b_tok = at("b_tok", 194.5, [P, 3 * P])
        weights2 = [at("weight_a", 196.5, [P, 2, S]), at("weight_b", 144, [P, 2, S])]
        e_ac = at("e_ac", 200.5, [P, 2, S])
        sq_y = at("sq_y", 136, [P, 2, S])
        std_y = at("std_y", 140, [P, S])
        inv_y = at("inv_y", 142, [P, S])
        z_sg = at("z_sg", 204.5, [P, S])
        y_hi = at("y_hi", 170, [P, 16, S], F32R)
        qa_val = at("qa_val", 202, [P, 2, S])
        kva_val = at("kva_val", 168, [P, S])
        qn_hi = at("qn_hi", 136, [P, 2, S], F32R)
        qn_lo = at("qn_lo", 140, [P, 2, S], F32R)
        kn_hi = at("kn_hi", 144, [P, S], F32R)
        kn_lo = at("kn_lo", 146, [P, S], F32R)
        sq_s = at("sq_s", 158, [P, 2, S])
        std_s = at("std_s", 162, [P, S])
        inv_s = at("inv_s", 164, [P, S])
        y_ssd = at("y_ssd", 150, [P, KD, S])
        v_tok = at("v_tok", 104, [P, NT, XH * VD])
        o_tok = at("o_tok", 120, [P, NT, XH * VD])
        turned_x = [at("turned_x0", 166, [P, S]), at("turned_x1", 168, [P, S])]
        gm = at("gm", 170, [P, KD, S])
        q_s = at("q_s", 186, [QK, 2, S])
        k_s = at("k_s", 190, [QK, 2, S])
        sq_q = at("sq_q", 194, [QK, S])
        sq_k = at("sq_k", 196, [QK, S])
        rope = at("rope", 198, [P, S])
        rk_diag = at("rk_diag", 200, [P, S])
        probs_x = at("probs_x", 202, [P, 2, S])
        x_cols = at("x_cols", 206, [P, 4, XH * NT])
        r_qk = at("r_qk", 207, [P, 2, 2 * NT])
        o_hi = at("o_hi", 186, [P, KD, S], F32R)
        o_lo = at("o_lo", 104, [P, KD, S], F32R)
        fused_hi = at("fused_hi", 72, [P, KD, S], F32R)
        fused_lo = at("fused_lo", 88, [P, KD, S], F32R)
        sq_x = at("sq_x", 150, [P, 2, S])
        std_x = at("std_x", 154, [P, S])
        inv_x = at("inv_x", 156, [P, S])
        val_x = at("val_x", 158, [P, 2, S])
        u3_hi = at("u3_hi", 72, [P, KD, S], F32R)
        u3_lo = at("u3_lo", 88, [P, KD, S], F32R)
        act_hi = at("act_hi", 104, [P, FT, S], F32R)
        act_lo = at("act_lo", 148, [P, FT, S], F32R)
        ffn_g = at("ffn_g", 192, [P, 2, S])
        ffn_v = at("ffn_v", 196, [P, 2, S])
        ffn_sg = at("ffn_sg", 200, [P, 2, S])

        for name, n in (("y", 16), ("qn", 2), ("kn", 1), ("o", 8), ("fused", 8), ("u3", 8), ("act", FT)):
            n_lo[name] = n + max(n_lo.values())
        n_inv = 3 + MH
        conv_tiles = ([(t, 16 + i, b_t[:, i, :]) for i, t in enumerate(st["ssd_b"])]
                      + [(t, 20 + i, c_t[:, i, :]) for i, t in enumerate(st["ssd_c"])]
                      + [(t, i, y[:, i, :]) for i, t in enumerate(st["ssd_x"])])

        def weight(h):
            return weights2[h // 2 % 2][:, h % 2, :]

        heads = [(h, ti) for h in range(XH) for ti in range(NT)]
        consts2_in = sem("consts2_in")
        conv_in = sem("conv_in")
        conv_sg = sem("conv_sg")
        conv_ready = sem("conv_ready")
        dt_log = sem("dt_log")
        rate_ready = sem("rate_ready")
        acum_ready = sem("acum_ready")
        stack_a_ready = sem("stack_a_ready")
        dte_ready = sem("dte_ready")
        cols_turned = sem("cols_turned")
        ends_spread = sem("ends_spread")
        cols_ready = sem("cols_ready")
        grp_dot = sem("grp_dot")
        grp_copied = sem("grp_copied")
        x_turned = sem("x_turned")
        xdt_ready = sem("xdt_ready")
        xdec_ready = sem("xdec_ready")
        state_dot = sem("state_dot")
        state_ready = sem("state_ready")
        a_spread = sem("a_spread")
        l_ready = sem("l_ready")
        w_ready = sem("w_ready")
        e_spread = sem("e_spread")
        e_ready = sem("e_ready")
        z_ready = sem("z_ready")
        y_dot = sem("y_dot")
        off_dot = sem("off_dot")
        y_read = sem("y_read")
        y_ready = sem("y_ready")
        y_normed = sem("y_normed")
        krope_ready = sem("krope_ready")
        krope_sq = sem("krope_sq")
        head_sq = sem("head_sq")
        head_sums = sem("head_sums")
        k_ready = sem("k_ready")
        std_qk_ready = sem("std_qk_ready")
        r_qk_ready = sem("r_qk_ready")
        rk_diag_ready = sem("rk_diag_ready")
        rk_spread = sem("rk_spread")
        x_logits = sem("x_logits")
        x_max = sem("x_max")
        x_probs = sem("x_probs")
        x_turn = sem("x_turn")
        x_turned_out = sem("x_turned_out")
        x_sum = sem("x_sum")
        x_out = sem("x_out")
        gates_used = sem("gates_used")
        o_back = sem("o_back")
        act_in = sem("act_in")
        act_sg = sem("act_sg")
        block = ctx.enter_context(nc.Block())

        @block.sync
        def _(sp):
            for i in range(KD):
                sp.dma_start(xt[:, i, :], a["x_t"][:, i, :]).then_inc(x_in[i], 16)
            for j in range(RING):
                sp.dma_start(w_raw[:, j, :], a["weights"][j]).then_inc(w_landed[j], 16)
            with sp.Fori(1, N_CHUNK // RING) as g:
                for j in range(RING):
                    sp.wait_ge(w_lo_ready, RING * g + (j + 1 - RING))
                    sp.dma_start(w_raw[:, j, :],
                                 a["weights"][bass.ds(RING * g + j, 1)].rearrange("a p n -> (a p) n")
                                 ).then_inc(w_landed[j], 16)
            for c in range(N_CHUNK // RING * RING, N_CHUNK):
                sp.wait_ge(w_lo_ready, c + 1 - RING)
                sp.dma_start(w_raw[:, c % RING, :], a["weights"][c]).then_inc(w_landed[c % RING], 16)
            for i, t in enumerate(st["down"]):
                sp.wait_ge(dve_freed, t["freed"][1])
                sp.dma_start(out[:, i, :], h_res[:, i, :]).then_inc(stored, 16)
            sp.wait_ge(stored, 16 * (1 + KD))

        @block.gpsimd
        def _(pool):
            def low_part(c, j):
                pool.wait_ge(w_hi_ready, c + 1)
                pool.tensor_tensor(w_lo[:, j, :], w_raw[:, j, :], w_hi[:, j, :].bitcast(F32),
                                   ALU.subtract).then_inc(w_lo_ready, 1)

            with pool.Fori(0, N_CHUNK // RING) as g:
                for j in range(RING):
                    low_part(RING * g + j, j)
            for c in range(N_CHUNK // RING * RING, N_CHUNK):
                low_part(c, c % RING)

        @block.tensor
        def _(pe):
            n_sq = [0]

            def rms(n, sq, b=4):
                for i in range(n):
                    square_sum(i, n, sq, b)

            def square_sum(i, n, sq, b=4):
                pe.wait_ge(sq_ready, n_sq[0] + 1)
                pe.matmul(bank[b][:, :], ones[:, 0:P], sq[:, i % 2, :], start=(i == 0),
                          stop=(i == n - 1)).then_inc(sq_used, 1)
                n_sq[0] += 1

            def open_bank(t):
                if t["before"]:
                    e, n = t["before"]
                    pe.wait_ge(freed[e], n)

            def column_tile(t, rhs, ready=None, part=None):
                n = len(t["parts"])
                first, end = part or (0, n)
                if first == 0:
                    open_bank(t)
                o = bank[t["bank"]][:, :]
                for i in range(first, end):
                    c, s = t["parts"][i]
                    if i == first or t["parts"][i - 1][0] != c:
                        pe.wait_ge(w_lo_ready, c + 1)
                    if ready is not None:
                        pe.wait_ge(lo_ready, ready + i + 1)
                    hi, lo = (w[:, c % RING, s * P:(s + 1) * P] for w in (w_hi, w_lo))
                    xh, xl = rhs(i)
                    pe.matmul(o, hi, xh, start=(i == 0), stop=False)
                    pe.matmul(o, hi, xl, start=False, stop=False)
                    mm = pe.matmul(o, lo, xh, start=False, stop=(i == n - 1))
                    if i in t["ends"]:
                        mm.then_inc(dense_done, 1)

            def column_tiles(tiles, rhs, ready=None):
                for i, t in enumerate(tiles):
                    column_tile(t, rhs, ready if i == 0 else None)

            def row_tiles(tiles, lhs):
                for t in tiles:
                    open_bank(t)
                parts, ends = tiles[0]["parts"], tiles[0]["ends"]
                for k, (c, s) in enumerate(parts):
                    pe.wait_ge(w_lo_ready, c + 1)
                    hi, lo = (w[:, c % RING, s * S:(s + 1) * S] for w in (w_hi, w_lo))
                    for t in range(NT):
                        xh, xl = (x[:, t * P:(t + 1) * P] for x in lhs(k))
                        o = bank[t][:, :]
                        pe.matmul(o, xh, hi, start=(k == 0), stop=False)
                        pe.matmul(o, xl, hi, start=False, stop=False)
                        mm = pe.matmul(o, xh, lo, start=False, stop=(k == len(parts) - 1))
                    if k in ends:
                        mm.then_inc(dense_done, 1)

            def of_u(k):
                return u_hi[:, k, :], u_lo[:, k, :]

            pe.wait_ge(ones_ready, 1)
            rms(KD, sq)
            pe.wait_ge(consts_in, 16 * 9)
            w = HANK // 2
            for j in range(2):
                mm = pe.matmul(bank[5 + j][0:AH, 0:w], rel[:, :], buckets[:, j * w:(j + 1) * w], start=True, stop=True)
            mm.then_inc(bias_dot, 1)
            column_tiles(st["idx_q"] + st["idx_k"] + st["small"], of_u, 0)
            pe.wait_ge(act_freed, st["small"][0]["freed"][1])
            pe.wait_ge(bias_ready, 1)
            for ti in range(1, NT):
                mm = pe.transpose(bank[5][:, (ti - 1) * IH:ti * IH], small[64:64 + IH, ti * P:(ti + 1) * P],
                                  ident[64:64 + IH, 64:64 + IH])
            mm.then_inc(iw_turned, 1)
            n = 0
            for ti in range(1, NT):
                for h in range(IH):
                    if n >= 2:
                        pe.wait_ge(idx_relu, n - 1)
                    r = slice(64 * (h % 2), 64 * (h % 2) + 64)
                    W = (ti + 1) * P
                    pe.matmul(bank[6 + n % 2][:, 0:W], iq[r, h // 2, ti * P:W], ik[r, 0:W],
                              start=True, stop=True).then_inc(idx_dot, 1)
                    n += 1
            for t in st["att_q"] + st["att_k"]:
                column_tile(t, of_u)
            row_tiles(st["att_v"], of_u)
            row_tiles(st["mem_v"][0:4], of_u)
            row_tiles(st["mem_v"][4:8], of_u)
            pe.wait_ge(rows_ready, 1)
            for ti in range(NT):
                mm = pe.transpose(bank[5][:, ti * MH:(ti + 1) * MH], r_a[:, ti * P:(ti + 1) * P], ident[0:MH, 0:MH])
            mm.then_inc(acol_turned, 1)
            for t in st["att_z"]:
                column_tile(t, of_u)

            def logits(n):
                h, ti = units[n]
                W = (ti + 1) * P
                r = slice(64 * (h % 2), 64 * (h % 2) + 64)
                if n >= 2:
                    pe.wait_ge(da_max, n - 1)
                if ti == 0:
                    pe.wait_ge(hank_in[h % 2], 16 * (h // 2 + 1))
                o = bank[4 + n % 2][:, 0:W]
                pe.matmul(o, att_q[r, h // 2, ti * P:W], att_k[r, h // 2, 0:W], start=True, stop=False)
                pe.matmul(o, flip[:, :], hank[:, h % 2, S - W:S], start=False, stop=True).then_inc(da_logits, 1)

            def turn(n):
                h, ti = units[n]
                pe.wait_ge(da_probs, n + 1)
                if n:
                    pe.wait_ge(da_turned, n)
                for j in range(ti + 1):
                    mm = pe.transpose(bank[6][:, j * P:(j + 1) * P], probs[:, n % 2, j * P:(j + 1) * P], ident[:, :])
                mm.then_inc(da_turn, 1)

            def values(n):
                h, ti = units[n]
                pe.wait_ge(da_turned, n + 1)
                if n:
                    pe.wait_ge(da_out, n)
                for j in range(ti + 1):
                    mm = pe.matmul(bank[7][:, 0:ADH], turned[:, n % 2, j * P:(j + 1) * P],
                                   att_v[:, j, h * ADH:(h + 1) * ADH], start=(j == 0), stop=(j == ti))
                mm.then_inc(da_sum, 1)

            pe.wait_ge(acol_ready, 1)
            logits(0)
            logits(1)
            per = len(units) // 8
            for n in range(len(units)):
                if n + 2 < len(units):
                    logits(n + 2)
                k = n % per * KD // per
                column_tile(st["mem_qk"][n // per], of_u, part=(k, k + KD // per))
                turn(n)
                if n:
                    values(n - 1)
            values(len(units) - 1)
            pe.wait_ge(da_out, len(units))
            for i in range(4):
                if i >= 2:
                    pe.wait_ge(val_ready, n_lo["u"] + i - 1)
                for ti in range(NT):
                    mm = pe.transpose(bank[6 + i % 2][:, ti * P:(ti + 1) * P], att_o[:, ti, i * P:(i + 1) * P],
                                      ident[:, :])
                mm.then_inc(da_back, 1)

            pe.wait_ge(stack_ready, 2)
            oz = st["mem_oz"]

            def memory_spread(h):
                sel = sel_m[:, h * P:(h + 1) * P]
                if h:
                    pe.wait_ge(std_ready, 1 + h)
                pe.matmul(bank[4][:, :], sel, stack_m[:, :], start=True, stop=True)
                pe.matmul(bank[5][:, :], sel, stack_m[:, :], start=True, stop=False)
                pe.matmul(bank[5][:, :], ident_b[:, :], later4_b[:, :], start=False, stop=True).then_inc(ml_spread, 1)

            memory_spread(0)
            for h in range(MH):
                column_tile(oz[4 * h], of_u)
                column_tile(oz[4 * h + 1], of_u, part=(0, 3))
                pe.wait_ge(mem_qk_ready, MH + h + 1)
                pe.wait_ge(ml_decay, h + 1)
                for j in range(NT):
                    if j >= 2:
                        pe.wait_ge(ml_weight, NT * h + j - 1)
                    pe.matmul(bank[4 + j % 2][:, 0:S - j * P], mem_qk[:, MH + h, j * P:(j + 1) * P],
                              mem_qk[:, h, j * P:S], start=True, stop=True).then_inc(ml_score, 1)
                    if j:
                        column_tile(oz[4 * h + 1], of_u, part=((3, 5), (5, 7), (7, 8))[j - 1])
                if h:
                    pe.wait_ge(ml_h, 2 * h)
                else:
                    pe.wait_ge(val_ready, n_lo["mixa"])
                pe.wait_ge(ml_weight, NT * h + NT)
                for j in range(NT):
                    pe.matmul(bank[4][:, j * P:S], ones[:, 0:P], e_t(h, j), start=(j == 0), stop=(j == NT - 1))
                pe.matmul(bank[5][:, :], sel_m[:, h * P:(h + 1) * P], stack_f[:, :], start=True,
                          stop=True).then_inc(ml_sums, 1)
                for v in range(2):
                    for j in range(NT):
                        mm = pe.matmul(bank[6 + v][:, j * P:S], mem_v[:, j, h * MV + v * P:h * MV + (v + 1) * P],
                                       e_t(h, j), start=(j == 0), stop=(j == NT - 1))
                    mm.then_inc(ml_values, 1)
                column_tile(oz[4 * h + 2], of_u)
                column_tile(oz[4 * h + 3], of_u, part=(0, 2))
                pe.wait_ge(ml_floor, 2 * h + 2)
                rms(2, sq_m)
                column_tile(oz[4 * h + 3], of_u, part=(2, 8))
                if h + 1 < MH:
                    memory_spread(h + 1)

            def of_mix(k):
                if k < 4:
                    return mixa_hi[:, k, :], mixa_lo[:, k, :]
                return mix_hi[:, k - 4, :], mix_lo[:, (k - 4) // 2 + MH * (k % 2), :]

            column_tiles(st["out"], of_mix, n_lo["mixa"] - 4)
            column_tiles(st["ple"], lambda k: (p_hi[:, k, :], p_lo[:, k, :]), n_lo["p"] - 2)
            def two_sums(i):
                for k in range(2):
                    pe.wait_ge(sq_ready, n_sq[0] + 1)
                    pe.matmul(bank[4 + k][:, :], ones[:, 0:P], sq_f[:, 2 * (i % 2) + k, :], start=(i == 0),
                              stop=(i == KD - 1)).then_inc(sq_used, 1)
                    n_sq[0] += 1

            for i, t in enumerate(st["gate"]):
                column_tile(t, lambda k: (h_hi[:, k, :], h_lo[:, k, :]), None if i else n_lo["h"] - KD)
                if i >= 2:
                    two_sums(i - 2)
            two_sums(KD - 2)
            two_sums(KD - 1)

            def of_u2(k):
                return u2_hi[:, k, :], u2_lo[:, k, :]

            column_tiles(st["small2"] + st["ssd_b"] + st["ssd_c"], of_u2, n_lo["u2"] - KD)
            pe.wait_ge(acum_ready, 1)
            pe.wait_ge(dte_ready, NT)
            for c in range(NT):
                for i, r in enumerate((r_dt, r_dte, r_ac)):
                    k = SSD_H * (3 * c + i)
                    mm = pe.transpose(bank[5][:, k:k + SSD_H], r[:, c * P:(c + 1) * P], ident[0:SSD_H, 0:SSD_H])
            mm.then_inc(cols_turned, 1)
            pe.wait_ge(stack_a_ready, 1)
            pe.wait_ge(std_ready, n_inv)
            pe.matmul(bank[4][:, 0:2 * SSD_H], ones[0:SSD_H, 0:P], ends_diag[:, :], start=True,
                      stop=True).then_inc(ends_spread, 1)
            for t in st["ssd_x"]:
                column_tile(t, of_u2)
            pe.wait_ge(consts2_in, 16 * 3)

            def spread(p):
                for h in (2 * p, 2 * p + 1):
                    if p:
                        pe.wait_ge(l_ready, h - 1)
                    o = bank[4 + h % 2][:, :]
                    pe.matmul(o, one_hot[:, h:h + 1].broadcast_to([96, P]), stack_a[:, :], start=True, stop=False)
                    pe.matmul(o, ident_b[:, :], later4_b[:, :], start=False, stop=True).then_inc(a_spread, 1)
                if p:
                    pe.wait_ge(e_ready, p)
                else:
                    column_tile(st["z"][0], of_u2, part=(0, 2))
                    pe.wait_ge(conv_ready, len(conv_tiles))
                for h in (2 * p, 2 * p + 1):
                    r = slice(64 * (h % 2), 64 * (h % 2) + 64)
                    mm = pe.matmul(bank[2][r, :], one_hot[:, h:h + 1].broadcast_to([96, SSD_P]), stack_a[:, :],
                                   start=True, stop=True)
                mm.then_inc(e_spread, 1)

            def turn_x(g, c):
                for i in range(4):
                    mm = pe.transpose(bank[6 + c % 2][:, i * P:(i + 1) * P], y[:, 4 * g + i, c * P:(c + 1) * P],
                                      ident[:, :])
                mm.then_inc(x_turned, 1)

            def chunk_state(g, c):
                pe.wait_ge(xdec_ready, 3 * g + c + 1)
                pe.matmul(bank[6 + c % 2][:, :], b_tok[:, c * P:(c + 1) * P], xdec[:, c, :], start=True,
                          stop=True).then_inc(state_dot, 1)

            spread(0)
            pe.wait_ge(cols_ready, 3)
            for g in range(SSD_G):
                if g:
                    column_tile(st["z"][4 * g], of_u2, part=(0, 2))
                    pe.wait_ge(y_read, 4 * g)
                for c in range(NT):
                    mm = pe.matmul(bank[6][:, c * P:(c + 1) * P], b_t[:, g, c * P:(c + 1) * P],
                                   c_t[:, g, c * P:(c + 1) * P], start=True, stop=True)
                mm.then_inc(grp_dot, 1)
                for c in range(3):
                    mm = pe.transpose(bank[7][:, c * P:(c + 1) * P], b_t[:, g, c * P:(c + 1) * P], ident[:, :])
                mm.then_inc(grp_dot, 1)
                pe.wait_ge(grp_copied, 2 * g + 1)
                turn_x(g, 0)
                pe.wait_ge(grp_copied, 2 * g + 2)
                turn_x(g, 1)
                column_tile(st["z"][4 * g], of_u2, part=(2, 4))
                for c in (2, 3):
                    pe.wait_ge(xdt_ready, NT * g + c - 1)
                    turn_x(g, c)
                column_tile(st["z"][4 * g], of_u2, part=(4, 5))
                for c in (0, 1):
                    pe.wait_ge(xdt_ready, NT * g + c + 3)
                    chunk_state(g, c)
                column_tile(st["z"][4 * g], of_u2, part=(5, 6))
                pe.wait_ge(state_ready, 3 * g + 1)
                chunk_state(g, 2)
                column_tile(st["z"][4 * g], of_u2, part=(6, 8))
                for q in range(4):
                    p = 4 * g + q
                    if q:
                        column_tile(st["z"][p], of_u2)
                    if g and q == 2:
                        rms(4, sq_y, 3)
                    if p + 1 < 16:
                        spread(p + 1)
                    if q == 0:
                        pe.wait_ge(state_ready, 3 * (g + 1))
                    else:
                        pe.wait_ge(y_read, p)
                    for h in (2 * p, 2 * p + 1):
                        pe.wait_ge(w_ready, h + 1)
                        r, f = slice(64 * (h % 2), 64 * (h % 2) + 64), (h % 8) * SSD_P
                        for c in range(NT):
                            mm = pe.matmul(bank[6][r, c * P:(c + 1) * P], xdt[:, c, f:f + SSD_P],
                                           weight(h)[:, c * P:(c + 1) * P], start=True, stop=True)
                        mm.then_inc(y_dot, 1)
                    for c in range(1, NT):
                        mm = pe.matmul(bank[7][:, c * P:(c + 1) * P], states[:, c - 1, q * P:(q + 1) * P],
                                       c_t[:, g, c * P:(c + 1) * P], start=True, stop=True)
                    mm.then_inc(off_dot, 1)
            column_tile(st["qa"][0], of_u2)
            column_tile(st["qa"][1], of_u2)
            rms(4, sq_y, 3)
            column_tile(st["kva"][0], of_u2)
            pe.wait_ge(e_ready, 16)
            for i, t in enumerate(st["ssd_out"]):
                column_tile(t, lambda k: (y_hi[:, k, :], y_lo[:, k, :]), None if i else n_lo["y"] - 16)
                if i < 2:
                    rms(2 - i, sq_s)

            pe.wait_ge(lo_ready, n_lo["kn"])
            for half in range(2):
                row_tiles(st["v"][4 * half:4 * half + 4], lambda k: (kn_hi, kn_lo))

            def project(h):
                if h:
                    pe.wait_ge(std_qk_ready, 2 * h)
                    pe.wait_ge(k_ready, h)
                column_tile(st["head_q"][h], lambda k: (qn_hi[:, k, :], qn_lo[:, k, :]))
                column_tile(st["head_k"][h], lambda k: (kn_hi[:, :], kn_lo[:, :]))

            def norm_sums(h):
                pe.wait_ge(head_sq, 2 * h + 2)
                if h == 0:
                    pe.wait_ge(krope_sq, 1)
                pe.wait_ge(dve_freed, st["head_q"][h]["freed"][1])
                for i, src in enumerate((sq_q, sq_k)):
                    for ti in range(NT):
                        k = NT * i + ti
                        mm = pe.matmul(bank[1][:, k:k + 1], src[:, ti * P:(ti + 1) * P], ones[0:QK, 0:1], start=True,
                                       stop=True)
                mm.then_inc(head_sums, 1)

            def key_spread(h):
                pe.wait_ge(rk_diag_ready, h + 1)
                pe.wait_ge(dve_freed, st["head_k"][h]["freed"][1])
                pe.matmul(bank[2][0:QK, :], ones[:, 0:QK], rk_diag[:, :], start=True, stop=True).then_inc(rk_spread, 1)

            def head_logits(n):
                h, ti = heads[n]
                W = (ti + 1) * P
                if ti == 0:
                    pe.wait_ge(k_ready, h + 1)
                    pe.wait_ge(dve_freed, st["head_q"][h]["freed"][1])
                if n >= 2:
                    pe.wait_ge(x_probs, n - 1)
                o = bank[4 + n % 2]
                pe.matmul(o[:, 0:W], q_s[:, h % 2, ti * P:W], k_s[:, h % 2, 0:W], start=True, stop=False)
                pe.matmul(o[:, ti * P:W], ident_b[:, :], tri_b[:, :], start=False, stop=True).then_inc(x_logits, 1)

            def head_turn(n):
                h, ti = heads[n]
                pe.wait_ge(x_probs, n + 1)
                if n:
                    pe.wait_ge(x_turned_out, n)
                for j in range(ti + 1):
                    mm = pe.transpose(bank[6][:, j * P:(j + 1) * P], probs_x[:, n % 2, j * P:(j + 1) * P], ident[:, :])
                mm.then_inc(x_turn, 1)

            def head_values(n):
                h, ti = heads[n]
                pe.wait_ge(x_turned_out, n + 1)
                if n:
                    pe.wait_ge(x_out, n)
                o = bank[7][:, 0:VD]
                for j in range(ti + 1):
                    mm = pe.matmul(o, turned_x[n % 2][:, j * P:(j + 1) * P], v_tok[:, j, h * VD:(h + 1) * VD],
                                   start=(j == 0), stop=(j == ti))
                mm.then_inc(x_sum, 1)

            project(0)
            column_tile(st["mix_gate"][0], of_u2, part=(0, 4))
            norm_sums(0)
            column_tile(st["mix_gate"][0], of_u2, part=(4, 7))
            key_spread(0)
            project(1)
            column_tile(st["mix_gate"][0], of_u2, part=(7, 8))
            head_logits(0)
            head_logits(1)
            for n, (h, ti) in enumerate(heads):
                if n + 2 < len(heads):
                    head_logits(n + 2)
                if ti == 0 and h + 1 < XH:
                    norm_sums(h + 1)
                if ti == 1 and h + 1 < XH:
                    key_spread(h + 1)
                if ti == 2 and h + 2 < XH:
                    project(h + 2)
                if h:
                    column_tile(st["mix_gate"][h], of_u2, part=((0, 3), (3, 5), (5, 6), (6, 8))[ti])
                head_turn(n)
                if n:
                    head_values(n - 1)
            head_values(len(heads) - 1)
            pe.wait_ge(x_out, len(heads))
            for i in range(KD):
                if i >= 2:
                    pe.wait_ge(lo_ready, n_lo["kn"] + i - 1)
                for ti in range(NT):
                    mm = pe.transpose(bank[6 + i % 2][:, ti * P:(ti + 1) * P], o_tok[:, ti, i * P:(i + 1) * P],
                                      ident[:, :])
                mm.then_inc(o_back, 1)

            column_tiles(st["mla_out"], lambda k: (o_hi[:, k, :], o_lo[:, k, :]), n_lo["o"] - KD)
            for i, t in enumerate(st["mix_out"]):
                column_tile(t, lambda k: (fused_hi[:, k, :], fused_lo[:, k, :]), None if i else n_lo["fused"] - KD)
                if i:
                    square_sum(i - 1, KD, sq_x)
            square_sum(KD - 1, KD, sq_x)
            column_tiles(st["up"], lambda k: (u3_hi[:, k, :], u3_lo[:, k, :]), n_lo["u3"] - KD)
            column_tiles(st["down"], lambda k: (act_hi[:, k, :], act_lo[:, k, :]), n_lo["act"] - FT)


        @block.scalar
        def _(act):
            next_hi, steps, evs, sqs, his = [0], [0], [0], [0], [0]

            def split_weights(done):
                while next_hi[0] <= min(done + RING, N_CHUNK - 1):
                    c = next_hi[0]
                    act.wait_ge(w_landed[c % RING], 16 * (c // RING + 1))
                    if c >= RING:
                        act.wait_ge(dense_done, plan.used_at[c - RING])
                    act.activation(w_hi[:, c % RING, :], w_raw[:, c % RING, :], ACT.Copy).then_inc(w_hi_ready, 1)
                    next_hi[0] += 1

            def after(t):
                split_weights(t["upto"])

            def link(ins):
                steps[0] += 1
                ins.then_inc(act_step, 1)
                act.wait_ge(act_step, steps[0])

            def rms(src, n, width, sq, std, b=4):
                for i in range(n):
                    if sqs[0] >= 2:
                        act.wait_ge(sq_used, sqs[0] - 1)
                    act.activation(sq[:, i % 2, :], src(i), ACT.Square).then_inc(sq_ready, 1)
                    sqs[0] += 1
                act.wait_ge(sq_used, sqs[0])
                act.activation(std[:, :], bank[b][:, :], ACT.Sqrt, bias=vec("eps"),
                               scale=1.0 / width).then_inc(std_ready, 1)

            vals = [0]

            def high_parts(dst, src, n):
                for i in range(n):
                    vals[0] += 1
                    act.wait_ge(val_ready, vals[0])
                    act.activation(dst(i), src(i), ACT.Copy).then_inc(hi_ready, 1)

            def tile_done(t):
                act.wait_ge(dense_done, t["full"])

            def rows_out(tiles, dst):
                for c, s in tiles[0]["parts"][:-1]:
                    if s == CH * P // S - 1:
                        split_weights(c)
                for i in (0, 2):
                    tile_done(tiles[i])
                    act.copy(dst(i), bank[tiles[i]["bank"]][:, :]).then_inc(act_freed, 1)
                after(tiles[0])

            def sigmoid_of(t):
                tile_done(t)
                if evs[0] >= 2:
                    act.wait_ge(ev_used, evs[0] - 1)
                act.activation(ev[:, evs[0] % 2, :], bank[t["bank"]][:, :], ACT.Sigmoid).then_inc(ev_ready, 1)
                evs[0] += 1
                after(t)

            for dst, name in ((ident, "ident"), (flip, "flip"), (tri, "tri"), (ident_b, "ident_b"),
                              (later4_b, "later4_b"), (vecs, "vecs"), (sel_m, "sel_m"), (rel, "rel"),
                              (buckets, "buckets")):
                act.dma_start(dst[:, :], a[name]).then_inc(consts_in, 16)

            def x_tile(i):
                act.wait_ge(x_in[i], 16)
                return xt[:, i, :]

            act.wait_ge(consts_in, 16 * 9)
            rms(x_tile, KD, D, sq, rms_std)
            split_weights(-1)
            act.wait_ge(bias_dot, 1)
            w = HANK // 2
            for j in range(2):
                ins = act.mul(bias_row[:, j * w:(j + 1) * w], bank[5 + j][0:AH, 0:w], ADH ** 0.5)
                ins.then_inc(bias_out, 1)
            act.wait_ge(bias_out, 2)
            act.dma_start(bias_dram, bias_row[:, :]).then_inc(stored, 16)
            act.sem_inc(bias_ready, 1)
            high_parts(lambda i: u_hi[:, i, :], lambda i: u_val[:, i % 2, :], KD)
            for i, t in enumerate(st["idx_q"]):
                tile_done(t)
                act.mul(iq[:, i, :], bank[t["bank"]][:, :], IDH ** -0.5).then_inc(act_freed, 1)
                after(t)
            t = st["idx_k"][0]
            tile_done(t)
            act.copy(ik[:, :], bank[t["bank"]][:, :]).then_inc(act_freed, 1)
            after(t)
            t = st["small"][0]
            tile_done(t)
            act.activation(small[:, :], bank[t["bank"]][:, :], ACT.Identity, bias=vec("gate_bias"),
                           scale=vec("gate_scale")).then_inc(act_freed, 1)
            after(t)
            act.wait_ge(iw_turned, 1)
            act.copy(iw[:, :, :].rearrange("p a b -> p (a b)"), bank[5][:, 0:3 * IH]).then_inc(iw_ready, 1)
            n = 0
            for ti in range(1, NT):
                W = (ti + 1) * P
                for h in range(IH):
                    act.wait_ge(idx_dot, n + 1)
                    if n >= 2:
                        act.wait_ge(idx_added, n - 1)
                    act.activation(relu[:, n % 2, 0:W], bank[6 + n % 2][:, 0:W], ACT.Relu).then_inc(idx_relu, 1)
                    n += 1
            for name, dst in (("att_q", att_q), ("att_k", att_k)):
                for i, t in enumerate(st[name]):
                    tile_done(t)
                    act.copy(dst[:, i, :], bank[t["bank"]][:, :]).then_inc(act_freed, 1)
                    after(t)
            rows_out(st["att_v"], lambda i: att_v[:, i, :])
            act.wait_ge(ml_f, 1)
            link(act.activation(r_t[:, :], r_f[:, :], ACT.Abs))
            link(act.activation(r_t[:, :], r_t[:, :], ACT.Exp, scale=-1.0))
            act.activation(r_t[:, :], r_t[:, :], ACT.Ln, bias=1.0).then_inc(ml_log, 1)
            for half in range(2):
                rows_out(st["mem_v"][4 * half:4 * half + 4], lambda i: mem_v[:, i, half * S:(half + 1) * S])
            act.wait_ge(acol_turned, 1)
            act.copy(acol[:, :], bank[5][:, 0:NT * MH]).then_inc(acol_ready, 1)
            def load_bias(h):
                if h >= 2:
                    act.wait_ge(da_logits, NT * (h - 1))
                src = bass.AP(bias_dram.tensor, h * HANK, [[1, P], [1, S]])
                act.dma_start(hank[:, h % 2, :], src).then_inc(hank_in[h % 2], 16)

            act.wait_ge(stored, 16)
            load_bias(0)
            load_bias(1)
            act.wait_ge(chosen_ready, NT)
            for t in st["att_z"]:
                sigmoid_of(t)

            def newest_tap(i):
                t = st["mem_qk"][i]
                tile_done(t)
                if evs[0] >= 2:
                    act.wait_ge(ev_used, evs[0] - 1)
                act.activation(ev[:, evs[0] % 2, :], bank[t["bank"]][:, :], ACT.Copy,
                               scale=vec("conv_w", 4 * i + 3)).then_inc(ev_ready, 1)
                evs[0] += 1
                after(t)

            def conv_sigmoid(i):
                act.wait_ge(taps_ready, i + 1)
                if i:
                    act.wait_ge(mem_qk_ready, i)
                act.activation(sg[:, :], mem_qk[:, i, :], ACT.Sigmoid).then_inc(sg_ready, 1)

            def da_exp(n):
                h, ti = units[n]
                W = (ti + 1) * P
                act.wait_ge(da_max, n + 1)
                act.activation(probs[:, n % 2, 0:W], probs[:, n % 2, 0:W], ACT.Exp, bias=da_cols[:, 1, n:n + 1],
                               scale=ADH ** -0.5, accum_out=da_cols[:, 2, n:n + 1]).then_inc(da_probs, 1)

            da_exp(0)
            for n, (h, ti) in enumerate(units):
                W = (ti + 1) * P
                if n + 1 < len(units):
                    da_exp(n + 1)
                if ti == 3 and h < AH - 2:
                    load_bias(h + 2)
                if ti == 0 and h:
                    newest_tap(h - 1)
                if ti == 2 and h:
                    conv_sigmoid(h - 1)
                act.wait_ge(da_turn, n + 1)
                if n >= 2:
                    act.wait_ge(da_sum, n - 1)
                act.copy(turned[:, n % 2, 0:W], bank[6][:, 0:W]).then_inc(da_turned, 1)
            newest_tap(AH - 1)
            conv_sigmoid(AH - 1)
            high_parts(lambda i: mixa_hi[:, i, :], lambda i: val_m[:, i % 2, :], 4)

            act.wait_ge(stack_ready, 2)
            oz = st["mem_oz"]

            def decays(h):
                act.wait_ge(ml_spread, h + 1)
                if h >= 2:
                    act.wait_ge(ml_sums, h - 1)
                for j in range(NT):
                    col = acol[:, j * MH + h:j * MH + h + 1]
                    e = e_t(h, j)
                    if j < NT - 1:
                        act.activation(e[:, P:], bank[4][:, (j + 1) * P:S], ACT.Exp, bias=col)
                    ins = act.activation(e[:, 0:P], bank[5][:, j * P:(j + 1) * P], ACT.Exp, bias=col)
                ins.then_inc(ml_decay, 1)

            def out_gate(h, k):
                t = oz[4 * h + k]
                if k % 2:
                    sigmoid_of(t)
                else:
                    tile_done(t)
                    act.activation(mem_o[:, 2 * h + k // 2, :], bank[t["bank"]][:, :],
                                   ACT.Sigmoid).then_inc(act_freed, 1)
                    after(t)

            decays(0)
            for h in range(MH):
                out_gate(h, 0)
                out_gate(h, 1)
                act.wait_ge(ml_sums, h + 1)
                if h:
                    act.wait_ge(ml_h, 2 * h)
                act.activation(den[:, :], bank[4][:, :], ACT.Abs).then_inc(ml_floor, 1)
                act.activation(floor[:, :], bank[5][:, :], ACT.Exp).then_inc(ml_floor, 1)
                out_gate(h, 2)
                for v in range(2):
                    act.wait_ge(ml_h, 2 * h + v + 1)
                    act.activation(sq_m[:, v, :], h_val[:, v, :], ACT.Square).then_inc(sq_ready, 1)
                    sqs[0] += 1
                act.wait_ge(sq_used, sqs[0])
                if h:
                    act.wait_ge(inv_ready, 1 + h)
                act.activation(std_m[:, :], bank[4][:, :], ACT.Sqrt, bias=vec("eps"),
                               scale=1.0 / MV).then_inc(std_ready, 1)
                if h + 1 < MH:
                    decays(h + 1)
                out_gate(h, 3)
                if h == MH - 1:
                    act.dma_start(xt2[:, :, :], a["x_t"]).then_inc(x2_in, 16)
                    act.dma_start(p_val[:, :, :], a["p_t"]).then_inc(p_in, 16)
                high_parts(lambda i: mix_hi[:, 2 * h + i, :], lambda i: val_m[:, i, :], 2)
            act.wait_ge(p_in, 16)
            for i in range(2):
                act.activation(p_hi[:, i, :], p_val[:, i, :], ACT.Copy).then_inc(hi_ready, 1)
            for i, t in enumerate(st["out"]):
                tile_done(t)
                after(t)
                act.wait_ge(h_res_ready, i + 1)
                act.activation(h_hi[:, i, :], h_res[:, i, :], ACT.Copy).then_inc(hi_ready, 1)
            for i, t in enumerate(st["ple"]):
                tile_done(t)
                act.copy(ple[:, i, :], bank[t["bank"]][:, :]).then_inc(act_freed, 1)
                after(t)

            def two_squares(i):
                act.wait_ge(ple_added, i + 1)
                for k, scale in enumerate((1.0, vec("norm_final", i))):
                    if sqs[0] >= 3:
                        act.wait_ge(sq_used, sqs[0] - (3 if i >= 2 else 0))
                    act.activation(sq_f[:, 2 * (i % 2) + k, :], h_res[:, i, :], ACT.Square,
                                   scale=scale).then_inc(sq_ready, 1)
                    sqs[0] += 1

            for i, t in enumerate(st["gate"]):
                tile_done(t)
                if i >= 2:
                    act.wait_ge(ple_added, i - 1)
                act.activation(gate[:, i % 2, :], bank[t["bank"]][:, :], ACT.Sigmoid).then_inc(act_freed, 1)
                after(t)
                if i:
                    two_squares(i - 1)
            two_squares(KD - 1)
            act.wait_ge(norm_sums_in, 1)
            act.activation(std_f[:, :], std_f[:, :], ACT.Sqrt, bias=vec("eps2"), scale=1.0 / D).then_inc(std_ready, 1)
            act.activation(std_g[:, :], bank[4][:, :], ACT.Sqrt, bias=vec("eps"), scale=1.0 / D).then_inc(std_ready, 1)
            high_parts(lambda i: u2_hi[:, i, :], lambda i: val_f[:, i % 2, :], KD)

            for dst, name in ((one_hot, "one_hot"), (trig, "trig"), (tri_b, "tri_b")):
                act.dma_start(dst[:, :], a[name]).then_inc(consts2_in, 16)
            t = st["small2"][0]
            tile_done(t)
            act.activation(small2[:, :], bank[t["bank"]][:, :], ACT.Identity, bias=vec("dt_bias")).then_inc(act_freed, 1)
            after(t)
            act.wait_ge(act_freed, t["freed"][1])
            link(act.activation(r_t2[:, :], small2[0:SSD_H, :], ACT.Abs))
            link(act.activation(r_t2[:, :], r_t2[:, :], ACT.Exp, scale=-1.0))
            act.activation(rate[:, :], vecs[0:SSD_H, VEC["a_log"][0]:VEC["a_log"][0] + 1], ACT.Exp).then_inc(rate_ready, 1)
            act.activation(r_t2[:, :], r_t2[:, :], ACT.Ln, bias=1.0).then_inc(dt_log, 1)
            for i in range(len(conv_tiles) + 1):
                if i < len(conv_tiles):
                    t, w, _ = conv_tiles[i]
                    tile_done(t)
                    if i >= 2:
                        act.wait_ge(conv_ready, i - 1)
                    act.activation(taps[:, i % 2, :], bank[t["bank"]][:, :], ACT.Identity, bias=vec("ssd_conv_b", w),
                                   scale=vec("ssd_conv_w", 4 * w + 3)).then_inc(conv_in, 1)
                    after(t)
                if i == 2:
                    act.wait_ge(acum_ready, 1)
                    for c in range(NT):
                        act.activation(r_dte[:, c * P:(c + 1) * P], r_ac[:, c * P:(c + 1) * P], ACT.Exp, scale=-1.0,
                                       bias=r_ac[:, (c + 1) * P - 1:(c + 1) * P]).then_inc(dte_ready, 1)
                if i == 10:
                    act.wait_ge(cols_turned, 1)
                    act.copy(cols[:, :, :].rearrange("p a b -> p (a b)"), bank[5][:, 0:3 * NT * SSD_H]
                             ).then_inc(cols_ready, 1)
                    act.wait_ge(cols_ready, 1)
                    for c in range(NT):
                        ins = act.mul(cols[:, 3 * c + 2, :], cols[:, 3 * c + 2, :], -1.0)
                    ins.then_inc(cols_ready, 1)
                    act.wait_ge(ends_spread, 1)
                    act.activation(chunk_decay[:, :], bank[4][:, 0:2 * SSD_H], ACT.Exp).then_inc(cols_ready, 1)
                if i:
                    act.wait_ge(dve_freed, conv_tiles[i - 1][0]["freed"][1])
                    act.activation(taps_sg[:, (i - 1) % 2, :], taps[:, (i - 1) % 2, :], ACT.Sigmoid).then_inc(conv_sg, 1)

            def decays(p):
                for h in (2 * p, 2 * p + 1):
                    act.wait_ge(a_spread, h + 1)
                    if h >= 4:
                        act.wait_ge(y_dot, h - 3)
                    for c in range(NT):
                        ins = act.activation(weight(h)[:, c * P:(c + 1) * P], bank[4 + h % 2][:, c * P:(c + 1) * P],
                                             ACT.Exp, bias=cols[:, 3 * c + 2, h:h + 1])
                    ins.then_inc(l_ready, 1)
                act.wait_ge(e_spread, p + 1)
                if p >= 2:
                    act.wait_ge(y_ready, p - 1)
                act.activation(e_ac[:, p % 2, :], bank[2][:, :], ACT.Exp).then_inc(e_ready, 1)

            act.wait_ge(stack_a_ready, 2)
            act.wait_ge(conv_ready, len(conv_tiles))
            decays(0)
            for g in range(SSD_G):
                act.wait_ge(grp_dot, 2 * g + 1)
                if g:
                    act.wait_ge(w_ready, 8 * g)
                act.copy(scores[:, :], bank[6][:, :]).then_inc(grp_copied, 1)
                act.wait_ge(grp_dot, 2 * g + 2)
                act.copy(b_tok[:, :], bank[7][:, 0:3 * P]).then_inc(grp_copied, 1)
                for p in range(4 * g, 4 * g + 4):
                    t = st["z"][p]
                    tile_done(t)
                    if p:
                        act.wait_ge(y_ready, p)
                    act.activation(z_sg[:, :], bank[t["bank"]][:, :], ACT.Sigmoid).then_inc(z_ready, 1)
                    after(t)
                    if p + 1 < 16:
                        decays(p + 1)
                    if g and p % 4 == 1:
                        rms(lambda i: y[:, 4 * (g - 1) + i, :], 4, 512, sq_y, std_y, 3)
            act.wait_ge(y_ready, 16)

            def y_high(first, end):
                for i in range(first, end):
                    act.wait_ge(y_normed, i + 1)
                    act.activation(y_hi[:, i, :], y[:, i, :], ACT.Copy).then_inc(hi_ready, 1)

            def latent(t, dst):
                tile_done(t)
                act.copy(dst, bank[t["bank"]][:, :]).then_inc(act_freed, 1)
                after(t)

            rms(lambda i: y[:, 12 + i, :], 4, 512, sq_y, std_y, 3)
            latent(st["qa"][0], qa_val[:, 0, :])
            y_high(0, 4)
            latent(st["qa"][1], qa_val[:, 1, :])
            y_high(4, 12)
            latent(st["kva"][0], kva_val[:, :])
            y_high(12, 16)
            act.wait_ge(act_freed, st["kva"][0]["freed"][1])
            rms(lambda i: qa_val[:, i, :], 2, 256, sq_s, std_s)
            after(st["ssd_out"][0])
            high_parts(lambda i: qn_hi[:, i, :], lambda i: qa_val[:, i, :], 2)
            act.wait_ge(inv_ready, n_inv + SSD_G + 1)
            rms(lambda i: kva_val[:, :], 1, 128, sq_s, std_s)
            after(st["ssd_out"][1])
            high_parts(lambda i: kn_hi[:, :], lambda i: kva_val[:, :], 1)
            for i, t in enumerate(st["ssd_out"]):
                for c, s in t["parts"][:-1]:
                    if s == CH - 1:
                        split_weights(c)
                tile_done(t)
                act.copy(y_ssd[:, i, :], bank[t["bank"]][:, :]).then_inc(act_freed, 1)
                after(t)

            for half in range(2):
                rows_out(st["v"][4 * half:4 * half + 4], lambda i: v_tok[:, i, half * S:(half + 1) * S])
            act.activation(sq_k[NOPE:QK, :], small2[NOPE:QK, :], ACT.Square).then_inc(krope_sq, 1)

            def head_parts(h):
                tq, tk2 = st["head_q"][h], st["head_k"][h]
                tile_done(tk2)
                if h:
                    act.wait_ge(head_sums, h)
                act.activation(sq_q[:, :], bank[tq["bank"]][0:QK, :], ACT.Square).then_inc(head_sq, 1)
                act.activation(sq_k[0:NOPE, :], bank[tk2["bank"]][0:NOPE, :], ACT.Square).then_inc(head_sq, 1)
                after(tk2)

            def head_norms(h):
                act.wait_ge(head_sums, h + 1)
                if h >= 2:
                    act.wait_ge(x_probs, NT * (h - 1))
                    act.wait_ge(rk_diag_ready, h - 1)
                r = r_qk[:, h % 2, :]
                act.activation(r[:, 0:NT], bank[1][:, 0:NT], ACT.Sqrt, bias=vec("eps_q")).then_inc(std_qk_ready, 1)
                act.activation(r[:, NT:2 * NT], bank[1][:, NT:2 * NT], ACT.Sqrt, bias=vec("eps"),
                               scale=1.0 / QK).then_inc(std_qk_ready, 1)

            def mix_gate(h):
                t = st["mix_gate"][h]
                tile_done(t)
                if h >= KD:
                    act.wait_ge(gates_used, h - KD + 1)
                act.activation(gm[:, h % KD, :], bank[t["bank"]][:, :], ACT.Sigmoid,
                               bias=vec("gate_b", h)).then_inc(act_freed, 1)

            def head_probs(n):
                h, ti = heads[n]
                W = (ti + 1) * P
                act.wait_ge(x_max, n + 1)
                if n >= 2:
                    act.wait_ge(x_turn, n - 1)
                act.activation(probs_x[:, n % 2, 0:W], bank[4 + n % 2][:, 0:W], ACT.Exp, bias=x_cols[:, 1, n:n + 1],
                               scale=r_qk[:, h % 2, ti:ti + 1], accum_out=x_cols[:, 2, n:n + 1]).then_inc(x_probs, 1)

            def head_turned(n):
                W = (heads[n][1] + 1) * P
                act.wait_ge(x_turn, n + 1)
                if n >= 2:
                    act.wait_ge(x_sum, n - 1)
                act.copy(turned_x[n % 2][:, 0:W], bank[6][:, 0:W]).then_inc(x_turned_out, 1)

            head_parts(0)
            head_norms(0)
            head_parts(1)
            head_probs(0)
            for n, (h, ti) in enumerate(heads):
                if ti == 1 and h:
                    mix_gate(h - 1)
                if n + 1 < len(heads):
                    head_probs(n + 1)
                if ti == 0 and h + 1 < XH:
                    head_norms(h + 1)
                if ti == 3 and h + 2 < XH:
                    head_parts(h + 2)
                head_turned(n)
                if ti == 1 and h:
                    after(st["mix_gate"][h - 1])
            mix_gate(XH - 1)
            after(st["mix_gate"][XH - 1])
            for i in range(KD):
                act.wait_ge(o_back, i + 1)
                act.activation(o_hi[:, i, :], bank[6 + i % 2][:, :], ACT.Copy).then_inc(hi_ready, 1)

            for i, t in enumerate(st["mla_out"]):
                tile_done(t)
                after(t)
                high_parts(lambda _: fused_hi[:, i, :], lambda _: gm[:, i, :], 1)
            for i, t in enumerate(st["mix_out"]):
                tile_done(t)
                after(t)
                act.wait_ge(dve_freed, t["freed"][1])
                act.wait_ge(sq_used, sqs[0] - 1)
                act.activation(sq_x[:, i % 2, :], h_res[:, i, :], ACT.Square).then_inc(sq_ready, 1)
                sqs[0] += 1
            act.wait_ge(sq_used, sqs[0])
            act.activation(std_x[:, :], bank[4][:, :], ACT.Sqrt, bias=vec("eps"), scale=1.0 / D).then_inc(std_ready, 1)
            high_parts(lambda i: u3_hi[:, i, :], lambda i: val_x[:, i % 2, :], KD)
            for i in range(2 * FT + 1):
                if i < 2 * FT:
                    t, d = st["up"][i], (ffn_g, ffn_v)[i % 2]
                    tile_done(t)
                    if i >= 4:
                        act.wait_ge(lo_ready, n_lo["u3"] + i // 2 - 1)
                    act.activation(d[:, i // 2 % 2, :], bank[t["bank"]][:, :], ACT.Identity, bias=vec("ffn_conv_b", i),
                                   scale=vec("ffn_conv_w", 3 * i + 2)).then_inc(act_in, 1)
                    after(t)
                if i >= 2 and i % 2 == 0:
                    k = i // 2 - 1
                    act.wait_ge(dve_freed, st["up"][2 * k]["freed"][1])
                    act.activation(ffn_sg[:, k % 2, :], ffn_g[:, k % 2, :], ACT.Sigmoid).then_inc(act_sg, 1)
                    high_parts(lambda _: act_hi[:, k, :], lambda _: ffn_g[:, k % 2, :], 1)
            for t in st["down"]:
                for c, s in t["parts"][:-1]:
                    if s == CH - 1:
                        split_weights(c)
                tile_done(t)
                after(t)

        @block.vector
        def _(dve):
            steps, his, vals, evs, frees, invs = [0], [0], [0], [0], [0], [0]

            def link(ins):
                steps[0] += 1
                ins.then_inc(dve_step, 1)
                dve.wait_ge(dve_step, steps[0])

            def split(n, make, src, hi, lo):
                for i in range(n + 1):
                    if i < n:
                        if his[0]:
                            dve.wait_ge(lo_ready, his[0])
                        make(i).then_inc(val_ready, 1)
                        vals[0] += 1
                    if i:
                        dve.wait_ge(val_ready, vals[0] - (1 if i < n else 0))
                        low(src(i - 1), hi(i - 1), lo(i - 1))

            def low(src, hi, lo):
                his[0] += 1
                dve.wait_ge(hi_ready, his[0])
                dve.tensor_tensor(lo, src, hi.bitcast(F32), ALU.subtract).then_inc(lo_ready, 1)

            def inverse(inv, std):
                invs[0] += 1
                dve.wait_ge(std_ready, invs[0])
                dve.reciprocal(inv[:, :], std[:, :]).then_inc(inv_ready, 1)
                dve.wait_ge(inv_ready, invs[0])

            def free(ins):
                frees[0] += 1
                ins.then_inc(dve_freed, 1)

            def silu(dst, t):
                evs[0] += 1
                dve.wait_ge(ev_ready, evs[0])
                free(dve.tensor_tensor(dst, bank[t["bank"]][:, :], ev[:, (evs[0] - 1) % 2, :], ALU.mult))
                dve.wait_ge(dve_freed, frees[0])
                dve.sem_inc(ev_used, 1)

            def rows_out(tiles, dst):
                for i in (1, 3):
                    dve.wait_ge(dense_done, tiles[i]["full"])
                    free(dve.tensor_copy(dst(i), bank[tiles[i]["bank"]][:, :]))

            dve.memset(ones[:, :], 1.0).then_inc(ones_ready, 1)
            inverse(rms_inv, rms_std)
            split(KD, lambda i: dve.scalar_tensor_tensor(u_val[:, i % 2, :], xt[:, i, :], vec("norm_in", i),
                                                         rms_inv[:, :], ALU.mult, ALU.mult),
                  lambda i: u_val[:, i % 2, :], lambda i: u_hi[:, i, :], lambda i: u_lo[:, i, :])
            dve.wait_ge(iw_ready, 1)
            n = 0
            for ti in range(1, NT):
                W = (ti + 1) * P
                sc = score[:, ti - 1, 0:W]
                for h in range(IH):
                    dve.wait_ge(idx_relu, n + 1)
                    w = iw[:, ti - 1, h:h + 1]
                    if h == 0:
                        dve.tensor_scalar(sc, relu[:, n % 2, 0:W], w, None, ALU.mult).then_inc(idx_added, 1)
                    else:
                        dve.wait_ge(idx_added, n)
                        dve.scalar_tensor_tensor(sc, relu[:, n % 2, 0:W], w, sc, ALU.mult,
                                                 ALU.add).then_inc(idx_added, 1)
                    n += 1
                dve.wait_ge(idx_added, n)
                d = score[:, ti - 1, ti * P:W]
                link(dve.tensor_tensor(d, d, tri[:, :], ALU.add))

            def wk(ti):
                return work[:, ti - 1, 0:(ti + 1) * P] if ti < 3 else work2[:, :]

            for ti in range(1, NT):
                dve.tensor_copy(wk(ti), score[:, ti - 1, 0:(ti + 1) * P]).then_inc(top_gone, 1)
            rounds = TOPK // 8 - 1
            for r in range(rounds):
                for ti in range(1, NT):
                    dve.wait_ge(top_gone, 3 * r + ti)
                    dve.max(top8[:, ti - 1, :], wk(ti)).then_inc(top_found, 1)
                for ti in range(1, NT):
                    dve.wait_ge(top_found, 3 * r + ti)
                    dve.match_replace(wk(ti), top8[:, ti - 1, :], wk(ti), -3e38).then_inc(top_gone, 1)
            for ti in range(1, NT):
                dve.wait_ge(top_gone, 3 * rounds + ti)
                dve.max(top8[:, ti - 1, :], wk(ti)).then_inc(top_found, 1)
            dve.tensor_copy(chosen[:, 0, 0:P], tri[:, :]).then_inc(chosen_ready, 1)
            for ti in range(1, NT):
                W = (ti + 1) * P
                dve.wait_ge(top_found, 3 * rounds + ti)
                sc, th = score[:, ti - 1, 0:W], top8[:, ti - 1, 7:8]
                gt, eq, cs = relu[:, 0, 0:W], relu[:, 1, 0:W], wk(ti)
                cnt, need = tk[:, ti - 1, 0:1], tk[:, ti - 1, 1:2]
                link(dve.tensor_scalar(gt, sc, th, 0.0, ALU.is_gt, ALU.add, accum_out=cnt))
                link(dve.tensor_scalar(need, cnt, -1.0, float(TOPK), ALU.mult, ALU.add))
                link(dve.tensor_scalar(eq, sc, th, None, ALU.is_equal))
                link(dve.tensor_tensor_scan(cs, ones[:, 0:W], eq, 0.0, ALU.mult, ALU.add))
                link(dve.scalar_tensor_tensor(eq, cs, need, eq, ALU.is_le, ALU.mult))
                link(dve.tensor_tensor(gt, gt, eq, ALU.add))
                dve.tensor_scalar(chosen[:, ti, 0:W], gt, -NEG, NEG, ALU.mult, ALU.add).then_inc(chosen_ready, 1)
                dve.wait_ge(chosen_ready, ti + 1)

            dve.tensor_copy(r_f[:, :], small[32:32 + MH, :]).then_inc(ml_f, 1)
            rows_out(st["att_v"], lambda i: att_v[:, i, :])
            dve.wait_ge(ml_log, 1)
            link(dve.scalar_tensor_tensor(r_lf[:, :], r_f[:, :], 0.0, r_t[:, :], ALU.min, ALU.subtract))
            link(dve.tensor_tensor_scan(r_b[:, :], ones[0:MH, :], r_lf[:, :], 0.0, ALU.mult, ALU.add))
            link(dve.tensor_tensor(r_a[:, :], small[0:MH, :], r_b[:, :], ALU.subtract))
            dve.sem_inc(rows_ready, 1)
            link(dve.tensor_tensor_scan(r_m[:, :], ones[0:MH, :], r_a[:, :], 0.0, ALU.mult, ALU.max))
            for stack, first in ((stack_m, True), (stack_f, False)):
                if first:
                    link(dve.tensor_scalar(r_n[:, :], r_m[:, :], -1.0, None, ALU.mult))
                else:
                    link(dve.scalar_tensor_tensor(r_n[:, :], r_b[:, :], -1.0, r_m[:, :], ALU.mult, ALU.subtract))
                link(dve.memset(stack[:, :], 0.0))
                link(dve.tensor_copy(stack[0:MH, :], r_n[:, :]))
                link(dve.tensor_tensor(r_n[:, :], r_n[:, :], stack[0:MH, :], ALU.subtract))
                link(dve.tensor_copy(r_p[:, 0, :], r_n[:, :]))
                link(dve.tensor_copy(stack[32:32 + MH, :], r_p[:, 0, :]))
                link(dve.tensor_tensor(r_n[:, :], r_n[:, :], r_p[:, 0, :], ALU.subtract))
                dve.tensor_copy(stack[64:64 + MH, :], r_n[:, :]).then_inc(stack_ready, 1)
                dve.wait_ge(stack_ready, 1 if first else 2)
            for half in range(2):
                rows_out(st["mem_v"][4 * half:4 * half + 4], lambda i: mem_v[:, i, half * S:(half + 1) * S])
            dve.wait_ge(stored, 16)
            for i, t in enumerate(st["att_z"]):
                silu(att_z[:, i, :], t)

            def masked(n):
                h, ti = units[n]
                W = (ti + 1) * P
                dve.wait_ge(da_logits, n + 1)
                if n >= 2:
                    dve.wait_ge(da_turn, n - 1)
                link(dve.tensor_tensor_reduce(out=probs[:, n % 2, 0:W], in0=bank[4 + n % 2][:, 0:W],
                                              in1=chosen[:, ti, 0:W], scale=1.0, scalar=-3e38, op0=ALU.add,
                                              op1=ALU.max, accum_out=da_cols[:, 0, n:n + 1]))
                dve.tensor_scalar(da_cols[:, 1, n:n + 1], da_cols[:, 0, n:n + 1], -(ADH ** -0.5), None,
                                  ALU.mult).then_inc(da_max, 1)

            def weighed(n):
                h, ti = units[n]
                dve.wait_ge(da_probs, n + 1)
                link(dve.reciprocal(da_cols[:, 3, n:n + 1], da_cols[:, 2, n:n + 1]))
                dve.wait_ge(da_sum, n + 1)
                dve.tensor_scalar(att_o[:, ti, h * ADH:(h + 1) * ADH], bank[7][:, 0:ADH], da_cols[:, 3, n:n + 1],
                                  None, ALU.mult).then_inc(da_out, 1)

            def older_taps(i):
                t = st["mem_qk"][i]
                evs[0] += 1
                dve.wait_ge(ev_ready, evs[0])
                e, b = ev[:, (evs[0] - 1) % 2, :], bank[t["bank"]]
                for back in (1, 2):
                    link(dve.scalar_tensor_tensor(e[:, back:S], b[:, 0:S - back], vec("conv_w", 4 * i + 3 - back),
                                                  e[:, back:S], ALU.mult, ALU.add))
                link(dve.scalar_tensor_tensor(mem_qk[:, i, 3:S], b[:, 0:S - 3], vec("conv_w", 4 * i),
                                              e[:, 3:S], ALU.mult, ALU.add))
                free(dve.tensor_copy(mem_qk[:, i, 0:3], e[:, 0:3]))
                dve.wait_ge(dve_freed, frees[0])
                dve.sem_inc(taps_ready, 1)
                dve.sem_inc(ev_used, 1)

            def conv_silu(i):
                m = mem_qk[:, i, :]
                dve.wait_ge(sg_ready, i + 1)
                dve.tensor_tensor(m, m, sg[:, :], ALU.mult).then_inc(mem_qk_ready, 1)

            masked(0)
            masked(1)
            for n, (h, ti) in enumerate(units):
                if ti == 1 and h:
                    older_taps(h - 1)
                if ti == 3 and h:
                    conv_silu(h - 1)
                if n + 2 < len(units):
                    masked(n + 2)
                if n:
                    weighed(n - 1)
            weighed(len(units) - 1)
            older_taps(AH - 1)
            conv_silu(AH - 1)

            def gated_out(i):
                dve.wait_ge(da_back, i + 1)
                return dve.tensor_tensor(val_m[:, i % 2, :], bank[6 + i % 2][:, :], att_z[:, i, :], ALU.mult)

            split(4, gated_out, lambda i: val_m[:, i % 2, :], lambda i: mixa_hi[:, i, :], lambda i: mixa_lo[:, i, :])

            oz = st["mem_oz"]

            def out_gate(i):
                o = mem_o[:, i, :]
                t = oz[2 * i + 1]
                dve.wait_ge(act_freed, oz[2 * i]["freed"][1])
                evs[0] += 1
                dve.wait_ge(ev_ready, evs[0])
                e = ev[:, (evs[0] - 1) % 2, :]
                link(dve.tensor_tensor(o, o, e, ALU.mult))
                dve.sem_inc(ev_used, 1)
                free(dve.tensor_tensor(o, o, bank[t["bank"]][:, :], ALU.mult))
                dve.wait_ge(dve_freed, frees[0])

            for h in range(MH):
                dve.wait_ge(ml_decay, h + 1)
                for j in range(NT):
                    n = NT * h + j
                    dve.wait_ge(ml_score, n + 1)
                    dve.scalar_tensor_tensor(e_t(h, j), bank[4 + j % 2][:, 0:S - j * P], MQK ** -0.5, e_t(h, j),
                                             ALU.mult, ALU.mult).then_inc(ml_weight, 1)
                out_gate(2 * h)
                dve.wait_ge(ml_floor, 2 * h + 2)
                link(dve.tensor_tensor(den[:, :], den[:, :], floor[:, :], ALU.max))
                link(dve.reciprocal(inv_den[:, :], den[:, :]))
                for v in range(2):
                    dve.wait_ge(ml_values, 2 * h + v + 1)
                    dve.tensor_tensor(h_val[:, v, :], bank[6 + v][:, :], inv_den[:, :], ALU.mult).then_inc(ml_h, 1)
                inverse(inv_m, std_m)
                out_gate(2 * h + 1)

                def gated(i):
                    v = val_m[:, i, :]
                    link(dve.scalar_tensor_tensor(v, h_val[:, i, :], vec("m_norm", 2 * h + i), inv_m[:, :],
                                                  ALU.mult, ALU.mult))
                    return dve.tensor_tensor(v, v, mem_o[:, 2 * h + i, :], ALU.mult)

                split(2, gated, lambda i: val_m[:, i, :], lambda i: mix_hi[:, 2 * h + i, :],
                      lambda i: mix_lo[:, h + MH * i, :])
            for i in range(2):
                low(p_val[:, i, :], p_hi[:, i, :], p_lo[:, i, :])
            dve.wait_ge(x2_in, 16)
            for i, t in enumerate(st["out"]):
                dve.wait_ge(dense_done, t["full"])
                free(dve.tensor_tensor(h_res[:, i, :], bank[t["bank"]][:, :], xt2[:, i, :], ALU.add))
                dve.wait_ge(dve_freed, frees[0])
                dve.sem_inc(h_res_ready, 1)
                low(h_res[:, i, :], h_hi[:, i, :], h_lo[:, i, :])
            for i, t in enumerate(st["gate"]):
                dve.wait_ge(act_freed, t["freed"][1])
                g = gate[:, i % 2, :]
                link(dve.tensor_tensor(ple[:, i, :], ple[:, i, :], g, ALU.mult))
                dve.tensor_tensor(h_res[:, i, :], h_res[:, i, :], ple[:, i, :], ALU.add).then_inc(ple_added, 1)
            dve.wait_ge(sq_used, KD + 2 * MH + 2 * KD)
            link(dve.tensor_scalar(std_f[:, :], bank[4][:, :], EPS, None, ALU.mult))
            dve.tensor_tensor(std_f[:, :], std_f[:, :], bank[5][:, :], ALU.add).then_inc(norm_sums_in, 1)
            n0 = VEC["norm_mix"][0]
            n1 = VEC["norm_final"][0]
            link(dve.tensor_tensor(gain2[:, :], vecs[:, n0:n0 + KD], vecs[:, n1:n1 + KD], ALU.mult))
            inverse(inv_f, std_f)
            split(KD, lambda i: dve.scalar_tensor_tensor(val_f[:, i % 2, :], h_res[:, i, :], gain2[:, i:i + 1],
                                                         inv_f[:, :], ALU.mult, ALU.mult),
                  lambda i: val_f[:, i % 2, :], lambda i: u2_hi[:, i, :], lambda i: u2_lo[:, i, :])
            inverse(inv_g, std_g)
            for i in range(KD):
                dve.scalar_tensor_tensor(h_res[:, i, :], h_res[:, i, :], vec("norm_final", i), inv_g[:, :], ALU.mult,
                                         ALU.mult).then_inc(x2_ready, 1)
            dve.wait_ge(x2_ready, KD)

            def add_taps(acc, b, w, n):
                for back in range(1, n):
                    ins = dve.scalar_tensor_tensor(acc[:, back:S], b[:, 0:S - back], w(n - 1 - back), acc[:, back:S],
                                                   ALU.mult, ALU.add)
                    if back < n - 1:
                        link(ins)
                free(ins)

            def spread_col(i, h0, n):
                return cols[:, i, h0:h0 + n].unsqueeze(2).broadcast_to([P, n, SSD_P])

            dve.wait_ge(dt_log, 1)
            dve.wait_ge(rate_ready, 1)
            link(dve.scalar_tensor_tensor(r_dt[:, :], small2[0:SSD_H, :], 0.0, r_t2[:, :], ALU.max, ALU.add))
            link(dve.tensor_scalar(r_t2[:, :], r_dt[:, :], rate[:, :], -1.0, ALU.mult, ALU.mult))
            for c in range(NT):
                ins = dve.tensor_tensor_scan(r_ac[:, c * P:(c + 1) * P], ones[0:SSD_H, 0:P],
                                             r_t2[:, c * P:(c + 1) * P], 0.0, ALU.mult, ALU.add)
                link(ins)
            dve.sem_inc(acum_ready, 1)
            for c in (1, 2):
                ins = dve.tensor_scalar(ends_diag[:, (c - 1) * SSD_H:c * SSD_H], ident[0:SSD_H, 0:SSD_H],
                                        r_ac[:, (c + 1) * P - 1:(c + 1) * P], None, ALU.mult)
                link(ins)
            dve.sem_inc(stack_a_ready, 1)
            link(dve.tensor_copy(stack_a[0:32, :], r_ac[:, :]))
            link(dve.tensor_tensor(r_n2[:, :], r_ac[:, :], stack_a[0:32, :], ALU.subtract))
            link(dve.tensor_copy(r_p2[:, 0, :], r_n2[:, :]))
            link(dve.tensor_copy(stack_a[32:64, :], r_p2[:, 0, :]))
            link(dve.tensor_tensor(r_n2[:, :], r_n2[:, :], r_p2[:, 0, :], ALU.subtract))
            dve.tensor_copy(stack_a[64:96, :], r_n2[:, :]).then_inc(stack_a_ready, 1)
            dve.wait_ge(stack_a_ready, 2)
            for i in range(len(conv_tiles) + 1):
                if i < len(conv_tiles):
                    t, w, _ = conv_tiles[i]
                    dve.wait_ge(conv_in, i + 1)
                    add_taps(taps[:, i % 2, :], bank[t["bank"]], lambda k: vec("ssd_conv_w", 4 * w + k), 4)
                if i:
                    dve.wait_ge(conv_sg, i)
                    dve.tensor_tensor(conv_tiles[i - 1][2], taps[:, (i - 1) % 2, :], taps_sg[:, (i - 1) % 2, :],
                                      ALU.mult).then_inc(conv_ready, 1)
            dve.wait_ge(conv_ready, len(conv_tiles))
            dve.wait_ge(cols_ready, 3)

            def group_norm(g):
                for i in range(4 * g, 4 * g + 4):
                    dve.scalar_tensor_tensor(y[:, i, :], y[:, i, :], vec("ssd_g", i), inv_y[:, :], ALU.mult,
                                             ALU.mult).then_inc(y_normed, 1)

            for g in range(SSD_G):
                for c in range(NT):
                    n = NT * g + c
                    dve.wait_ge(x_turned, n + 1)
                    x3 = xdt[:, c, :].rearrange("p (h f) -> p h f", f=SSD_P)
                    dve.tensor_tensor(x3, bank[6 + c % 2][:, :].rearrange("p (h f) -> p h f", f=SSD_P),
                                      spread_col(3 * c, 8 * g, 8), ALU.mult).then_inc(xdt_ready, 1)
                    if c < 3:
                        dve.wait_ge(xdt_ready, n + 1)
                        dve.tensor_tensor(xdec[:, c, :].rearrange("p (h f) -> p h f", f=SSD_P), x3,
                                          spread_col(3 * c + 1, 8 * g, 8), ALU.mult).then_inc(xdec_ready, 1)
                for c in range(3):
                    dve.wait_ge(state_dot, 3 * g + c + 1)
                    if c == 0:
                        dve.tensor_copy(states[:, 0, :], bank[6][:, :]).then_inc(state_ready, 1)
                    else:
                        dve.wait_ge(state_ready, 3 * g + c)
                        for e in range(8):
                            f, h = slice(e * SSD_P, (e + 1) * SSD_P), (c - 1) * SSD_H + 8 * g + e
                            ins = dve.scalar_tensor_tensor(states[:, c, f], states[:, c - 1, f],
                                                           chunk_decay[:, h:h + 1], bank[6 + c % 2][:, f], ALU.mult,
                                                           ALU.add)
                        ins.then_inc(state_ready, 1)
                for p in range(4 * g, 4 * g + 4):
                    for h in (2 * p, 2 * p + 1):
                        dve.wait_ge(l_ready, h + 1)
                        dve.wait_ge(grp_copied, 2 * g + 1)
                        dve.tensor_tensor(weight(h), weight(h), scores[:, :], ALU.mult).then_inc(w_ready, 1)
                    yp, e = y[:, p, :], e_ac[:, p % 2, P:S]
                    dve.wait_ge(z_ready, p + 1)
                    free(dve.tensor_tensor(z_sg[:, :], z_sg[:, :], bank[st["z"][p]["bank"]][:, :], ALU.mult))
                    dve.wait_ge(y_dot, 2 * p + 2)
                    link(dve.scalar_tensor_tensor(yp, yp, vec("d_skip", p), bank[6][:, :], ALU.mult, ALU.add))
                    dve.wait_ge(off_dot, p + 1)
                    dve.wait_ge(e_ready, p + 1)
                    dve.tensor_tensor(e, bank[7][:, P:S], e, ALU.mult).then_inc(y_read, 1)
                    dve.wait_ge(y_read, p + 1)
                    link(dve.tensor_tensor(yp[:, P:S], yp[:, P:S], e, ALU.add))
                    dve.wait_ge(dve_freed, frees[0])
                    dve.tensor_tensor(yp, yp, z_sg[:, :], ALU.mult).then_inc(y_ready, 1)
                    if g and p % 4 == 2:
                        if g >= 2:
                            dve.wait_ge(y_normed, 4 * g - 4)
                        inverse(inv_y, std_y)
                    if g and p % 4 == 3:
                        group_norm(g - 1)

            def y_low(first, end):
                dve.wait_ge(y_normed, end)
                for i in range(first, end):
                    low(y[:, i, :], y_hi[:, i, :], y_lo[:, i, :])

            y_low(0, 4)
            dve.wait_ge(y_ready, 16)
            dve.wait_ge(y_normed, 12)
            inverse(inv_y, std_y)
            group_norm(3)
            y_low(4, 16)
            inverse(inv_s, std_s)
            split(2, lambda i: dve.scalar_tensor_tensor(qa_val[:, i, :], qa_val[:, i, :], vec("qa_g", i), inv_s[:, :],
                                                        ALU.mult, ALU.mult),
                  lambda i: qa_val[:, i, :], lambda i: qn_hi[:, i, :], lambda i: qn_lo[:, i, :])
            inverse(inv_s, std_s)
            split(1, lambda i: dve.scalar_tensor_tensor(kva_val[:, :], kva_val[:, :], vec("kva_g"), inv_s[:, :],
                                                        ALU.mult, ALU.mult),
                  lambda i: kva_val[:, :], lambda i: kn_hi[:, :], lambda i: kn_lo[:, :])

            def gain(name, r0, r1):
                return vecs[r0:r1, VEC[name][0]:VEC[name][0] + 1]

            for half in range(2):
                rows_out(st["v"][4 * half:4 * half + 4], lambda i: v_tok[:, i, half * S:(half + 1) * S])
            link(dve.scalar_tensor_tensor(rope[96:P, :], small2[96:P, :], gain("k_g", 96, P), trig[96:P, :], ALU.mult,
                                          ALU.mult))
            link(dve.tensor_copy(q_s[64:96, 1, :], rope[96:P, :]))
            link(dve.scalar_tensor_tensor(rope[64:96, :], small2[64:96, :], gain("k_g", 64, 96), trig[64:96, :],
                                          ALU.mult, ALU.mult))
            link(dve.tensor_tensor(rope[64:96, :], rope[64:96, :], q_s[64:96, 1, :], ALU.add))

            def head_features(h):
                b = bank[st["head_q"][h]["bank"]]
                dve.wait_ge(head_sq, 2 * h + 1)
                dve.tensor_scalar(q_s[0:64, h % 2, :], b[0:64, :], gain("q_g", 0, 64), None, ALU.mult)
                link(dve.scalar_tensor_tensor(rope[96:P, :], b[96:P, :], gain("q_g", 96, P), trig[96:P, :], ALU.mult,
                                              ALU.mult))
                link(dve.scalar_tensor_tensor(b[64:96, :], b[64:96, :], gain("q_g", 64, 96), trig[64:96, :], ALU.mult,
                                              ALU.mult))
                free(dve.tensor_tensor(q_s[64:96, h % 2, :], b[64:96, :], rope[96:P, :], ALU.add))
                dve.wait_ge(head_sq, 2 * h + 2)
                if h:
                    dve.wait_ge(k_ready, h)
                free(dve.tensor_scalar(rope[0:64, :], bank[st["head_k"][h]["bank"]][0:64, :], gain("k_g", 0, 64), None,
                                       ALU.mult))
                dve.wait_ge(dve_freed, frees[0])

            def head_scales(h):
                r = r_qk[:, h % 2, :]
                dve.wait_ge(std_qk_ready, 2 * h + 2)
                dve.reciprocal(r, r).then_inc(r_qk_ready, 1)
                dve.wait_ge(r_qk_ready, h + 1)
                if h:
                    dve.wait_ge(rk_spread, h)
                dve.tensor_tensor(rk_diag[:, :].rearrange("p (c t) -> p c t", c=NT),
                                  ident[:, :].unsqueeze(1).broadcast_to([P, NT, P]),
                                  r[:, NT:2 * NT].unsqueeze(2).broadcast_to([P, NT, P]),
                                  ALU.mult).then_inc(rk_diag_ready, 1)

            def head_keys(h):
                dve.wait_ge(rk_spread, h + 1)
                dve.tensor_tensor(k_s[:, h % 2, :], rope[0:QK, :], bank[2][0:QK, :], ALU.mult).then_inc(k_ready, 1)

            def head_max(n):
                h, ti = heads[n]
                dve.wait_ge(x_logits, n + 1)
                link(dve.reduce_max(x_cols[:, 0, n:n + 1], bank[4 + n % 2][:, 0:(ti + 1) * P], AX_X))
                dve.tensor_scalar(x_cols[:, 1, n:n + 1], x_cols[:, 0, n:n + 1], r_qk[:, h % 2, ti:ti + 1], -1.0,
                                  ALU.mult, ALU.mult).then_inc(x_max, 1)

            def head_out(n):
                h, ti = heads[n]
                dve.wait_ge(x_probs, n + 1)
                link(dve.reciprocal(x_cols[:, 3, n:n + 1], x_cols[:, 2, n:n + 1]))
                dve.wait_ge(x_sum, n + 1)
                dve.tensor_scalar(o_tok[:, ti, h * VD:(h + 1) * VD], bank[7][:, 0:VD], x_cols[:, 3, n:n + 1],
                                  None, ALU.mult).then_inc(x_out, 1)

            head_features(0)
            head_scales(0)
            head_keys(0)
            head_features(1)
            head_max(0)
            head_max(1)
            for n, (h, ti) in enumerate(heads):
                if n + 2 < len(heads):
                    head_max(n + 2)
                if ti == 0 and h + 1 < XH:
                    head_scales(h + 1)
                if ti == 1 and h + 1 < XH:
                    head_keys(h + 1)
                if ti == 3 and h + 2 < XH:
                    head_features(h + 2)
                if ti == 3 and 1 <= h <= KD:
                    dve.wait_ge(act_freed, st["mix_gate"][h - 1]["freed"][1])
                    dve.tensor_tensor(y_ssd[:, h - 1, :], y_ssd[:, h - 1, :], gm[:, h - 1, :],
                                      ALU.mult).then_inc(gates_used, 1)
                if n:
                    head_out(n - 1)
            head_out(len(heads) - 1)
            dve.wait_ge(gates_used, KD)
            for i in range(KD):
                low(bank[6 + i % 2][:, :], o_hi[:, i, :], o_lo[:, i, :])

            def fuse(i):
                t = st["mla_out"][i]
                dve.wait_ge(dense_done, t["full"])
                if i == 0:
                    dve.wait_ge(act_freed, st["mix_gate"][-1]["freed"][1])
                free(dve.tensor_tensor(gm[:, i, :], gm[:, i, :], bank[t["bank"]][:, :], ALU.mult))
                dve.wait_ge(dve_freed, frees[0])
                return dve.tensor_tensor(gm[:, i, :], gm[:, i, :], y_ssd[:, i, :], ALU.add)

            split(KD, fuse, lambda i: gm[:, i, :], lambda i: fused_hi[:, i, :], lambda i: fused_lo[:, i, :])
            for i, t in enumerate(st["mix_out"]):
                dve.wait_ge(dense_done, t["full"])
                free(dve.tensor_tensor(h_res[:, i, :], h_res[:, i, :], bank[t["bank"]][:, :], ALU.add))
            dve.wait_ge(dve_freed, frees[0])
            inverse(inv_x, std_x)
            split(KD, lambda i: dve.scalar_tensor_tensor(val_x[:, i % 2, :], h_res[:, i, :], vec("norm_ffn", i),
                                                         inv_x[:, :], ALU.mult, ALU.mult),
                  lambda i: val_x[:, i % 2, :], lambda i: u3_hi[:, i, :], lambda i: u3_lo[:, i, :])
            for i in range(2 * FT + 1):
                if i < 2 * FT:
                    dve.wait_ge(act_in, i + 1)
                    add_taps((ffn_g, ffn_v)[i % 2][:, i // 2 % 2, :], bank[st["up"][i]["bank"]],
                             lambda k: vec("ffn_conv_w", 3 * i + k), 3)
                if i >= 2 and i % 2 == 0:
                    k = i // 2 - 1
                    g2, v2 = ffn_g[:, k % 2, :], ffn_v[:, k % 2, :]
                    dve.wait_ge(act_sg, k + 1)
                    dve.wait_ge(dve_freed, frees[0] - (1 if i < 2 * FT else 0))
                    link(dve.tensor_tensor(v2, v2, g2, ALU.mult))
                    dve.tensor_tensor(g2, v2, ffn_sg[:, k % 2, :], ALU.mult).then_inc(val_ready, 1)
                    vals[0] += 1
                    dve.wait_ge(val_ready, vals[0])
                    low(g2, act_hi[:, k, :], act_lo[:, k, :])
            for i, t in enumerate(st["down"]):
                dve.wait_ge(dense_done, t["full"])
                free(dve.tensor_tensor(h_res[:, i, :], h_res[:, i, :], bank[t["bank"]][:, :], ALU.add))



def _columns(w, n_k):
    k, n = w.shape
    return w.reshape(n_k, P, n // P, P).transpose(2, 0, 1, 3).reshape(-1, P, P)


def _rows(w, n_k):
    k, n = w.shape
    return w.reshape(n_k, P, n // S, S // P, P).transpose(2, 0, 3, 1, 4).reshape(-1, P, P)


def _chunks(*parts):
    out = []
    for tiles in parts:
        n = -(-len(tiles) // CH) * CH
        t = np.zeros((n, P, P), np.float32)
        t[:len(tiles)] = tiles
        out.append(t)
    t = np.concatenate(out)
    return np.ascontiguousarray(t.reshape(-1, CH, P, P).transpose(0, 2, 1, 3).reshape(-1, P, CH * P))


def _col(v):
    return np.ascontiguousarray(v).reshape(-1, P).T


def _put(rows, *pieces):
    first = pieces[0][1]
    out = np.zeros((P,) + first.shape[1:], np.float32)
    for r, v in pieces:
        out[r:r + len(v)] = v
    return out


def _bucket(dist):
    half = BUCKETS // 2
    large = half + (np.log(np.maximum(dist, 1).astype(np.float32) / np.float32(half))
                    / np.float32(np.log(128 / half)) * np.float32(BUCKETS - half)).astype(np.int32)
    return np.where(dist < half, dist, np.minimum(large, BUCKETS - 1))


def layout(i):
    i = {k: np.asarray(v) for k, v in i.items()}
    bf = mybir.dt.np(BF16)
    a = {}
    w = i["w_in"][0]
    cut = np.cumsum([512, 512, 1024, 1024, 1024, 8, 512, 512, 512, 512, 512, 64, 8])
    mq, mk, mv, mo, mz, mif, aq, ak, av, az, ixq, ixk, ixw = np.split(w, cut[:-1], axis=1)
    small = np.zeros((D, P), np.float32)
    small[:, 0:4], small[:, 32:36], small[:, 64:72] = mif[:, 0:4], mif[:, 4:8], ixw
    oz = np.stack([mo.reshape(D, 8, P), mz.reshape(D, 8, P)], 2).reshape(D, 16 * P)
    parts = [_columns(x, KD) for x in (ixq, np.concatenate([ixk, ixk], 1), small, aq, ak)]
    parts += [_rows(av, KD), _rows(mv, KD), _columns(az, KD), _columns(np.concatenate([mq, mk], 1), KD),
              _columns(oz, KD), _columns(np.concatenate([i["w_out"][0, MH * MV:], i["w_out"][0, :MH * MV]]), 12), _columns(i["w_ple"][0], 2),
              _columns(i["w_ple_gate"][0], KD)]
    w = i["w_in_2"][0]
    cut = np.cumsum([2048, 2048, 512, 512, 32, 256, 128, 32, 2048])
    wz, wx, wb, wc, wdt, wqa, wkva, wkr, wgate = np.split(w, cut[:-1], axis=1)
    small2 = np.zeros((D, P), np.float32)
    small2[:, 0:32], small2[:, 64:96], small2[:, 96:112], small2[:, 112:128] = wdt, wkr, wkr[:, 16:], wkr[:, :16]
    parts += [_columns(x, KD) for x in (small2, wb, wc, wx, wz, wqa, wkva)]
    parts.append(_columns(i["w_ssd_proj_2"][0], 16))
    ukv = i["w_ukv_2"][0].reshape(P, XH, NOPE + VD)
    parts.append(_rows(np.ascontiguousarray(ukv[:, :, NOPE:]).reshape(P, XH * VD), 1))
    uq = i["w_uq_2"][0].reshape(2, P, XH, QK)
    wq = np.concatenate([uq, uq[..., 80:96], uq[..., 64:80]], axis=-1).transpose(2, 0, 1, 3)
    wk = np.concatenate([ukv[:, :, :NOPE], np.zeros_like(ukv[:, :, :NOPE])], axis=2).transpose(1, 0, 2)[:, None]
    wqk = np.concatenate([wq, wk], axis=1)
    gates = _columns(wgate, KD).reshape(XH, KD, P, P)
    parts.append(wqk[0:2].reshape(6, P, P))
    for h in range(XH):
        parts.append(gates[h])
        if h % 2 == 0 and h + 2 < XH:
            parts.append(wqk[h + 2:h + 4].reshape(6, P, P))
    up = i["w_up_2"][0].reshape(D, 2, FT, P).transpose(0, 2, 1, 3).reshape(D, 2 * FT * P)
    parts += [_columns(x, KD) for x in (i["w_mla_proj_2"][0], i["w_o_2"][0], up)]
    parts.append(_columns(i["w_down_2"][0], FT))
    a["weights"] = _chunks(*parts)
    a["x_t"] = np.ascontiguousarray(i["x"][0].T.reshape(KD, P, S).transpose(1, 0, 2))
    a["p_t"] = np.ascontiguousarray(i["p"][0, 0].T.reshape(2, P, S).transpose(1, 0, 2))
    a["rel"] = np.ascontiguousarray(i["rel_bias"])
    e, r = np.eye(P, dtype=np.float32), np.arange(P)
    a["ident"], a["flip"], a["ident_b"] = e, np.ascontiguousarray(e[::-1]), e.astype(bf)
    a["tri"] = np.where(r[None, :] > r[:, None], np.float32(NEG), np.float32(0))
    a["later4_b"] = np.tile(np.where(r[:, None] > r[None, :], np.float32(NEG), np.float32(0)), (1, 4)).astype(bf)
    a["sel_m"] = np.repeat(np.tile(np.eye(32, dtype=np.float32)[:, :MH], (3, 1)), P, axis=1).astype(bf)
    d = S - 1 - np.arange(HANK)
    a["buckets"] = ((_bucket(np.maximum(d, 0))[None] == np.arange(BUCKETS)[:, None]) & (d >= 0)).astype(np.float32)
    v = {n: np.zeros((P, c), np.float32) for n, (_, c) in VEC.items()}
    v["norm_in"], v["m_norm"] = _col(i["norm_in"][0]), _col(i["m_norm"][0])
    v["conv_w"] = i["conv_w"][0].reshape(4, 8, P).transpose(2, 1, 0).reshape(P, 32)
    v["gate_bias"][0:4, 0], v["gate_bias"][32:36, 0] = i["b_gate"][0, 0:4], i["b_gate"][0, 4:8]
    v["gate_scale"][:] = 1
    v["gate_scale"][64:72] = IH ** -0.5
    v["norm_final"], v["eps"][:] = _col(i["norm_final"]), EPS
    v["eps_q"][:], v["eps2"][:] = QK * EPS, EPS * EPS
    v["norm_mix"] = _col(i["norm_mix_g_2"][0])
    v["ssd_conv_w"] = i["conv_ssd_w_2"][0].reshape(4, 24, P).transpose(2, 1, 0).reshape(P, 96)
    v["ssd_conv_b"], v["ssd_g"] = _col(i["conv_ssd_b_2"][0]), _col(i["ssd_norm_g_2"][0])
    v["dt_bias"][0:32, 0], v["a_log"][0:32, 0] = i["dt_bias_2"][0], i["a_log_2"][0]
    v["d_skip"] = _col(np.repeat(i["d_skip_2"][0], SSD_P))
    v["qa_g"], v["kva_g"] = _col(i["q_a_norm_g_2"][0]), _col(i["kv_a_norm_g_2"][0])
    for name in ("q_g", "k_g"):
        g = i[name[0] + "_norm_g_2"][0]
        v[name][:, 0] = np.concatenate([g, g[80:96], g[64:80]])
    v["gate_b"], v["norm_ffn"] = _col(i["gate_b_2"][0]), _col(i["norm_ffn_g_2"][0])
    v["ffn_conv_w"] = i["conv_ffn_w_2"][0].reshape(3, 2, FT, P).transpose(3, 2, 1, 0).reshape(P, 6 * FT)
    v["ffn_conv_b"] = i["conv_ffn_b_2"][0].reshape(2, FT, P).transpose(2, 1, 0).reshape(P, 2 * FT)
    a["one_hot"] = np.tile(np.eye(SSD_H, dtype=np.float32), (3, 1)).astype(bf)
    inv = 1.0 / (np.float32(10000.0) ** (np.arange(0, ROPE, 2, dtype=np.float32) / np.float32(ROPE)))
    ang = np.arange(S, dtype=np.float32)[None, :] * inv.astype(np.float32)[:, None]
    a["trig"] = np.zeros((P, S), np.float32)
    a["trig"][64:] = np.concatenate([np.cos(ang), np.cos(ang), -np.sin(ang), np.sin(ang)])
    a["tri_b"] = a["tri"].astype(bf)
    a["vecs"] = np.ascontiguousarray(np.concatenate([v[n] for n in VEC], axis=1))
    return a


def kernel(**inputs):
    import concourse.bacc as _bacc
    from concourse.bass_utils import run_bass_kernel_spmd as _run

    arrays = layout(inputs)
    nc = _bacc.Bacc("TRN2", target_bir_lowering=False, num_devices=1)
    aps = {name: nc.dram_tensor(name, v.shape, mybir.dt.from_np(v.dtype), kind="ExternalInput").ap()
           for name, v in arrays.items()}
    out = nc.dram_tensor("out", (P, KD, S), F32, kind="ExternalOutput").ap()
    build(nc, aps, out)
    r = _run(nc, [arrays], core_ids=[0])
    return np.ascontiguousarray(r.results[0]["out"].transpose(1, 0, 2).reshape(1, D, S).transpose(0, 2, 1))
```

```python
from contextlib import ExitStack

import numpy as np

import concourse.bass as bass
from concourse import mybir
from concourse.alu_op_type import AluOpType as ALU

F32 = mybir.dt.float32
F32R = mybir.dt.float32r
BF16 = mybir.dt.bfloat16
ACT = mybir.ActivationFunctionType
AX_X = mybir.AxisListType.X

P = 128
S = 512
NT = S // P
D = 1024
KD = D // P
EPS = 1e-6
NEG = -1e30

MH, MQK, MV = 4, 128, 256
AH, ADH = 8, 64
IH, IDH = 8, 64
TOPK = S // 4
BUCKETS = 32
HANK = S + P
SSD_H, SSD_P, SSD_G = 32, 64, 4
XH, QK, NOPE, ROPE, VD = 16, 96, 64, 32, 64
D_FF = 2816
FT = D_FF // P

CH = 8
RING = 4

VEC = {}
_n = 0
for _name, _w in (("norm_in", KD), ("conv_w", 8 * 4), ("m_norm", KD), ("gate_bias", 1), ("gate_scale", 1),
                  ("norm_final", KD), ("norm_mix", KD), ("ssd_conv_w", 24 * 4), ("ssd_conv_b", 24),
                  ("dt_bias", 1), ("a_log", 1), ("d_skip", 16), ("ssd_g", 16), ("qa_g", 2), ("kva_g", 1),
                  ("q_g", 1), ("k_g", 1), ("gate_b", 16), ("norm_ffn", KD), ("ffn_conv_w", 2 * FT * 3),
                  ("ffn_conv_b", 2 * FT), ("eps", 1), ("eps_q", 1), ("eps2", 1)):
    VEC[_name] = (_n, _w)
    _n += _w
NVEC = _n


class Plan:

    def __init__(self):
        self.chunks = self.events = self.turn = 0
        self.banks, self.last = [0, 1, 2, 3], {}
        self.stage, self.used_at, self.count = {}, {}, {"A": 0, "D": 0}
        self.upto = -1

    def use_banks(self, *banks):
        self.banks, self.turn = list(banks), 0

    def chunk(self):
        self.chunks += 1
        return self.chunks - 1

    def event(self, c=None):
        self.events += 1
        if c is not None:
            self.used_at[c] = self.events
            while self.upto + 1 in self.used_at:
                self.upto += 1

    def open(self, name, parts, ends):
        bank = self.banks[self.turn % len(self.banks)]
        self.turn += 1
        t = dict(parts=parts, ends=ends, bank=bank, before=self.last.get(bank))
        self.stage.setdefault(name, []).append(t)
        return t

    def close(self, t, reader):
        t.update(full=self.events, upto=self.upto)
        self.count[reader] += 1
        t["freed"] = self.last[t["bank"]] = (reader, self.count[reader])

    def tile(self, name, parts, reader, last=None):
        t = self.open(name, parts, [])
        self.fill(t, reader, last)

    def fill(self, t, reader, last=None):
        parts, ends = t["parts"], t["ends"]
        for i, (c, s) in enumerate(parts):
            done = c in last if last is not None else s == CH - 1
            if i == len(parts) - 1 or (parts[i + 1][0] != c and done):
                self.event(c if done else None)
                ends.append(i)
        self.close(t, reader)

    def columns(self, name, n, kt, readers):
        c0 = self.chunks
        self.chunks += -(-n * kt // CH)
        for t in range(n):
            parts = [(c0 + f // CH, f % CH) for f in range(t * kt, (t + 1) * kt)]
            last = {c for c, s in parts if s == CH - 1 or (c, s) == (c0 + (n * kt - 1) // CH, (n * kt - 1) % CH)}
            self.tile(name, parts, readers[t % len(readers)], last)

    def rows(self, name, kt, readers, *banks):
        halves = len(banks)
        per = CH * P // S
        flat = [(self.chunks + f // per, f % per) for f in range(halves * kt)]
        self.chunks = flat[-1][0] + 1
        for h in range(halves):
            self.use_banks(*banks[h])
            parts = flat[h * kt:(h + 1) * kt]
            ends = [i for i, (c, s) in enumerate(parts) if s == per - 1 or i == kt - 1]
            for i in ends:
                c, s = parts[i]
                self.event(c if s == per - 1 or (h, i) == (halves - 1, kt - 1) else None)
            for t in range(NT):
                self.close(self.open(name, parts, ends), readers[t % len(readers)])


def make_plan():
    plan = Plan()
    for name, n, kt, reader in (("idx_q", 4, KD, "A"), ("idx_k", 1, KD, "A"), ("small", 1, KD, "A"),
                                ("att_q", 4, KD, "A"), ("att_k", 4, KD, "A")):
        plan.columns(name, n, kt, reader)
    low_banks, high_banks = (0, 1, 2, 3), (4, 5, 6, 7)
    plan.rows("att_v", KD, "AD", high_banks)
    plan.rows("mem_v", KD, "AD", low_banks, high_banks)
    plan.use_banks(*low_banks)
    for name, n, kt, reader in (("att_z", 4, KD, "D"), ("mem_qk", 8, KD, "D"), ("mem_oz", 16, KD, "AD"),
                                ("out", 8, 12, "D"), ("ple", 8, 2, "A"), ("gate", 8, KD, "A"),
                                ("small2", 1, KD, "A"), ("ssd_b", 4, KD, "D"), ("ssd_c", 4, KD, "D"),
                                ("ssd_x", 16, KD, "D")):
        plan.columns(name, n, kt, reader)
    plan.use_banks(1, 0)
    for name, n, reader in (("z", 16, "D"), ("qa", 2, "A"), ("kva", 1, "A")):
        plan.columns(name, n, KD, reader)
    plan.use_banks(0, 1, 2, 3)
    plan.columns("ssd_out", 8, 16, "A")
    plan.use_banks(1, 2)
    pairs = {}

    def project(h):
        if h % 2 == 0:
            pairs[h // 2] = plan.chunk()
        c, s = pairs[h // 2], 3 * (h % 2)
        plan.tile("head_q", [(c, s), (c, s + 1)], "D", ())
        plan.tile("head_k", [(c, s + 2)], "D", (c,) if h % 2 else ())

    project(0)
    plan.rows("v", 1, "AD", high_banks, high_banks)
    for h in range(XH):
        plan.use_banks(3 * (h % 2))
        c = plan.chunk()
        t = plan.open("mix_gate", [(c, s) for s in range(KD)], [])
        plan.use_banks(1, 2)
        if h == 0:
            project(1)
            plan.fill(t, "A")
        if h + 2 < XH:
            project(h + 2)
        if h:
            plan.fill(t, "A")
    plan.use_banks(0, 1, 2, 3)
    for name, n, kt in (("mla_out", 8, KD), ("mix_out", 8, KD), ("up", 2 * FT, KD), ("down", 8, FT)):
        plan.columns(name, n, kt, "D")
    return plan


def build(nc, a, out):
    plan = make_plan()
    st = plan.stage
    N_CHUNK = plan.chunks
    ctx = ExitStack()
    with ctx:
        base = (nc.sbuf_base + 63) // 64 * 64

        def at(name, kb, shape, dt=F32):
            return nc.alloc_sbuf_tensor_at(name, shape, dt, offset=base + int(kb * 1024))

        def sem(name):
            return ctx.enter_context(nc.semaphore(name))

        bank = [ctx.enter_context(nc.psum_tensor(f"bank{i}", [P, 512], F32)) for i in range(8)]

        w_raw = at("w_raw", 0, [P, RING, CH * P])
        w_hi = at("w_hi", 16, [P, RING, CH * P], F32R)
        w_lo = at("w_lo", 32, [P, RING, CH * P], F32R)
        ones = at("ones", 48, [P, 512])
        squares_f = at("squares_f", 50, [P, 2 * P])
        ident, tri = squares_f[:, 0:P], squares_f[:, P:2 * P]
        squares_b = at("squares_b", 51.5, [P, 5 * P], BF16)
        ident_b, later4_b = squares_b[:, 0:P], squares_b[:, P:5 * P]
        vecs = at("vecs", 52.75, [P, NVEC])
        sel_m = at("sel_m", 54.5, [96, MH * P], BF16)
        u_hi = at("u_hi", 56, [P, KD, S], F32R)
        u_lo = at("u_lo", 72, [P, KD, S], F32R)
        iq = at("iq", 88, [P, 4, S])
        ik = at("ik", 96, [P, S])
        relu = at("relu", 98, [P, 2, S])
        score = at("score", 102, [P, 3, S])
        work = at("work", 108, [P, 2, S])
        work2 = at("work2", 200, [P, S])
        small = at("small", 202, [P, S])
        top8 = at("top8", 204, [P, 3, 8])
        tk = at("tk", 204.25, [P, 3, 4])
        iw = at("iw", 204.5, [P, 3, IH])
        acol = at("acol", 205, [P, NT * MH])
        da_cols = at("da_cols", 205.5, [P, 4, AH * NT])
        chosen = at("chosen", 112, [P, NT, S])
        xt = at("xt", 120, [P, KD, S])
        sq = at("sq", 136, [P, 2, S])
        u_diag = at("u_diag", 140, [P, S])
        u_val = at("u_val", 144, [P, 2, S])
        mem_qk = at("mem_qk", 120, [P, 8, S])
        mem_v = at("mem_v", 136, [P, NT, MH * MV])
        mem_o = at("mem_o", 152, [P, 8, S])
        att_q = at("att_q", 168, [P, 4, S])
        att_k = at("att_k", 176, [P, 4, S])
        att_v = at("att_v", 184, [P, NT, AH * ADH])
        att_z = at("att_z", 192, [P, 4, S])
        ev = at("ev", 108, [P, 2, S])
        sg = at("sg", 200, [P, S])
        bias_row = at("bias_row", 192, [AH, HANK])
        by_bucket = at("by_bucket", 194.5, [BUCKETS, AH + HANK])
        rel, buckets = by_bucket[:, 0:AH], by_bucket[:, AH:AH + HANK]
        r_f = at("r_f", 152, [MH, S])
        r_t = at("r_t", 154, [MH, S])
        r_lf = at("r_lf", 156, [MH, S])
        r_b = at("r_b", 158, [MH, S])
        r_a = at("r_a", 160, [MH, S])
        r_m = at("r_m", 162, [MH, S])
        r_n = at("r_n", 164, [MH, S])
        r_p = at("r_p", 166, [MH, 2, S], BF16)
        stack_m = at("stack_m", 206, [96, S], BF16)
        stack_f = at("stack_f", 204, [96, S], BF16)
        decay = at("decay", 176, [P, 2, 1280])
        h_val = at("h_val", 186, [P, 2, S])
        floor = at("floor", 190, [P, S])
        den = at("den", 88, [P, S])
        inv_den = at("inv_den", 90, [P, S])
        sq_m = at("sq_m", 96, [P, 2, S])
        std_m = at("std_m", 92, [P, S])
        inv_m = at("inv_m", 94, [P, S])
        val_m = at("val_m", 112, [P, 2, S])
        mix_hi = at("mix_hi", 152, [P, 8, S], F32R)
        mix_lo = at("mix_lo", 120, [P, 8, S], F32R)
        hank = at("hank", 88, [P, 2, S])
        biased = at("biased", 92, [P, 2, S])
        probs = at("probs", 152, [P, 3, S])
        turned = at("turned", 96, [P, 2, S])
        att_o = at("att_o", 100, [P, NT, S])
        mixa_hi = at("mixa_hi", 192, [P, 4, S], F32R)
        mixa_lo = at("mixa_lo", 168, [P, 4, S], F32R)
        xt2 = at("xt2", 72, [P, KD, S])
        h_res = at("h_res", 56, [P, KD, S])
        h_hi = at("h_hi", 72, [P, KD, S], F32R)
        h_lo = at("h_lo", 88, [P, KD, S], F32R)
        p_val = at("p_val", 136, [P, 2, S])
        p_hi = at("p_hi", 140, [P, 2, S], F32R)
        p_lo = at("p_lo", 144, [P, 2, S], F32R)
        ple = at("ple", 168, [P, KD, S])
        gate = at("gate", 184, [P, 2, S])
        sq_f = at("sq_f", 136, [P, 4, S])
        x2_diag = at("x2_diag", 192, [P, 2, S])
        norm_col = at("norm_col", 207.5, [P, 3, NT])
        gain2 = at("gain2", 206.75, [P, KD])
        val_f = at("val_f", 196, [P, 2, S])
        u2_hi = at("u2_hi", 72, [P, KD, S], F32R)
        u2_lo = at("u2_lo", 88, [P, KD, S], F32R)
        bias_dram = nc.dram_tensor("bias_dram", (AH, P, HANK), F32).ap()

        def vec(name, i=0):
            return vecs[:, VEC[name][0] + i:VEC[name][0] + i + 1]

        def e_t(h, j):
            o = sum(S - i * P for i in range(j))
            return decay[:, h % 2, o:o + S - j * P]

        units = [(h, ti) for h in range(AH) for ti in range(NT)]
        n_lo = {}
        for name, n in (("u", KD), ("mixa", 4), ("mix", 8), ("p", 2), ("h", KD), ("u2", KD)):
            n_lo[name] = n + (max(n_lo.values()) if n_lo else 0)

        w_landed = [sem(f"w_landed{i}") for i in range(RING)]
        w_hi_ready = sem("w_hi_ready")
        w_lo_ready = sem("w_lo_ready")
        dense_done = sem("dense_done")
        act_freed = sem("act_freed")
        dve_freed = sem("dve_freed")
        freed = {"A": act_freed, "D": dve_freed}
        vecs_in = sem("vecs_in")
        squares_in = sem("squares_in")
        consts_in = sem("consts_in")
        x_in = [sem(f"x_in{i}") for i in range(KD)]
        sq_ready = sem("sq_ready")
        sq_used = sem("sq_used")
        std_ready = sem("std_ready")
        inv_ready = sem("inv_ready")
        val_ready = sem("val_ready")
        hi_ready = sem("hi_ready")
        lo_ready = sem("lo_ready")
        dve_step = sem("dve_step")
        act_step = sem("act_step")
        ones_ready = sem("ones_ready")
        iw_turned = sem("iw_turned")
        iw_ready = sem("iw_ready")
        idx_dot = sem("idx_dot")
        idx_relu = sem("idx_relu")
        idx_added = sem("idx_added")
        top_found = sem("top_found")
        top_gone = sem("top_gone")
        chosen_ready = sem("chosen_ready")
        ev_ready = sem("ev_ready")
        ev_used = sem("ev_used")
        taps_ready = sem("taps_ready")
        sg_ready = sem("sg_ready")
        mem_qk_ready = sem("mem_qk_ready")
        ml_f = sem("ml_f")
        ml_log = sem("ml_log")
        rows_ready = sem("rows_ready")
        stack_ready = sem("stack_ready")
        acol_turned = sem("acol_turned")
        acol_ready = sem("acol_ready")
        ml_spread = sem("ml_spread")
        ml_decay = sem("ml_decay")
        ml_score = sem("ml_score")
        ml_weight = sem("ml_weight")
        ml_sums = sem("ml_sums")
        ml_values = sem("ml_values")
        ml_floor = sem("ml_floor")
        ml_h = sem("ml_h")
        bias_dot = sem("bias_dot")
        bias_ready = sem("bias_ready")
        bias_out = sem("bias_out")
        hank_in = [sem("hank_in0"), sem("hank_in1")]
        da_logits = sem("da_logits")
        da_bias = sem("da_bias")
        da_max = sem("da_max")
        da_probs = sem("da_probs")
        da_turn = sem("da_turn")
        da_turned = sem("da_turned")
        da_sum = sem("da_sum")
        da_out = sem("da_out")
        da_back = sem("da_back")
        x2_in = sem("x2_in")
        p_in = sem("p_in")
        h_res_ready = sem("h_res_ready")
        ple_added = sem("ple_added")
        x2_ready = sem("x2_ready")
        v_tok_ready = sem("v_tok_ready")
        norm_sums_in = sem("norm_sums_in")
        norm_std = sem("norm_std")
        norm_diag = sem("norm_diag")
        norm_spread = sem("norm_spread")
        stored = sem("stored")
        tri_b = at("tri_b", 55.5, [P, P], BF16)
        y = at("y", 104, [P, 16, S])
        y_lo = at("y_lo", 104, [P, 16, S], F32R)
        one_hot = at("one_hot", 206.5, [96, SSD_H], BF16)
        trig = at("trig", 148, [P, S])
        b_t = at("b_t", 150, [P, SSD_G, S])
        c_t = at("c_t", 158, [P, SSD_G, S])
        small2 = at("small2", 166, [P, S])
        stack_a = at("stack_a", 168, [96, S], BF16)
        cols = at("cols", 169, [P, 3 * NT, SSD_H])
        rate = at("rate", 170.5, [SSD_H, 1])
        chunk_decay = at("chunk_decay", 171, [P, 2 * SSD_H])
        ends_diag = at("ends_diag", 171.75, [SSD_H, 2 * SSD_H])
        r_dt = at("r_dt", 172.5, [SSD_H, S])
        r_ac = at("r_ac", 174.5, [SSD_H, S])
        r_dte = at("r_dte", 176.5, [SSD_H, S])
        r_t2 = at("r_t2", 178.5, [SSD_H, S])
        r_p2 = at("r_p2", 188.5, [SSD_H, 2, S], BF16)
        r_n2 = at("r_n2", 190.5, [SSD_H, S])
        taps = at("taps", 180.5, [P, 2, S])
        taps_sg = at("taps_sg", 184.5, [P, 2, S])
        states = at("states", 172.5, [P, 3, S])
        scores = at("scores", 178.5, [P, S])
        xdt = at("xdt", 180.5, [P, NT, S])
        xdec = at("xdec", 188.5, [P, 3, S])
        b_tok = at("b_tok", 194.5, [P, 3 * P])
        weights2 = [at("weight_a", 196.5, [P, 2, S]), at("weight_b", 144, [P, 2, S])]
        e_ac = at("e_ac", 200.5, [P, 2, S])
        sq_y = at("sq_y", 136, [P, 2, S])
        std_y = at("std_y", 140, [P, S])
        inv_y = at("inv_y", 142, [P, S])
        z_sg = at("z_sg", 204.5, [P, S])
        y_hi = at("y_hi", 170, [P, 16, S], F32R)
        qa_val = at("qa_val", 202, [P, 2, S])
        kva_val = at("kva_val", 168, [P, S])
        qn_hi = at("qn_hi", 136, [P, 2, S], F32R)
        qn_lo = at("qn_lo", 140, [P, 2, S], F32R)
        kn_hi = at("kn_hi", 144, [P, S], F32R)
        kn_lo = at("kn_lo", 146, [P, S], F32R)
        sq_s = at("sq_s", 158, [P, 2, S])
        std_s = at("std_s", 162, [P, S])
        inv_s = at("inv_s", 164, [P, S])
        y_ssd = at("y_ssd", 150, [P, KD, S])
        v_tok = at("v_tok", 104, [P, NT, XH * VD])
        o_tok = at("o_tok", 120, [P, NT, XH * VD])
        turned_x = [at("turned_x0", 166, [P, S]), at("turned_x1", 168, [P, S])]
        gm = at("gm", 170, [P, KD, S])
        q_s = at("q_s", 186, [QK, 2, S])
        k_s = at("k_s", 190, [QK, 2, S])
        sq_q = at("sq_q", 194, [QK, S])
        sq_k = at("sq_k", 196, [QK, S])
        rope = at("rope", 202, [P, S])
        rk_diag = at("rk_diag", 204, [P, S])
        probs_x = at("probs_x", 198, [P, 2, S])
        x_cols = at("x_cols", 206, [P, 4, XH * NT])
        r_qk = at("r_qk", 207, [P, 2, 2 * NT])
        o_hi = at("o_hi", 186, [P, KD, S], F32R)
        o_lo = at("o_lo", 104, [P, KD, S], F32R)
        fused_hi = at("fused_hi", 72, [P, KD, S], F32R)
        fused_lo = at("fused_lo", 88, [P, KD, S], F32R)
        sq_x = at("sq_x", 150, [P, 2, S])
        x3_diag = at("x3_diag", 154, [P, S])
        val_x = at("val_x", 158, [P, 2, S])
        u3_hi = at("u3_hi", 72, [P, KD, S], F32R)
        u3_lo = at("u3_lo", 88, [P, KD, S], F32R)
        act_hi = at("act_hi", 104, [P, FT, S], F32R)
        act_lo = at("act_lo", 148, [P, FT, S], F32R)
        ffn_g = at("ffn_g", 192, [P, 2, S])
        ffn_v = at("ffn_v", 196, [P, 2, S])
        ffn_sg = at("ffn_sg", 200, [P, 2, S])

        for name, n in (("y", 16), ("qn", 2), ("kn", 1), ("o", 8), ("fused", 8), ("u3", 8), ("act", FT)):
            n_lo[name] = n + max(n_lo.values())
        n_inv = MH
        conv_tiles = ([(t, 16 + i, b_t[:, i, :]) for i, t in enumerate(st["ssd_b"])]
                      + [(t, 20 + i, c_t[:, i, :]) for i, t in enumerate(st["ssd_c"])]
                      + [(t, i, y[:, i, :]) for i, t in enumerate(st["ssd_x"])])

        def weight(h):
            return weights2[h // 2 % 2][:, h % 2, :]

        heads = [(h, ti) for h in range(XH) for ti in range(NT)]
        up = st["up"]
        assert len(up) % 4 == 0 and all(t["bank"] == i % 4 for i, t in enumerate(up))
        UP_LOOPS, up_chunk = len(up) // 4, up[0]["parts"][0][0]
        up_done, up_freed = up[0]["full"], up[0]["freed"][1]

        def up_vec(name, i):
            return vecs[:, bass.ds(VEC[name][0] + i, 1)]

        consts2_in = sem("consts2_in")
        conv_in = sem("conv_in")
        conv_sg = sem("conv_sg")
        conv_ready = sem("conv_ready")
        dt_log = sem("dt_log")
        rate_ready = sem("rate_ready")
        acum_ready = sem("acum_ready")
        stack_a_ready = sem("stack_a_ready")
        dte_ready = sem("dte_ready")
        cols_turned = sem("cols_turned")
        ends_spread = sem("ends_spread")
        cols_ready = sem("cols_ready")
        grp_dot = sem("grp_dot")
        grp_copied = sem("grp_copied")
        x_turned = sem("x_turned")
        xdt_ready = sem("xdt_ready")
        xdec_ready = sem("xdec_ready")
        state_dot = sem("state_dot")
        state_ready = sem("state_ready")
        a_spread = sem("a_spread")
        l_ready = sem("l_ready")
        w_ready = sem("w_ready")
        e_spread = sem("e_spread")
        e_ready = sem("e_ready")
        z_ready = sem("z_ready")
        y_dot = sem("y_dot")
        off_dot = sem("off_dot")
        y_read = sem("y_read")
        y_ready = sem("y_ready")
        pool_step = sem("pool_step")
        sum_ready = sem("sum_ready")
        sum_used = sem("sum_used")
        y_normed = sem("y_normed")
        krope_ready = sem("krope_ready")
        krope_sq = sem("krope_sq")
        head_sq = sem("head_sq")
        head_sums = sem("head_sums")
        k_ready = sem("k_ready")
        std_qk_ready = sem("std_qk_ready")
        r_qk_ready = sem("r_qk_ready")
        rk_diag_ready = sem("rk_diag_ready")
        rk_spread = sem("rk_spread")
        x_logits = sem("x_logits")
        x_max = sem("x_max")
        x_probs = sem("x_probs")
        x_turn = sem("x_turn")
        x_turned_out = sem("x_turned_out")
        x_sum = sem("x_sum")
        x_out = sem("x_out")
        gates_used = sem("gates_used")
        o_back = sem("o_back")
        act_in = sem("act_in")
        act_sg = sem("act_sg")
        block = ctx.enter_context(nc.Block())

        @block.sync
        def _(sp):
            for i in range(KD):
                sp.dma_start(xt[:, i, :], a["x_t"][:, i, :]).then_inc(x_in[i], 16)
                if i == KD // 2:
                    sp.dma_start(w_raw[:, 0, :], a["weights"][0]).then_inc(w_landed[0], 16)
            for dst, name in ((by_bucket, "by_bucket"), (squares_b, "squares_b"), (sel_m, "sel_m")):
                sp.dma_start(dst[:, :], a[name]).then_inc(consts_in, 16)
            for j in range(1, RING):
                sp.dma_start(w_raw[:, j, :], a["weights"][j]).then_inc(w_landed[j], 16)
            with sp.Fori(1, N_CHUNK // RING) as g:
                for j in range(RING):
                    sp.wait_ge(w_lo_ready, RING * g + (j + 1 - RING))
                    sp.dma_start(w_raw[:, j, :],
                                 a["weights"][bass.ds(RING * g + j, 1)].rearrange("a p n -> (a p) n")
                                 ).then_inc(w_landed[j], 16)
            for c in range(N_CHUNK // RING * RING, N_CHUNK):
                sp.wait_ge(w_lo_ready, c + 1 - RING)
                sp.dma_start(w_raw[:, c % RING, :], a["weights"][c]).then_inc(w_landed[c % RING], 16)
            for i, t in enumerate(st["down"]):
                sp.wait_ge(dve_freed, t["freed"][1])
                sp.dma_start(out[:, i, :], h_res[:, i, :]).then_inc(stored, 16)
            sp.wait_ge(stored, 16 * (1 + KD))

        @block.gpsimd
        def _(pool):
            def low_part(c, j):
                pool.wait_ge(w_hi_ready, c + 1)
                pool.tensor_tensor(w_lo[:, j, :], w_raw[:, j, :], w_hi[:, j, :].bitcast(F32),
                                   ALU.subtract).then_inc(w_lo_ready, 1)

            def low_parts(first, end):
                start = -(-first // RING) * RING
                for c in range(first, min(start, end)):
                    low_part(c, c % RING)
                if start < end:
                    with pool.Fori(start // RING, end // RING) as g:
                        for j in range(RING):
                            low_part(RING * g + j, j)
                    for c in range(end // RING * RING, end):
                        low_part(c, c % RING)

            n_step = [0]

            def group_squares(g):
                pool.wait_ge(y_ready, 4 * g + 4)
                if g:
                    pool.wait_ge(sum_used, g)
                acc, square = sq_y[:, 0, :], sq_y[:, 1, :]
                for i in range(4):
                    t = y[:, 4 * g + i, :]
                    pool.tensor_tensor(square if i else acc, t, t, ALU.mult).then_inc(pool_step, 1)
                    n_step[0] += 1
                    pool.wait_ge(pool_step, n_step[0])
                    if i:
                        ins = pool.tensor_tensor(acc, acc, square, ALU.add)
                        ins.then_inc(sum_ready if i == 3 else pool_step, 1)
                    if i in (1, 2):
                        n_step[0] += 1
                        pool.wait_ge(pool_step, n_step[0])

            done, z_chunk = 0, st["z"][0]["parts"][0][0]
            for g in range(SSD_G):
                c = z_chunk + 4 * g + 3 + RING
                low_parts(done, c)
                group_squares(g)
                done = c
            low_parts(done, N_CHUNK)

        @block.tensor
        def _(pe):
            n_sq = [0]

            def rms(n, sq, b=4):
                for i in range(n):
                    square_sum(i, n, sq, b)

            def square_sum(i, n, sq, b=4):
                pe.wait_ge(sq_ready, n_sq[0] + 1)
                pe.matmul(bank[b][:, :], ones[:, 0:P], sq[:, i % 2, :], start=(i == 0),
                          stop=(i == n - 1)).then_inc(sq_used, 1)
                n_sq[0] += 1

            n_spread = [0]

            def token_sums(i, n, sq, k=0, of=1):
                pe.wait_ge(sq_ready, n_sq[0] + 1)
                for c in range(NT):
                    mm = pe.matmul(bank[4][:, NT * k + c:NT * k + c + 1], sq[:, c * P:(c + 1) * P], ones[:, 0:1],
                                   start=(i == 0 and k + c == 0), stop=(i == n - 1 and k + c == of + NT - 2))
                mm.then_inc(sq_used, 1)
                n_sq[0] += 1

            def spread_scale(diag, b):
                n_spread[0] += 1
                pe.wait_ge(norm_diag, n_spread[0])
                pe.matmul(bank[b][:, :], ones[:, 0:P], diag, start=True, stop=True).then_inc(norm_spread, 1)

            def open_bank(t):
                if t["before"]:
                    e, n = t["before"]
                    pe.wait_ge(freed[e], n)

            def column_tile(t, rhs, ready=None, part=None):
                n = len(t["parts"])
                first, end = part or (0, n)
                if first == 0:
                    open_bank(t)
                o = bank[t["bank"]][:, :]
                for i in range(first, end):
                    c, s = t["parts"][i]
                    if i == first or t["parts"][i - 1][0] != c:
                        pe.wait_ge(w_lo_ready, c + 1)
                    if ready is not None:
                        pe.wait_ge(lo_ready, ready + i + 1)
                    hi, lo = (w[:, c % RING, s * P:(s + 1) * P] for w in (w_hi, w_lo))
                    xh, xl = rhs(i)
                    pe.matmul(o, hi, xh, start=(i == 0), stop=False)
                    pe.matmul(o, hi, xl, start=False, stop=False)
                    mm = pe.matmul(o, lo, xh, start=False, stop=(i == n - 1))
                    if i in t["ends"]:
                        mm.then_inc(dense_done, 1)

            def column_pair(tiles, rhs, ready):
                n = len(tiles[0]["parts"])
                for t in tiles:
                    assert t["ends"] == [n - 1]
                    open_bank(t)
                for i in range(n):
                    pe.wait_ge(lo_ready, ready + i + 1)
                    xh, xl = rhs(i)
                    for t in tiles:
                        c, s = t["parts"][i]
                        if i == 0:
                            pe.wait_ge(w_lo_ready, c + 1)
                        hi, lo = (w[:, c % RING, s * P:(s + 1) * P] for w in (w_hi, w_lo))
                        o = bank[t["bank"]][:, :]
                        pe.matmul(o, hi, xh, start=(i == 0), stop=False)
                        pe.matmul(o, hi, xl, start=False, stop=False)
                        mm = pe.matmul(o, lo, xh, start=False, stop=(i == n - 1))
                        if i == n - 1:
                            mm.then_inc(dense_done, 1)

            def column_tiles(tiles, rhs, ready, pair=False):
                if pair:
                    column_pair(tiles[0:2], rhs, ready)
                else:
                    column_tile(tiles[0], rhs, ready)
                for t in tiles[1 + pair:]:
                    column_tile(t, rhs)

            def row_tiles(tiles, lhs):
                for t in tiles:
                    open_bank(t)
                parts, ends = tiles[0]["parts"], tiles[0]["ends"]
                for k, (c, s) in enumerate(parts):
                    pe.wait_ge(w_lo_ready, c + 1)
                    hi, lo = (w[:, c % RING, s * S:(s + 1) * S] for w in (w_hi, w_lo))
                    for t in range(NT):
                        xh, xl = (x[:, t * P:(t + 1) * P] for x in lhs(k))
                        o = bank[tiles[t]["bank"]][:, :]
                        pe.matmul(o, xh, hi, start=(k == 0), stop=False)
                        pe.matmul(o, xl, hi, start=False, stop=False)
                        mm = pe.matmul(o, xh, lo, start=False, stop=(k == len(parts) - 1))
                    if k in ends:
                        mm.then_inc(dense_done, 1)

            def of_u(k):
                return u_hi[:, k, :], u_lo[:, k, :]

            pe.wait_ge(ones_ready, 1)
            for i in range(KD):
                token_sums(i, KD, sq[:, i % 2, :])
            spread_scale(u_diag[:, :], 5)
            pe.wait_ge(consts_in, 16 * 3)
            w = HANK // 2
            for j in range(2):
                mm = pe.matmul(bank[6 + j][0:AH, 0:w], rel[:, :], buckets[:, j * w:(j + 1) * w], start=True, stop=True)
            mm.then_inc(bias_dot, 1)
            column_tiles(st["idx_q"] + st["idx_k"] + st["small"], of_u, 0, pair=True)
            column_tile(st["att_q"][0], of_u)
            pe.wait_ge(act_freed, st["small"][0]["freed"][1])
            pe.wait_ge(bias_ready, 1)
            for ti in range(1, NT):
                mm = pe.transpose(bank[5][:, (ti - 1) * IH:ti * IH], small[64:64 + IH, ti * P:(ti + 1) * P],
                                  ident[64:64 + IH, 64:64 + IH])
            mm.then_inc(iw_turned, 1)
            n = 0
            for ti in range(1, NT):
                for h in range(IH):
                    if n >= 2:
                        pe.wait_ge(idx_relu, n - 1)
                    r = slice(64 * (h % 2), 64 * (h % 2) + 64)
                    W = (ti + 1) * P
                    pe.matmul(bank[6 + n % 2][:, 0:W], iq[r, h // 2, ti * P:W], ik[r, 0:W],
                              start=True, stop=True).then_inc(idx_dot, 1)
                    n += 1
            for t in st["att_q"][1:] + st["att_k"]:
                column_tile(t, of_u)
            pe.wait_ge(idx_relu, n)
            row_tiles(st["att_v"], of_u)
            row_tiles(st["mem_v"][0:4], of_u)
            row_tiles(st["mem_v"][4:8], of_u)
            column_tile(st["att_z"][0], of_u)
            pe.wait_ge(act_freed, st["mem_v"][6]["freed"][1])
            pe.wait_ge(dve_freed, st["mem_v"][7]["freed"][1])
            pe.wait_ge(rows_ready, 1)
            for ti in range(NT):
                mm = pe.transpose(bank[5][:, ti * MH:(ti + 1) * MH], r_a[:, ti * P:(ti + 1) * P], ident[0:MH, 0:MH])
            mm.then_inc(acol_turned, 1)
            for t in st["att_z"][1:]:
                column_tile(t, of_u)

            def logits(n):
                h, ti = units[n]
                W = (ti + 1) * P
                r = slice(64 * (h % 2), 64 * (h % 2) + 64)
                if n >= 2:
                    pe.wait_ge(da_max, n - 1)
                pe.matmul(bank[4 + n % 2][:, 0:W], att_q[r, h // 2, ti * P:W], att_k[r, h // 2, 0:W], start=True,
                          stop=True).then_inc(da_logits, 1)

            def turn(n):
                h, ti = units[n]
                pe.wait_ge(da_probs, n + 1)
                if n:
                    pe.wait_ge(da_turned, n)
                for j in range(ti + 1):
                    mm = pe.transpose(bank[6][:, j * P:(j + 1) * P], probs[:, n % 3, j * P:(j + 1) * P], ident[:, :])
                mm.then_inc(da_turn, 1)

            def values(n):
                h, ti = units[n]
                pe.wait_ge(da_turned, n + 1)
                if n:
                    pe.wait_ge(da_out, n)
                for j in range(ti + 1):
                    mm = pe.matmul(bank[7][:, 0:ADH], turned[:, n % 2, j * P:(j + 1) * P],
                                   att_v[:, j, h * ADH:(h + 1) * ADH], start=(j == 0), stop=(j == ti))
                mm.then_inc(da_sum, 1)

            pe.wait_ge(acol_ready, 1)
            logits(0)
            logits(1)
            per = len(units) // 8
            for n in range(len(units)):
                k = n % per * KD // per
                part = (k, k + KD // per)
                if n == 0:
                    column_tile(st["mem_qk"][0], of_u, part=part)
                if n + 2 < len(units):
                    logits(n + 2)
                if n:
                    column_tile(st["mem_qk"][n // per], of_u, part=part)
                turn(n)
                if n:
                    values(n - 1)
            values(len(units) - 1)
            pe.wait_ge(da_out, len(units))
            for i in range(4):
                if i >= 2:
                    pe.wait_ge(val_ready, n_lo["u"] + i - 1)
                for ti in range(NT):
                    mm = pe.transpose(bank[6 + i % 2][:, ti * P:(ti + 1) * P], att_o[:, ti, i * P:(i + 1) * P],
                                      ident[:, :])
                mm.then_inc(da_back, 1)

            pe.wait_ge(stack_ready, 2)
            oz = st["mem_oz"]

            def memory_spread(h):
                sel = sel_m[:, h * P:(h + 1) * P]
                if h:
                    pe.wait_ge(std_ready, h)
                pe.matmul(bank[4][:, :], sel, stack_m[:, :], start=True, stop=True)
                pe.matmul(bank[5][:, :], sel, stack_m[:, :], start=True, stop=False)
                pe.matmul(bank[5][:, :], ident_b[:, :], later4_b[:, :], start=False, stop=True).then_inc(ml_spread, 1)

            memory_spread(0)
            for h in range(MH):
                column_tile(oz[4 * h], of_u)
                column_tile(oz[4 * h + 1], of_u, part=(0, 3))
                pe.wait_ge(mem_qk_ready, MH + h + 1)
                pe.wait_ge(ml_decay, h + 1)
                for j in range(NT):
                    if j >= 2:
                        pe.wait_ge(ml_weight, NT * h + j - 1)
                    pe.matmul(bank[4 + j % 2][:, 0:S - j * P], mem_qk[:, MH + h, j * P:(j + 1) * P],
                              mem_qk[:, h, j * P:S], start=True, stop=True).then_inc(ml_score, 1)
                    if j:
                        column_tile(oz[4 * h + 1], of_u, part=((3, 5), (5, 7), (7, 8))[j - 1])
                if h:
                    pe.wait_ge(ml_h, 2 * h)
                else:
                    pe.wait_ge(val_ready, n_lo["mixa"])
                pe.wait_ge(ml_weight, NT * h + NT)
                for j in range(NT):
                    pe.matmul(bank[4][:, j * P:S], ones[:, 0:P], e_t(h, j), start=(j == 0), stop=(j == NT - 1))
                pe.matmul(bank[5][:, :], sel_m[:, h * P:(h + 1) * P], stack_f[:, :], start=True,
                          stop=True).then_inc(ml_sums, 1)
                for v in range(2):
                    for j in range(NT):
                        mm = pe.matmul(bank[6 + v][:, j * P:S], mem_v[:, j, h * MV + v * P:h * MV + (v + 1) * P],
                                       e_t(h, j), start=(j == 0), stop=(j == NT - 1))
                    mm.then_inc(ml_values, 1)
                column_tile(oz[4 * h + 2], of_u)
                column_tile(oz[4 * h + 3], of_u, part=(0, 2))
                pe.wait_ge(ml_floor, 2 * h + 2)
                rms(2, sq_m)
                column_tile(oz[4 * h + 3], of_u, part=(2, 8))
                if h + 1 < MH:
                    memory_spread(h + 1)

            def of_mix(k):
                if k < 4:
                    return mixa_hi[:, k, :], mixa_lo[:, k, :]
                return mix_hi[:, k - 4, :], mix_lo[:, (k - 4) // 2 + MH * (k % 2), :]

            column_tiles(st["out"], of_mix, n_lo["mixa"] - 4)
            column_tiles(st["ple"], lambda k: (p_hi[:, k, :], p_lo[:, k, :]), n_lo["p"] - 2)
            def two_sums(i):
                for k in range(2):
                    token_sums(i, KD, sq_f[:, 2 * (i % 2) + k, :], k, 2)

            for i, t in enumerate(st["gate"]):
                column_tile(t, lambda k: (h_hi[:, k, :], h_lo[:, k, :]), None if i else n_lo["h"] - KD)
                if i >= 2:
                    two_sums(i - 2)
            two_sums(KD - 2)
            two_sums(KD - 1)
            spread_scale(x2_diag[:, 0, :], 5)

            def of_u2(k):
                return u2_hi[:, k, :], u2_lo[:, k, :]

            column_pair(st["small2"] + st["ssd_b"][0:1], of_u2, n_lo["u2"] - KD)
            spread_scale(x2_diag[:, 1, :], 6)
            for t in st["ssd_b"][1:] + st["ssd_c"]:
                column_tile(t, of_u2)
            pe.wait_ge(lo_ready, n_lo["u2"])
            pe.wait_ge(acum_ready, 1)
            pe.wait_ge(dte_ready, NT)
            for c in range(NT):
                for i, r in enumerate((r_dt, r_dte, r_ac)):
                    k = SSD_H * (3 * c + i)
                    mm = pe.transpose(bank[5][:, k:k + SSD_H], r[:, c * P:(c + 1) * P], ident[0:SSD_H, 0:SSD_H])
            mm.then_inc(cols_turned, 1)
            pe.wait_ge(stack_a_ready, 1)
            pe.wait_ge(norm_std, 3)
            pe.matmul(bank[4][:, 0:2 * SSD_H], ones[0:SSD_H, 0:P], ends_diag[:, :], start=True,
                      stop=True).then_inc(ends_spread, 1)
            def spread_keys(p):
                for h in (2 * p, 2 * p + 1):
                    if p:
                        pe.wait_ge(l_ready, h - 1)
                    o = bank[4 + h % 2][:, :]
                    pe.matmul(o, one_hot[:, h:h + 1].broadcast_to([96, P]), stack_a[:, :], start=True, stop=False)
                    pe.matmul(o, ident_b[:, :], later4_b[:, :], start=False, stop=True).then_inc(a_spread, 1)

            def spread_features(p):
                if p:
                    pe.wait_ge(e_ready, p)
                else:
                    pe.wait_ge(dve_freed, [t for t in st["ssd_x"] if t["bank"] == 2][-1]["freed"][1])
                for h in (2 * p, 2 * p + 1):
                    r = slice(64 * (h % 2), 64 * (h % 2) + 64)
                    mm = pe.matmul(bank[2][r, :], one_hot[:, h:h + 1].broadcast_to([96, SSD_P]), stack_a[:, :],
                                   start=True, stop=True)
                mm.then_inc(e_spread, 1)

            def group_dot(g):
                for c in range(NT):
                    mm = pe.matmul(bank[6][:, c * P:(c + 1) * P], b_t[:, g, c * P:(c + 1) * P],
                                   c_t[:, g, c * P:(c + 1) * P], start=True, stop=True)
                mm.then_inc(grp_dot, 1)
                for c in range(3):
                    mm = pe.transpose(bank[7][:, c * P:(c + 1) * P], b_t[:, g, c * P:(c + 1) * P], ident[:, :])
                mm.then_inc(grp_dot, 1)

            def group_sum(g):
                pe.wait_ge(sum_ready, g + 1)
                pe.matmul(bank[3][:, :], ones[:, 0:P], sq_y[:, 0, :], start=True, stop=True).then_inc(sum_used, 1)

            def turn_x(g, c):
                for i in range(4):
                    mm = pe.transpose(bank[6 + c % 2][:, i * P:(i + 1) * P], y[:, 4 * g + i, c * P:(c + 1) * P],
                                      ident[:, :])
                mm.then_inc(x_turned, 1)

            def chunk_state(g, c):
                pe.wait_ge(xdec_ready, 3 * g + c + 1)
                pe.matmul(bank[6 + c % 2][:, :], b_tok[:, c * P:(c + 1) * P], xdec[:, c, :], start=True,
                          stop=True).then_inc(state_dot, 1)

            early = len(st["ssd_x"]) - 4
            for t in st["ssd_x"][:early]:
                column_tile(t, of_u2)
            pe.wait_ge(consts2_in, 16 * 3)
            pe.wait_ge(cols_ready, 3)
            spread_keys(0)
            pe.wait_ge(conv_ready, 2 * SSD_G)
            group_dot(0)
            for t in st["ssd_x"][early:]:
                column_tile(t, of_u2)
            for g in range(SSD_G):
                z = st["z"][4 * g]
                if g:
                    column_tile(z, of_u2, part=(0, 2))
                    pe.wait_ge(y_read, 4 * g)
                    group_dot(g)
                else:
                    pe.wait_ge(conv_ready, 2 * SSD_G + 4)
                pe.wait_ge(grp_copied, 2 * g + 1)
                turn_x(g, 0)
                pe.wait_ge(grp_copied, 2 * g + 2)
                turn_x(g, 1)
                if g:
                    column_tile(z, of_u2, part=(2, 4))
                else:
                    column_tile(z, of_u2, part=(0, 5))
                    spread_features(0)
                for c in (2, 3):
                    pe.wait_ge(xdt_ready, NT * g + c - 1)
                    turn_x(g, c)
                if g:
                    column_tile(z, of_u2, part=(4, 5))
                for c in (0, 1):
                    pe.wait_ge(xdt_ready, NT * g + c + 3)
                    chunk_state(g, c)
                column_tile(z, of_u2, part=(5, 6))
                pe.wait_ge(state_ready, 3 * g + 1)
                chunk_state(g, 2)
                column_tile(z, of_u2, part=(6, 8))
                for q in range(4):
                    p = 4 * g + q
                    if q:
                        column_tile(st["z"][p], of_u2)
                    if g and q == 2:
                        group_sum(g - 1)
                    if p + 1 < 16:
                        spread_keys(p + 1)
                        spread_features(p + 1)
                    if q == 0:
                        pe.wait_ge(state_ready, 3 * (g + 1))
                    else:
                        pe.wait_ge(y_read, p)
                    for h in (2 * p, 2 * p + 1):
                        pe.wait_ge(w_ready, h + 1)
                        r, f = slice(64 * (h % 2), 64 * (h % 2) + 64), (h % 8) * SSD_P
                        for c in range(NT):
                            mm = pe.matmul(bank[6][r, c * P:(c + 1) * P], xdt[:, c, f:f + SSD_P],
                                           weight(h)[:, c * P:(c + 1) * P], start=True, stop=True)
                        mm.then_inc(y_dot, 1)
                    for c in range(1, NT):
                        mm = pe.matmul(bank[7][:, c * P:(c + 1) * P], states[:, c - 1, q * P:(q + 1) * P],
                                       c_t[:, g, c * P:(c + 1) * P], start=True, stop=True)
                    mm.then_inc(off_dot, 1)
            column_tile(st["qa"][0], of_u2)
            column_tile(st["qa"][1], of_u2)
            column_tile(st["kva"][0], of_u2, part=(0, 5))
            group_sum(SSD_G - 1)
            column_tile(st["kva"][0], of_u2, part=(5, 8))
            pe.wait_ge(e_ready, 16)
            for i, t in enumerate(st["ssd_out"]):
                column_tile(t, lambda k: (y_hi[:, k, :], y_lo[:, k, :]), None if i else n_lo["y"] - 16)
                if i < 2:
                    rms(2 - i, sq_s)

            pe.wait_ge(lo_ready, n_lo["kn"])

            def project(h):
                if h:
                    pe.wait_ge(std_qk_ready, 2 * h)
                    pe.wait_ge(k_ready, h)
                column_tile(st["head_q"][h], lambda k: (qn_hi[:, k, :], qn_lo[:, k, :]))
                column_tile(st["head_k"][h], lambda k: (kn_hi[:, :], kn_lo[:, :]))

            def query_sums(h):
                pe.wait_ge(head_sq, 2 * h + 1)
                pe.wait_ge(dve_freed, st["head_q"][h]["freed"][1])
                for ti in range(NT):
                    pe.matmul(bank[1][:, ti:ti + 1], sq_q[:, ti * P:(ti + 1) * P], ones[0:QK, 0:1], start=True,
                              stop=True)

            def key_sums(h):
                pe.wait_ge(head_sq, 2 * h + 2)
                if h == 0:
                    pe.wait_ge(krope_sq, 1)
                for ti in range(NT):
                    mm = pe.matmul(bank[1][:, NT + ti:NT + ti + 1], sq_k[:, ti * P:(ti + 1) * P], ones[0:QK, 0:1],
                                   start=True, stop=True)
                mm.then_inc(head_sums, 1)

            def key_spread(h):
                pe.wait_ge(rk_diag_ready, h + 1)
                pe.wait_ge(dve_freed, st["head_k"][h]["freed"][1])
                pe.matmul(bank[2][0:QK, :], ones[:, 0:QK], rk_diag[:, :], start=True, stop=True).then_inc(rk_spread, 1)

            def head_logits(n):
                h, ti = heads[n]
                W = (ti + 1) * P
                if ti == 0:
                    pe.wait_ge(k_ready, h + 1)
                    pe.wait_ge(dve_freed, st["head_q"][h]["freed"][1])
                if n >= 2:
                    pe.wait_ge(x_probs, n - 1)
                o = bank[4 + n % 2]
                pe.matmul(o[:, 0:W], q_s[:, h % 2, ti * P:W], k_s[:, h % 2, 0:W], start=True, stop=False)
                pe.matmul(o[:, ti * P:W], ident_b[:, :], tri_b[:, :], start=False, stop=True).then_inc(x_logits, 1)

            def head_turn(n):
                h, ti = heads[n]
                pe.wait_ge(x_probs, n + 1)
                if n:
                    pe.wait_ge(x_turned_out, n)
                for j in range(ti + 1):
                    mm = pe.transpose(bank[6][:, j * P:(j + 1) * P], probs_x[:, n % 2, j * P:(j + 1) * P], ident[:, :])
                mm.then_inc(x_turn, 1)

            def head_values(n):
                h, ti = heads[n]
                pe.wait_ge(x_turned_out, n + 1)
                if n:
                    pe.wait_ge(x_out, n)
                o = bank[7][:, 0:VD]
                for j in range(ti + 1):
                    mm = pe.matmul(o, turned_x[n % 2][:, j * P:(j + 1) * P], v_tok[:, j, h * VD:(h + 1) * VD],
                                   start=(j == 0), stop=(j == ti))
                mm.then_inc(x_sum, 1)

            def of_kn(k):
                return kn_hi, kn_lo

            gate0 = st["mix_gate"][0]
            project(0)
            row_tiles(st["v"][0:4], of_kn)
            column_tile(gate0, of_u2, part=(0, 3))
            query_sums(0)
            key_sums(0)
            row_tiles(st["v"][4:8], of_kn)
            column_tile(gate0, of_u2, part=(3, 4))
            key_spread(0)
            column_tile(gate0, of_u2, part=(4, 6))
            pe.wait_ge(act_freed, st["v"][6]["freed"][1])
            pe.wait_ge(dve_freed, st["v"][7]["freed"][1])
            head_logits(0)
            head_logits(1)
            project(1)
            column_tile(gate0, of_u2, part=(6, 8))
            for n, (h, ti) in enumerate(heads):
                if n + 2 < len(heads):
                    head_logits(n + 2)
                if ti == 2 and h + 2 < XH:
                    project(h + 2)
                if h:
                    column_tile(st["mix_gate"][h], of_u2, part=((0, 2), (3, 4), (5, 6), (6, 8))[ti])
                if ti == 1 and h + 1 < XH:
                    key_spread(h + 1)
                if h and ti == 1:
                    column_tile(st["mix_gate"][h], of_u2, part=(4, 5))
                if ti == 0:
                    if h + 1 < XH:
                        query_sums(h + 1)
                    if h:
                        column_tile(st["mix_gate"][h], of_u2, part=(2, 3))
                    if h + 1 < XH:
                        key_sums(h + 1)
                head_turn(n)
                if n:
                    head_values(n - 1)
            head_values(len(heads) - 1)
            pe.wait_ge(x_out, len(heads))
            for i in range(KD):
                if i >= 2:
                    pe.wait_ge(lo_ready, n_lo["kn"] + i - 1)
                for ti in range(NT):
                    mm = pe.transpose(bank[6 + i % 2][:, ti * P:(ti + 1) * P], o_tok[:, ti, i * P:(i + 1) * P],
                                      ident[:, :])
                mm.then_inc(o_back, 1)

            column_tiles(st["mla_out"], lambda k: (o_hi[:, k, :], o_lo[:, k, :]), n_lo["o"] - KD, pair=True)
            for i, t in enumerate(st["mix_out"]):
                column_tile(t, lambda k: (fused_hi[:, k, :], fused_lo[:, k, :]), None if i else n_lo["fused"] - KD)
                if i:
                    token_sums(i - 1, KD, sq_x[:, (i - 1) % 2, :])
            token_sums(KD - 1, KD, sq_x[:, (KD - 1) % 2, :])
            spread_scale(x3_diag[:, :], 5)

            def of_u3(k):
                return u3_hi[:, k, :], u3_lo[:, k, :]

            column_tiles(up[0:4], of_u3, n_lo["u3"] - KD, pair=True)
            with pe.Fori(1, UP_LOOPS) as g:
                for j in range(4):
                    pe.wait_ge(dve_freed, 4 * g + (up_freed + j - 4))
                    pe.wait_ge(w_lo_ready, 4 * g + (up_chunk + j + 1))
                    r = (up_chunk + j) % RING
                    for k in range(KD):
                        hi, lo = (w[:, r, k * P:(k + 1) * P] for w in (w_hi, w_lo))
                        xh, xl = of_u3(k)
                        pe.matmul(bank[j][:, :], hi, xh, start=(k == 0), stop=False)
                        pe.matmul(bank[j][:, :], hi, xl, start=False, stop=False)
                        mm = pe.matmul(bank[j][:, :], lo, xh, start=False, stop=(k == KD - 1))
                    mm.then_inc(dense_done, 1)
            column_tiles(st["down"], lambda k: (act_hi[:, k, :], act_lo[:, k, :]), n_lo["act"] - FT)


        @block.scalar
        def _(act):
            next_hi, steps, evs, sqs, his = [0], [0], [0], [0], [0]

            def split_weights(done):
                while next_hi[0] <= min(done + RING, N_CHUNK - 1):
                    c = next_hi[0]
                    act.wait_ge(w_landed[c % RING], 16 * (c // RING + 1))
                    if c >= RING:
                        act.wait_ge(dense_done, plan.used_at[c - RING])
                    act.activation(w_hi[:, c % RING, :], w_raw[:, c % RING, :], ACT.Copy).then_inc(w_hi_ready, 1)
                    next_hi[0] += 1

            def after(t):
                split_weights(t["upto"])

            def link(ins):
                steps[0] += 1
                ins.then_inc(act_step, 1)
                act.wait_ge(act_step, steps[0])

            def rms(src, n, width, sq, std, b=4):
                for i in range(n):
                    if sqs[0] >= 2:
                        act.wait_ge(sq_used, sqs[0] - 1)
                    act.activation(sq[:, i % 2, :], src(i), ACT.Square).then_inc(sq_ready, 1)
                    sqs[0] += 1
                act.wait_ge(sq_used, sqs[0])
                act.activation(std[:, :], bank[b][:, :], ACT.Sqrt, bias=vec("eps"),
                               scale=1.0 / width).then_inc(std_ready, 1)

            def load_root():
                act.activation(norm_col[:, 2, 0:1], vec("eps"), ACT.Sqrt)

            def token_std(sums, k, bias="eps"):
                act.wait_ge(sq_used, sqs[0])
                act.activation(norm_col[:, k, :], sums, ACT.Sqrt, bias=vec(bias), scale=1.0 / D).then_inc(norm_std, 1)

            vals = [0]

            def high_parts(dst, src, n):
                for i in range(n):
                    vals[0] += 1
                    act.wait_ge(val_ready, vals[0])
                    act.activation(dst(i), src(i), ACT.Copy).then_inc(hi_ready, 1)

            def tile_done(t):
                act.wait_ge(dense_done, t["full"])

            def rows_out(tiles, dst):
                for c, s in tiles[0]["parts"][:-1]:
                    if s == CH * P // S - 1:
                        split_weights(c)
                for i in (0, 2):
                    tile_done(tiles[i])
                    act.copy(dst(i), bank[tiles[i]["bank"]][:, :]).then_inc(act_freed, 1)
                after(tiles[0])

            def sigmoid_of(t):
                tile_done(t)
                if evs[0] >= 2:
                    act.wait_ge(ev_used, evs[0] - 1)
                act.activation(ev[:, evs[0] % 2, :], bank[t["bank"]][:, :], ACT.Sigmoid).then_inc(ev_ready, 1)
                evs[0] += 1
                after(t)

            act.dma_start(vecs[:, :], a["vecs"]).then_inc(vecs_in, 16)
            act.dma_start(squares_f[:, :], a["squares_f"]).then_inc(squares_in, 16)

            def x_tile(i):
                act.wait_ge(x_in[i], 16)
                return xt[:, i, :]

            act.wait_ge(vecs_in, 16)
            load_root()
            for i in range(KD):
                if i >= 2:
                    act.wait_ge(sq_used, i - 1)
                act.activation(sq[:, i % 2, :], x_tile(i), ACT.Square).then_inc(sq_ready, 1)
                if i == KD - 2:
                    split_weights(-RING)
            sqs[0] = KD
            token_std(bank[4][:, 0:NT], 0)
            split_weights(-1)
            high_parts(lambda i: u_hi[:, i, :], lambda i: u_val[:, i % 2, :], KD)
            act.wait_ge(bias_dot, 1)
            w = HANK // 2
            for j in range(2):
                ins = act.mul(bias_row[:, j * w:(j + 1) * w], bank[6 + j][0:AH, 0:w], ADH ** 0.5)
                ins.then_inc(bias_out, 1)
            act.wait_ge(bias_out, 2)
            rows = bias_row[:, :].unsqueeze(1).broadcast_to([AH, P, HANK])
            act.dma_start(bias_dram, rows).then_inc(stored, 16)
            act.sem_inc(bias_ready, 1)
            for i, t in enumerate(st["idx_q"]):
                tile_done(t)
                act.mul(iq[:, i, :], bank[t["bank"]][:, :], IDH ** -0.5).then_inc(act_freed, 1)
                after(t)
            t = st["idx_k"][0]
            tile_done(t)
            act.copy(ik[:, :], bank[t["bank"]][:, :]).then_inc(act_freed, 1)
            after(t)
            t = st["small"][0]
            tile_done(t)
            act.activation(small[:, :], bank[t["bank"]][:, :], ACT.Identity, bias=vec("gate_bias"),
                           scale=vec("gate_scale")).then_inc(act_freed, 1)
            after(t)
            act.wait_ge(iw_turned, 1)
            act.copy(iw[:, :, :].rearrange("p a b -> p (a b)"), bank[5][:, 0:3 * IH]).then_inc(iw_ready, 1)
            n = 0
            for ti in range(1, NT):
                W = (ti + 1) * P
                for h in range(IH):
                    act.wait_ge(idx_dot, n + 1)
                    if n >= 2:
                        act.wait_ge(idx_added, n - 1)
                    act.activation(relu[:, n % 2, 0:W], bank[6 + n % 2][:, 0:W], ACT.Relu).then_inc(idx_relu, 1)
                    n += 1
            for name, dst in (("att_q", att_q), ("att_k", att_k)):
                for i, t in enumerate(st[name]):
                    tile_done(t)
                    act.copy(dst[:, i, :], bank[t["bank"]][:, :]).then_inc(act_freed, 1)
                    after(t)
            rows_out(st["att_v"], lambda i: att_v[:, i, :])
            act.wait_ge(ml_f, 1)
            link(act.activation(r_t[:, :], r_f[:, :], ACT.Abs))
            link(act.activation(r_t[:, :], r_t[:, :], ACT.Exp, scale=-1.0))
            act.activation(r_t[:, :], r_t[:, :], ACT.Ln, bias=1.0).then_inc(ml_log, 1)
            for half in range(2):
                rows_out(st["mem_v"][4 * half:4 * half + 4], lambda i: mem_v[:, i, half * S:(half + 1) * S])
            act.wait_ge(acol_turned, 1)
            act.copy(acol[:, :], bank[5][:, 0:NT * MH]).then_inc(acol_ready, 1)
            def load_bias(h):
                if h >= 2:
                    act.wait_ge(da_bias, NT * (h - 1))
                src = bass.AP(bias_dram.tensor, h * P * HANK + P - 1, [[HANK - 1, P], [1, S]])
                act.dma_start(hank[:, h % 2, :], src).then_inc(hank_in[h % 2], 16)

            act.wait_ge(stored, 16)
            load_bias(0)
            load_bias(1)
            act.wait_ge(chosen_ready, NT)
            for t in st["att_z"]:
                sigmoid_of(t)

            def newest_tap(i):
                t = st["mem_qk"][i]
                tile_done(t)
                if evs[0] >= 2:
                    act.wait_ge(ev_used, evs[0] - 1)
                act.activation(ev[:, evs[0] % 2, :], bank[t["bank"]][:, :], ACT.Copy,
                               scale=vec("conv_w", 4 * i + 3)).then_inc(ev_ready, 1)
                evs[0] += 1
                after(t)

            def conv_sigmoid(i):
                act.wait_ge(taps_ready, i + 1)
                if i:
                    act.wait_ge(mem_qk_ready, i)
                act.activation(sg[:, :], mem_qk[:, i, :], ACT.Sigmoid).then_inc(sg_ready, 1)

            def da_exp(n):
                h, ti = units[n]
                W = (ti + 1) * P
                act.wait_ge(da_max, n + 1)
                act.activation(probs[:, n % 3, 0:W], probs[:, n % 3, 0:W], ACT.Exp, bias=da_cols[:, 1, n:n + 1],
                               scale=ADH ** -0.5, accum_out=da_cols[:, 2, n:n + 1]).then_inc(da_probs, 1)

            da_exp(0)
            for n, (h, ti) in enumerate(units):
                W = (ti + 1) * P
                if n + 1 < len(units):
                    da_exp(n + 1)
                if ti == 3 and h < AH - 2:
                    load_bias(h + 2)
                if ti == 0 and h:
                    newest_tap(h - 1)
                if ti == 3 and h:
                    conv_sigmoid(h - 1)
                act.wait_ge(da_turn, n + 1)
                if n >= 2:
                    act.wait_ge(da_sum, n - 1)
                act.copy(turned[:, n % 2, 0:W], bank[6][:, 0:W]).then_inc(da_turned, 1)
            high_parts(lambda i: mixa_hi[:, i, :], lambda i: val_m[:, i % 2, :], 4)
            newest_tap(AH - 1)

            act.wait_ge(stack_ready, 2)
            oz = st["mem_oz"]

            def decays(h):
                act.wait_ge(ml_spread, h + 1)
                if h >= 2:
                    act.wait_ge(ml_sums, h - 1)
                for j in range(NT):
                    col = acol[:, j * MH + h:j * MH + h + 1]
                    e = e_t(h, j)
                    if j < NT - 1:
                        act.activation(e[:, P:], bank[4][:, (j + 1) * P:S], ACT.Exp, bias=col)
                    ins = act.activation(e[:, 0:P], bank[5][:, j * P:(j + 1) * P], ACT.Exp, bias=col)
                ins.then_inc(ml_decay, 1)

            def out_gate(h, k):
                t = oz[4 * h + k]
                if k % 2:
                    sigmoid_of(t)
                else:
                    tile_done(t)
                    act.activation(mem_o[:, 2 * h + k // 2, :], bank[t["bank"]][:, :],
                                   ACT.Sigmoid).then_inc(act_freed, 1)
                    after(t)

            decays(0)
            conv_sigmoid(AH - 1)
            for h in range(MH):
                out_gate(h, 0)
                out_gate(h, 1)
                act.wait_ge(ml_sums, h + 1)
                if h:
                    act.wait_ge(ml_h, 2 * h)
                act.activation(den[:, :], bank[4][:, :], ACT.Abs).then_inc(ml_floor, 1)
                act.activation(floor[:, :], bank[5][:, :], ACT.Exp).then_inc(ml_floor, 1)
                for v in range(2):
                    act.wait_ge(ml_h, 2 * h + v + 1)
                    act.activation(sq_m[:, v, :], h_val[:, v, :], ACT.Square).then_inc(sq_ready, 1)
                    sqs[0] += 1
                out_gate(h, 2)
                act.wait_ge(sq_used, sqs[0])
                if h:
                    act.wait_ge(inv_ready, h)
                act.activation(std_m[:, :], bank[4][:, :], ACT.Sqrt, bias=vec("eps"),
                               scale=1.0 / MV).then_inc(std_ready, 1)
                out_gate(h, 3)
                if h + 1 < MH:
                    decays(h + 1)
                if h == MH - 1:
                    act.dma_start(xt2[:, :, :], a["x_t"]).then_inc(x2_in, 16)
                    act.dma_start(p_val[:, :, :], a["p_t"]).then_inc(p_in, 16)
                high_parts(lambda i: mix_hi[:, 2 * h + i, :], lambda i: val_m[:, i, :], 2)
            act.wait_ge(p_in, 16)
            for i in range(2):
                act.activation(p_hi[:, i, :], p_val[:, i, :], ACT.Copy).then_inc(hi_ready, 1)
            for i, t in enumerate(st["out"]):
                tile_done(t)
                after(t)
                act.wait_ge(h_res_ready, i + 1)
                act.activation(h_hi[:, i, :], h_res[:, i, :], ACT.Copy).then_inc(hi_ready, 1)
            for i, t in enumerate(st["ple"]):
                tile_done(t)
                act.copy(ple[:, i, :], bank[t["bank"]][:, :]).then_inc(act_freed, 1)
                after(t)

            def two_squares(i):
                act.wait_ge(ple_added, i + 1)
                for k, scale in enumerate((1.0, vec("norm_final", i))):
                    if i >= 2 or i == k == 0:
                        act.wait_ge(sq_used, sqs[0] - (3 if i else 0))
                    act.activation(sq_f[:, 2 * (i % 2) + k, :], h_res[:, i, :], ACT.Square,
                                   scale=scale).then_inc(sq_ready, 1)
                    sqs[0] += 1

            for i, t in enumerate(st["gate"]):
                tile_done(t)
                if i >= 2:
                    act.wait_ge(ple_added, i - 1)
                act.activation(gate[:, i % 2, :], bank[t["bank"]][:, :], ACT.Sigmoid).then_inc(act_freed, 1)
                after(t)
                if i:
                    two_squares(i - 1)
            two_squares(KD - 1)
            load_root()
            act.wait_ge(norm_sums_in, 1)
            token_std(norm_col[:, 0, :], 0, "eps2")
            token_std(bank[4][:, 0:NT], 1)
            high_parts(lambda i: u2_hi[:, i, :], lambda i: val_f[:, i % 2, :], KD)

            for dst, name in ((one_hot, "one_hot"), (trig, "trig"), (tri_b, "tri_b")):
                act.dma_start(dst[:, :], a[name]).then_inc(consts2_in, 16)
            t = st["small2"][0]
            tile_done(t)
            act.activation(small2[:, :], bank[t["bank"]][:, :], ACT.Identity, bias=vec("dt_bias")).then_inc(act_freed, 1)
            after(t)
            act.wait_ge(act_freed, t["freed"][1])
            link(act.activation(r_t2[:, :], small2[0:SSD_H, :], ACT.Abs))
            link(act.activation(r_t2[:, :], r_t2[:, :], ACT.Exp, scale=-1.0))
            act.activation(rate[:, :], vecs[0:SSD_H, VEC["a_log"][0]:VEC["a_log"][0] + 1], ACT.Exp).then_inc(rate_ready, 1)
            act.activation(r_t2[:, :], r_t2[:, :], ACT.Ln, bias=1.0).then_inc(dt_log, 1)
            def key_decays(p):
                for h in (2 * p, 2 * p + 1):
                    act.wait_ge(a_spread, h + 1)
                    if h >= 4:
                        act.wait_ge(y_dot, h - 3)
                    for c in range(NT):
                        ins = act.activation(weight(h)[:, c * P:(c + 1) * P], bank[4 + h % 2][:, c * P:(c + 1) * P],
                                             ACT.Exp, bias=cols[:, 3 * c + 2, h:h + 1])
                    ins.then_inc(l_ready, 1)

            def start_decays(p):
                act.wait_ge(e_spread, p + 1)
                if p >= 2:
                    act.wait_ge(y_ready, p - 1)
                act.activation(e_ac[:, p % 2, :], bank[2][:, :], ACT.Exp).then_inc(e_ready, 1)

            def group_out(g):
                act.wait_ge(grp_dot, 2 * g + 1)
                if g:
                    act.wait_ge(w_ready, 8 * g)
                act.copy(scores[:, :], bank[6][:, :]).then_inc(grp_copied, 1)
                act.wait_ge(grp_dot, 2 * g + 2)
                act.copy(b_tok[:, :], bank[7][:, 0:3 * P]).then_inc(grp_copied, 1)

            for i in range(len(conv_tiles) + 1):
                if i < len(conv_tiles):
                    t, w, _ = conv_tiles[i]
                    tile_done(t)
                    if i >= 2:
                        act.wait_ge(conv_ready, i - 1)
                    act.activation(taps[:, i % 2, :], bank[t["bank"]][:, :], ACT.Identity, bias=vec("ssd_conv_b", w),
                                   scale=vec("ssd_conv_w", 4 * w + 3)).then_inc(conv_in, 1)
                    after(t)
                if i == 2:
                    act.wait_ge(acum_ready, 1)
                    for c in range(NT):
                        act.activation(r_dte[:, c * P:(c + 1) * P], r_ac[:, c * P:(c + 1) * P], ACT.Exp, scale=-1.0,
                                       bias=r_ac[:, (c + 1) * P - 1:(c + 1) * P]).then_inc(dte_ready, 1)
                if i == 10:
                    act.wait_ge(cols_turned, 1)
                    act.copy(cols[:, :, :].rearrange("p a b -> p (a b)"), bank[5][:, 0:3 * NT * SSD_H]
                             ).then_inc(cols_ready, 1)
                    act.wait_ge(cols_ready, 1)
                    for c in range(NT):
                        ins = act.mul(cols[:, 3 * c + 2, :], cols[:, 3 * c + 2, :], -1.0)
                    ins.then_inc(cols_ready, 1)
                    act.wait_ge(ends_spread, 1)
                    act.activation(chunk_decay[:, :], bank[4][:, 0:2 * SSD_H], ACT.Exp).then_inc(cols_ready, 1)
                if i == len(conv_tiles) - 4:
                    act.wait_ge(stack_a_ready, 2)
                    act.wait_ge(cols_ready, 3)
                    group_out(0)
                    key_decays(0)
                if i:
                    act.wait_ge(dve_freed, conv_tiles[i - 1][0]["freed"][1])
                    act.activation(taps_sg[:, (i - 1) % 2, :], taps[:, (i - 1) % 2, :], ACT.Sigmoid).then_inc(conv_sg, 1)

            def group_std(g):
                act.wait_ge(sum_used, g + 1)
                if g:
                    act.wait_ge(inv_ready, n_inv + g)
                act.activation(std_y[:, :], bank[3][:, :], ACT.Sqrt, bias=vec("eps"),
                               scale=1.0 / (4 * P)).then_inc(std_ready, 1)

            start_decays(0)
            for g in range(SSD_G):
                if g:
                    group_out(g)
                for p in range(4 * g, 4 * g + 4):
                    t = st["z"][p]
                    tile_done(t)
                    if p:
                        act.wait_ge(y_ready, p)
                    act.activation(z_sg[:, :], bank[t["bank"]][:, :], ACT.Sigmoid).then_inc(z_ready, 1)
                    after(t)
                    if p + 1 < 16:
                        key_decays(p + 1)
                        start_decays(p + 1)
                    if g and p % 4 == 1:
                        group_std(g - 1)
            act.wait_ge(y_ready, 16)

            def y_high(first, end):
                for i in range(first, end):
                    act.wait_ge(y_normed, i + 1)
                    act.activation(y_hi[:, i, :], y[:, i, :], ACT.Copy).then_inc(hi_ready, 1)

            def latent(t, dst):
                tile_done(t)
                act.copy(dst, bank[t["bank"]][:, :]).then_inc(act_freed, 1)
                after(t)

            y_high(0, 4)
            latent(st["qa"][0], qa_val[:, 0, :])
            latent(st["qa"][1], qa_val[:, 1, :])
            group_std(SSD_G - 1)
            y_high(4, 12)
            latent(st["kva"][0], kva_val[:, :])
            y_high(12, 16)
            act.wait_ge(act_freed, st["kva"][0]["freed"][1])
            rms(lambda i: qa_val[:, i, :], 2, 256, sq_s, std_s)
            after(st["ssd_out"][0])
            high_parts(lambda i: qn_hi[:, i, :], lambda i: qa_val[:, i, :], 2)
            act.wait_ge(inv_ready, n_inv + SSD_G + 1)
            rms(lambda i: kva_val[:, :], 1, 128, sq_s, std_s)
            after(st["ssd_out"][1])
            high_parts(lambda i: kn_hi[:, :], lambda i: kva_val[:, :], 1)
            for i, t in enumerate(st["ssd_out"]):
                for c, s in t["parts"][:-1]:
                    if s == CH - 1:
                        split_weights(c)
                tile_done(t)
                act.copy(y_ssd[:, i, :], bank[t["bank"]][:, :]).then_inc(act_freed, 1)
                after(t)

            act.activation(sq_k[NOPE:QK, :], small2[NOPE:QK, :], ACT.Square).then_inc(krope_sq, 1)

            def head_parts(h):
                tq, tk2 = st["head_q"][h], st["head_k"][h]
                tile_done(tk2)
                if h:
                    act.wait_ge(head_sums, h)
                act.activation(sq_q[:, :], bank[tq["bank"]][0:QK, :], ACT.Square).then_inc(head_sq, 1)
                act.activation(sq_k[0:NOPE, :], bank[tk2["bank"]][0:NOPE, :], ACT.Square).then_inc(head_sq, 1)
                after(tk2)

            def head_norms(h):
                act.wait_ge(head_sums, h + 1)
                if h >= 2:
                    act.wait_ge(x_probs, NT * (h - 1))
                    act.wait_ge(rk_diag_ready, h - 1)
                r = r_qk[:, h % 2, :]
                act.activation(r[:, 0:NT], bank[1][:, 0:NT], ACT.Sqrt, bias=vec("eps_q")).then_inc(std_qk_ready, 1)
                act.activation(r[:, NT:2 * NT], bank[1][:, NT:2 * NT], ACT.Sqrt, bias=vec("eps"),
                               scale=1.0 / QK).then_inc(std_qk_ready, 1)

            def mix_gate(h):
                t = st["mix_gate"][h]
                tile_done(t)
                if h >= KD:
                    act.wait_ge(gates_used, h - KD + 1)
                act.activation(gm[:, h % KD, :], bank[t["bank"]][:, :], ACT.Sigmoid,
                               bias=vec("gate_b", h)).then_inc(act_freed, 1)

            def head_probs(n):
                h, ti = heads[n]
                W = (ti + 1) * P
                act.wait_ge(x_max, n + 1)
                if n >= 2:
                    act.wait_ge(x_turn, n - 1)
                act.activation(probs_x[:, n % 2, 0:W], bank[4 + n % 2][:, 0:W], ACT.Exp, bias=x_cols[:, 1, n:n + 1],
                               scale=r_qk[:, h % 2, ti:ti + 1], accum_out=x_cols[:, 2, n:n + 1]).then_inc(x_probs, 1)

            def head_turned(n):
                W = (heads[n][1] + 1) * P
                act.wait_ge(x_turn, n + 1)
                if n >= 2:
                    act.wait_ge(x_sum, n - 1)
                act.copy(turned_x[n % 2][:, 0:W], bank[6][:, 0:W]).then_inc(x_turned_out, 1)

            def values_out(half):
                rows_out(st["v"][4 * half:4 * half + 4], lambda i: v_tok[:, i, half * S:(half + 1) * S])

            head_parts(0)
            values_out(0)
            head_norms(0)
            values_out(1)
            head_probs(0)
            head_parts(1)
            for n, (h, ti) in enumerate(heads):
                if ti == 1 and h:
                    mix_gate(h - 1)
                if n + 1 < len(heads):
                    head_probs(n + 1)
                if ti == 0 and h + 1 < XH:
                    head_norms(h + 1)
                if ti == 3 and h + 2 < XH:
                    head_parts(h + 2)
                head_turned(n)
                if ti == 1 and h:
                    after(st["mix_gate"][h - 1])
            mix_gate(XH - 1)
            after(st["mix_gate"][XH - 1])
            for i in range(KD):
                act.wait_ge(o_back, i + 1)
                act.activation(o_hi[:, i, :], bank[6 + i % 2][:, :], ACT.Copy).then_inc(hi_ready, 1)

            for i, t in enumerate(st["mla_out"]):
                tile_done(t)
                after(t)
                high_parts(lambda _: fused_hi[:, i, :], lambda _: gm[:, i, :], 1)
            load_root()
            for i, t in enumerate(st["mix_out"]):
                tile_done(t)
                after(t)
                act.wait_ge(dve_freed, t["freed"][1])
                act.wait_ge(sq_used, sqs[0] - 1)
                act.activation(sq_x[:, i % 2, :], h_res[:, i, :], ACT.Square).then_inc(sq_ready, 1)
                sqs[0] += 1
            token_std(bank[4][:, 0:NT], 0)
            high_parts(lambda i: u3_hi[:, i, :], lambda i: val_x[:, i % 2, :], KD)
            v0 = vals[0]

            def up_tile(g, j):
                act.wait_ge(dense_done, 4 * g + (up_done + j))
                act.activation((ffn_g, ffn_v)[j % 2][:, j // 2, :], bank[j][:, :], ACT.Identity,
                               bias=up_vec("ffn_conv_b", 4 * g + j),
                               scale=up_vec("ffn_conv_w", 12 * g + (3 * j + 2))).then_inc(act_in, 1)
                c = up_chunk + j + RING
                act.wait_ge(w_landed[c % RING], 16 * g + 16 * (c // RING + 1))
                act.activation(w_hi[:, c % RING, :], w_raw[:, c % RING, :], ACT.Copy).then_inc(w_hi_ready, 1)

            def up_pair(k, b):
                act.wait_ge(dve_freed, 2 * k + up_freed)
                act.activation(ffn_sg[:, b, :], ffn_g[:, b, :], ACT.Sigmoid).then_inc(act_sg, 1)
                act.wait_ge(val_ready, k + (v0 + 1))
                act.activation(act_hi[:, bass.ds(k, 1), :].rearrange("p a n -> p (a n)"), ffn_g[:, b, :],
                               ACT.Copy).then_inc(hi_ready, 1)

            for j in range(4):
                up_tile(0, j)
                if j == 2:
                    up_pair(0, 0)
            with act.Fori(1, UP_LOOPS) as g:
                for j in range(4):
                    act.wait_ge(lo_ready, 2 * g + (n_lo["u3"] + j // 2 - 1))
                    up_tile(g, j)
                    if j == 0:
                        up_pair(2 * g - 1, 1)
                    if j == 2:
                        up_pair(2 * g, 0)
            up_pair(FT - 1, 1)
            vals[0] += FT
            next_hi[0] = up_chunk + len(up) + RING
            for t in st["down"]:
                for c, s in t["parts"][:-1]:
                    if s == CH - 1:
                        split_weights(c)
                tile_done(t)
                after(t)

        @block.vector
        def _(dve):
            steps, his, vals, evs, frees, invs = [0], [0], [0], [0], [0], [0]

            def link(ins):
                steps[0] += 1
                ins.then_inc(dve_step, 1)
                dve.wait_ge(dve_step, steps[0])

            def split(n, make, src, hi, lo):
                for i in range(n + 1):
                    if i < n:
                        if his[0]:
                            dve.wait_ge(lo_ready, his[0])
                        make(i).then_inc(val_ready, 1)
                        vals[0] += 1
                    if i:
                        dve.wait_ge(val_ready, vals[0] - (1 if i < n else 0))
                        low(src(i - 1), hi(i - 1), lo(i - 1))

            def low(src, hi, lo):
                his[0] += 1
                dve.wait_ge(hi_ready, his[0])
                dve.tensor_tensor(lo, src, hi.bitcast(F32), ALU.subtract).then_inc(lo_ready, 1)

            def inverse(inv, std):
                first_inverses(inv, std, 0)
                last_inverses(inv, std, 0)

            def first_inverses(inv, std, n):
                invs[0] += 1
                dve.wait_ge(std_ready, invs[0])
                if n:
                    dve.reciprocal(inv[:, 0:n], std[:, 0:n])

            def last_inverses(inv, std, n):
                dve.reciprocal(inv[:, n:S], std[:, n:S]).then_inc(inv_ready, 1)
                dve.wait_ge(inv_ready, invs[0])

            n_norms = [0]

            def scales(diags):
                n = len(diags)
                dve.wait_ge(norm_std, n_norms[0] + n)
                r = norm_col[:, 0:n, :]
                link(dve.reciprocal(r, r))
                for j, diag in enumerate(diags):
                    dve.tensor_tensor(diag.rearrange("p (c t) -> p c t", c=NT),
                                      ident[:, :].unsqueeze(1).broadcast_to([P, NT, P]),
                                      norm_col[:, j, :].unsqueeze(2).broadcast_to([P, NT, P]),
                                      ALU.mult).then_inc(norm_diag, 1)
                n_norms[0] += n

            def free(ins):
                frees[0] += 1
                ins.then_inc(dve_freed, 1)

            def silu(dst, t):
                evs[0] += 1
                dve.wait_ge(ev_ready, evs[0])
                free(dve.tensor_tensor(dst, bank[t["bank"]][:, :], ev[:, (evs[0] - 1) % 2, :], ALU.mult))
                dve.wait_ge(dve_freed, frees[0])
                dve.sem_inc(ev_used, 1)

            def rows_out(tiles, dst):
                for i in (1, 3):
                    dve.wait_ge(dense_done, tiles[i]["full"])
                    free(dve.tensor_copy(dst(i), bank[tiles[i]["bank"]][:, :]))

            dve.memset(ones[:, :], 1.0).then_inc(ones_ready, 1)
            dve.wait_ge(vecs_in, 16)
            dve.wait_ge(squares_in, 16)
            scales([u_diag[:, :]])
            dve.wait_ge(norm_spread, 1)
            split(KD, lambda i: dve.scalar_tensor_tensor(u_val[:, i % 2, :], xt[:, i, :], vec("norm_in", i),
                                                         bank[5][:, :], ALU.mult, ALU.mult),
                  lambda i: u_val[:, i % 2, :], lambda i: u_hi[:, i, :], lambda i: u_lo[:, i, :])
            dve.wait_ge(iw_ready, 1)
            n = 0
            for ti in range(1, NT):
                W = (ti + 1) * P
                sc = score[:, ti - 1, 0:W]
                for h in range(IH):
                    dve.wait_ge(idx_relu, n + 1)
                    w = iw[:, ti - 1, h:h + 1]
                    if h == 0:
                        dve.tensor_scalar(sc, relu[:, n % 2, 0:W], w, None, ALU.mult).then_inc(idx_added, 1)
                    else:
                        dve.wait_ge(idx_added, n)
                        dve.scalar_tensor_tensor(sc, relu[:, n % 2, 0:W], w, sc, ALU.mult,
                                                 ALU.add).then_inc(idx_added, 1)
                    n += 1
                dve.wait_ge(idx_added, n)
                d = score[:, ti - 1, ti * P:W]
                link(dve.tensor_tensor(d, d, tri[:, :], ALU.add))

            def wk(ti):
                return work[:, ti - 1, 0:(ti + 1) * P] if ti < 3 else work2[:, :]

            for ti in range(1, NT):
                dve.tensor_copy(wk(ti), score[:, ti - 1, 0:(ti + 1) * P]).then_inc(top_gone, 1)
            rounds = TOPK // 8 - 1
            for r in range(rounds):
                for ti in range(1, NT):
                    dve.wait_ge(top_gone, 3 * r + ti)
                    dve.max(top8[:, ti - 1, :], wk(ti)).then_inc(top_found, 1)
                for ti in range(1, NT):
                    dve.wait_ge(top_found, 3 * r + ti)
                    dve.match_replace(wk(ti), top8[:, ti - 1, :], wk(ti), -3e38).then_inc(top_gone, 1)
            for ti in range(1, NT):
                dve.wait_ge(top_gone, 3 * rounds + ti)
                dve.max(top8[:, ti - 1, :], wk(ti)).then_inc(top_found, 1)
            dve.tensor_copy(chosen[:, 0, 0:P], tri[:, :]).then_inc(chosen_ready, 1)
            for ti in range(1, NT):
                W = (ti + 1) * P
                dve.wait_ge(top_found, 3 * rounds + ti)
                sc, th = score[:, ti - 1, 0:W], top8[:, ti - 1, 7:8]
                gt, eq, cs = relu[:, 0, 0:W], relu[:, 1, 0:W], wk(ti)
                cnt, need = tk[:, ti - 1, 0:1], tk[:, ti - 1, 1:2]
                link(dve.tensor_scalar(gt, sc, th, 0.0, ALU.is_gt, ALU.add, accum_out=cnt))
                link(dve.tensor_scalar(need, cnt, -1.0, float(TOPK), ALU.mult, ALU.add))
                link(dve.tensor_scalar(eq, sc, th, None, ALU.is_equal))
                link(dve.tensor_tensor_scan(cs, ones[:, 0:W], eq, 0.0, ALU.mult, ALU.add))
                link(dve.scalar_tensor_tensor(eq, cs, need, eq, ALU.is_le, ALU.mult))
                link(dve.tensor_tensor(gt, gt, eq, ALU.add))
                dve.tensor_scalar(chosen[:, ti, 0:W], gt, -NEG, NEG, ALU.mult, ALU.add).then_inc(chosen_ready, 1)
                dve.wait_ge(chosen_ready, ti + 1)

            dve.tensor_copy(r_f[:, :], small[32:32 + MH, :]).then_inc(ml_f, 1)
            rows_out(st["att_v"], lambda i: att_v[:, i, :])
            dve.wait_ge(ml_log, 1)
            link(dve.scalar_tensor_tensor(r_lf[:, :], r_f[:, :], 0.0, r_t[:, :], ALU.min, ALU.subtract))
            link(dve.tensor_tensor_scan(r_b[:, :], ones[0:MH, :], r_lf[:, :], 0.0, ALU.mult, ALU.add))
            link(dve.tensor_tensor(r_a[:, :], small[0:MH, :], r_b[:, :], ALU.subtract))
            dve.sem_inc(rows_ready, 1)
            link(dve.tensor_tensor_scan(r_m[:, :], ones[0:MH, :], r_a[:, :], 0.0, ALU.mult, ALU.max))
            for stack, first in ((stack_m, True), (stack_f, False)):
                if first:
                    link(dve.tensor_scalar(r_n[:, :], r_m[:, :], -1.0, None, ALU.mult))
                else:
                    link(dve.scalar_tensor_tensor(r_n[:, :], r_b[:, :], -1.0, r_m[:, :], ALU.mult, ALU.subtract))
                link(dve.memset(stack[:, :], 0.0))
                link(dve.tensor_copy(stack[0:MH, :], r_n[:, :]))
                link(dve.tensor_tensor(r_n[:, :], r_n[:, :], stack[0:MH, :], ALU.subtract))
                link(dve.tensor_copy(r_p[:, 0, :], r_n[:, :]))
                link(dve.tensor_copy(stack[32:32 + MH, :], r_p[:, 0, :]))
                link(dve.tensor_tensor(r_n[:, :], r_n[:, :], r_p[:, 0, :], ALU.subtract))
                dve.tensor_copy(stack[64:64 + MH, :], r_n[:, :]).then_inc(stack_ready, 1)
                dve.wait_ge(stack_ready, 1 if first else 2)
            for half in range(2):
                rows_out(st["mem_v"][4 * half:4 * half + 4], lambda i: mem_v[:, i, half * S:(half + 1) * S])
            dve.wait_ge(stored, 16)
            for i, t in enumerate(st["att_z"]):
                silu(att_z[:, i, :], t)

            def bias_and_mask(n):
                if n >= len(units):
                    return
                h, ti = units[n]
                W = (ti + 1) * P
                if ti == 0:
                    dve.wait_ge(hank_in[h % 2], 16 * (h // 2 + 1))
                if n >= 2:
                    dve.wait_ge(da_max, n - 1)
                dve.tensor_tensor(biased[:, n % 2, 0:W], hank[:, h % 2, S - W:S], chosen[:, ti, 0:W],
                                  ALU.add).then_inc(da_bias, 1)

            def masked(n):
                h, ti = units[n]
                W = (ti + 1) * P
                dve.wait_ge(da_bias, n + 1)
                if n >= 3:
                    dve.wait_ge(da_turn, n - 2)
                dve.wait_ge(da_logits, n + 1)
                link(dve.tensor_tensor_reduce(out=probs[:, n % 3, 0:W], in0=bank[4 + n % 2][:, 0:W],
                                              in1=biased[:, n % 2, 0:W], scale=1.0, scalar=-3e38, op0=ALU.add,
                                              op1=ALU.max, accum_out=da_cols[:, 0, n:n + 1]))
                dve.tensor_scalar(da_cols[:, 1, n:n + 1], da_cols[:, 0, n:n + 1], -(ADH ** -0.5), None,
                                  ALU.mult).then_inc(da_max, 1)

            def weighed(n):
                h, ti = units[n]
                dve.wait_ge(da_probs, n + 1)
                link(dve.reciprocal(da_cols[:, 3, n:n + 1], da_cols[:, 2, n:n + 1]))
                dve.wait_ge(da_sum, n + 1)
                dve.tensor_scalar(att_o[:, ti, h * ADH:(h + 1) * ADH], bank[7][:, 0:ADH], da_cols[:, 3, n:n + 1],
                                  None, ALU.mult).then_inc(da_out, 1)

            def older_tap(i, back):
                t = st["mem_qk"][i]
                if back == 1:
                    evs[0] += 1
                    dve.wait_ge(ev_ready, evs[0])
                e, b = ev[:, (evs[0] - 1) % 2, :], bank[t["bank"]]
                if back < 3:
                    link(dve.scalar_tensor_tensor(e[:, back:S], b[:, 0:S - back], vec("conv_w", 4 * i + 3 - back),
                                                  e[:, back:S], ALU.mult, ALU.add))
                    return
                link(dve.scalar_tensor_tensor(mem_qk[:, i, 3:S], b[:, 0:S - 3], vec("conv_w", 4 * i),
                                              e[:, 3:S], ALU.mult, ALU.add))
                free(dve.tensor_copy(mem_qk[:, i, 0:3], e[:, 0:3]))
                dve.wait_ge(dve_freed, frees[0])
                dve.sem_inc(taps_ready, 1)
                dve.sem_inc(ev_used, 1)

            def conv_silu(i):
                m = mem_qk[:, i, :]
                dve.wait_ge(sg_ready, i + 1)
                dve.tensor_tensor(m, m, sg[:, :], ALU.mult).then_inc(mem_qk_ready, 1)

            bias_and_mask(0)
            bias_and_mask(1)
            masked(0)
            masked(1)
            bias_and_mask(2)
            for n, (h, ti) in enumerate(units):
                if n + 2 < len(units):
                    masked(n + 2)
                bias_and_mask(n + 3)
                if n:
                    weighed(n - 1)
                if ti == 0 and h >= 2:
                    conv_silu(h - 2)
                if ti < 3 and h:
                    older_tap(h - 1, ti + 1)
            weighed(len(units) - 1)
            conv_silu(AH - 2)

            def gated_out(i):
                dve.wait_ge(da_back, i + 1)
                return dve.tensor_tensor(val_m[:, i % 2, :], bank[6 + i % 2][:, :], att_z[:, i, :], ALU.mult)

            split(4, gated_out, lambda i: val_m[:, i % 2, :], lambda i: mixa_hi[:, i, :], lambda i: mixa_lo[:, i, :])

            for back in (1, 2, 3):
                older_tap(AH - 1, back)

            oz = st["mem_oz"]

            def out_gate(i):
                o = mem_o[:, i, :]
                t = oz[2 * i + 1]
                dve.wait_ge(act_freed, oz[2 * i]["freed"][1])
                evs[0] += 1
                dve.wait_ge(ev_ready, evs[0])
                e = ev[:, (evs[0] - 1) % 2, :]
                link(dve.tensor_tensor(o, o, e, ALU.mult))
                dve.sem_inc(ev_used, 1)
                free(dve.tensor_tensor(o, o, bank[t["bank"]][:, :], ALU.mult))
                dve.wait_ge(dve_freed, frees[0])

            for h in range(MH):
                dve.wait_ge(ml_decay, h + 1)
                for j in range(NT):
                    n = NT * h + j
                    dve.wait_ge(ml_score, n + 1)
                    dve.scalar_tensor_tensor(e_t(h, j), bank[4 + j % 2][:, 0:S - j * P], MQK ** -0.5, e_t(h, j),
                                             ALU.mult, ALU.mult).then_inc(ml_weight, 1)
                if h == 0:
                    conv_silu(AH - 1)
                out_gate(2 * h)
                dve.wait_ge(ml_floor, 2 * h + 2)
                link(dve.tensor_tensor(den[:, :], den[:, :], floor[:, :], ALU.max))
                link(dve.reciprocal(inv_den[:, :], den[:, :]))
                for v in range(2):
                    dve.wait_ge(ml_values, 2 * h + v + 1)
                    dve.tensor_tensor(h_val[:, v, :], bank[6 + v][:, :], inv_den[:, :], ALU.mult).then_inc(ml_h, 1)
                inverse(inv_m, std_m)
                out_gate(2 * h + 1)

                def gated(i):
                    v = val_m[:, i, :]
                    link(dve.scalar_tensor_tensor(v, h_val[:, i, :], vec("m_norm", 2 * h + i), inv_m[:, :],
                                                  ALU.mult, ALU.mult))
                    return dve.tensor_tensor(v, v, mem_o[:, 2 * h + i, :], ALU.mult)

                split(2, gated, lambda i: val_m[:, i, :], lambda i: mix_hi[:, 2 * h + i, :],
                      lambda i: mix_lo[:, h + MH * i, :])
            for i in range(2):
                low(p_val[:, i, :], p_hi[:, i, :], p_lo[:, i, :])
            dve.wait_ge(x2_in, 16)
            for i, t in enumerate(st["out"]):
                dve.wait_ge(dense_done, t["full"])
                free(dve.tensor_tensor(h_res[:, i, :], bank[t["bank"]][:, :], xt2[:, i, :], ALU.add))
                dve.wait_ge(dve_freed, frees[0])
                dve.sem_inc(h_res_ready, 1)
                low(h_res[:, i, :], h_hi[:, i, :], h_lo[:, i, :])
            for i, t in enumerate(st["gate"]):
                dve.wait_ge(act_freed, t["freed"][1])
                g = gate[:, i % 2, :]
                link(dve.tensor_tensor(ple[:, i, :], ple[:, i, :], g, ALU.mult))
                dve.tensor_tensor(h_res[:, i, :], h_res[:, i, :], ple[:, i, :], ALU.add).then_inc(ple_added, 1)
            dve.wait_ge(sq_used, KD + 2 * MH + 2 * KD)
            link(dve.tensor_scalar(norm_col[:, 0, :], bank[4][:, 0:NT], EPS, None, ALU.mult))
            dve.tensor_tensor(norm_col[:, 0, :], norm_col[:, 0, :], bank[4][:, NT:2 * NT],
                              ALU.add).then_inc(norm_sums_in, 1)
            n0, n1 = VEC["norm_mix"][0], VEC["norm_final"][0]
            link(dve.tensor_tensor(gain2[:, :], vecs[:, n0:n0 + KD], vecs[:, n1:n1 + KD], ALU.mult))
            scales([x2_diag[:, 0, :], x2_diag[:, 1, :]])
            dve.wait_ge(norm_spread, 2)
            split(KD, lambda i: dve.scalar_tensor_tensor(val_f[:, i % 2, :], h_res[:, i, :], gain2[:, i:i + 1],
                                                         bank[5][:, :], ALU.mult, ALU.mult),
                  lambda i: val_f[:, i % 2, :], lambda i: u2_hi[:, i, :], lambda i: u2_lo[:, i, :])
            dve.wait_ge(norm_spread, 3)
            for i in range(KD):
                dve.scalar_tensor_tensor(h_res[:, i, :], h_res[:, i, :], vec("norm_final", i), bank[6][:, :], ALU.mult,
                                         ALU.mult).then_inc(x2_ready, 1)
            dve.wait_ge(x2_ready, KD)

            def add_taps(acc, b, w, n):
                for back in range(1, n):
                    ins = dve.scalar_tensor_tensor(acc[:, back:S], b[:, 0:S - back], w(n - 1 - back), acc[:, back:S],
                                                   ALU.mult, ALU.add)
                    if back < n - 1:
                        link(ins)
                free(ins)

            def spread_col(i, h0, n):
                return cols[:, i, h0:h0 + n].unsqueeze(2).broadcast_to([P, n, SSD_P])

            dve.wait_ge(dt_log, 1)
            dve.wait_ge(rate_ready, 1)
            link(dve.scalar_tensor_tensor(r_dt[:, :], small2[0:SSD_H, :], 0.0, r_t2[:, :], ALU.max, ALU.add))
            link(dve.tensor_scalar(r_t2[:, :], r_dt[:, :], rate[:, :], -1.0, ALU.mult, ALU.mult))
            for c in range(NT):
                ins = dve.tensor_tensor_scan(r_ac[:, c * P:(c + 1) * P], ones[0:SSD_H, 0:P],
                                             r_t2[:, c * P:(c + 1) * P], 0.0, ALU.mult, ALU.add)
                link(ins)
            dve.sem_inc(acum_ready, 1)
            for c in (1, 2):
                ins = dve.tensor_scalar(ends_diag[:, (c - 1) * SSD_H:c * SSD_H], ident[0:SSD_H, 0:SSD_H],
                                        r_ac[:, (c + 1) * P - 1:(c + 1) * P], None, ALU.mult)
                link(ins)
            dve.sem_inc(stack_a_ready, 1)
            link(dve.tensor_copy(stack_a[0:32, :], r_ac[:, :]))
            link(dve.tensor_tensor(r_n2[:, :], r_ac[:, :], stack_a[0:32, :], ALU.subtract))
            link(dve.tensor_copy(r_p2[:, 0, :], r_n2[:, :]))
            link(dve.tensor_copy(stack_a[32:64, :], r_p2[:, 0, :]))
            link(dve.tensor_tensor(r_n2[:, :], r_n2[:, :], r_p2[:, 0, :], ALU.subtract))
            dve.tensor_copy(stack_a[64:96, :], r_n2[:, :]).then_inc(stack_a_ready, 1)
            dve.wait_ge(stack_a_ready, 2)
            for i in range(len(conv_tiles) + 1):
                if i < len(conv_tiles):
                    t, w, _ = conv_tiles[i]
                    dve.wait_ge(conv_in, i + 1)
                    add_taps(taps[:, i % 2, :], bank[t["bank"]], lambda k: vec("ssd_conv_w", 4 * w + k), 4)
                if i:
                    dve.wait_ge(conv_sg, i)
                    dve.tensor_tensor(conv_tiles[i - 1][2], taps[:, (i - 1) % 2, :], taps_sg[:, (i - 1) % 2, :],
                                      ALU.mult).then_inc(conv_ready, 1)
            dve.wait_ge(conv_ready, len(conv_tiles))
            dve.wait_ge(cols_ready, 3)

            def group_norm(g):
                for i in range(4 * g, 4 * g + 4):
                    dve.scalar_tensor_tensor(y[:, i, :], y[:, i, :], vec("ssd_g", i), inv_y[:, :], ALU.mult,
                                             ALU.mult).then_inc(y_normed, 1)

            for g in range(SSD_G):
                for c in range(NT):
                    n = NT * g + c
                    dve.wait_ge(x_turned, n + 1)
                    x3 = xdt[:, c, :].rearrange("p (h f) -> p h f", f=SSD_P)
                    dve.tensor_tensor(x3, bank[6 + c % 2][:, :].rearrange("p (h f) -> p h f", f=SSD_P),
                                      spread_col(3 * c, 8 * g, 8), ALU.mult).then_inc(xdt_ready, 1)
                    if c < 3:
                        dve.wait_ge(xdt_ready, n + 1)
                        dve.tensor_tensor(xdec[:, c, :].rearrange("p (h f) -> p h f", f=SSD_P), x3,
                                          spread_col(3 * c + 1, 8 * g, 8), ALU.mult).then_inc(xdec_ready, 1)
                for c in range(3):
                    dve.wait_ge(state_dot, 3 * g + c + 1)
                    if c == 0:
                        dve.tensor_copy(states[:, 0, :], bank[6][:, :]).then_inc(state_ready, 1)
                    else:
                        dve.wait_ge(state_ready, 3 * g + c)
                        for e in range(8):
                            f, h = slice(e * SSD_P, (e + 1) * SSD_P), (c - 1) * SSD_H + 8 * g + e
                            ins = dve.scalar_tensor_tensor(states[:, c, f], states[:, c - 1, f],
                                                           chunk_decay[:, h:h + 1], bank[6 + c % 2][:, f], ALU.mult,
                                                           ALU.add)
                        ins.then_inc(state_ready, 1)
                for p in range(4 * g, 4 * g + 4):
                    for h in (2 * p, 2 * p + 1):
                        dve.wait_ge(l_ready, h + 1)
                        dve.wait_ge(grp_copied, 2 * g + 1)
                        dve.tensor_tensor(weight(h), weight(h), scores[:, :], ALU.mult).then_inc(w_ready, 1)
                    if g and p % 4 == 3:
                        last_inverses(inv_y, std_y, S // 2)
                    yp, e = y[:, p, :], e_ac[:, p % 2, P:S]
                    dve.wait_ge(z_ready, p + 1)
                    free(dve.tensor_tensor(z_sg[:, :], z_sg[:, :], bank[st["z"][p]["bank"]][:, :], ALU.mult))
                    dve.wait_ge(y_dot, 2 * p + 2)
                    link(dve.scalar_tensor_tensor(yp, yp, vec("d_skip", p), bank[6][:, :], ALU.mult, ALU.add))
                    dve.wait_ge(off_dot, p + 1)
                    dve.wait_ge(e_ready, p + 1)
                    dve.tensor_tensor(e, bank[7][:, P:S], e, ALU.mult).then_inc(y_read, 1)
                    dve.wait_ge(y_read, p + 1)
                    link(dve.tensor_tensor(yp[:, P:S], yp[:, P:S], e, ALU.add))
                    dve.wait_ge(dve_freed, frees[0])
                    dve.tensor_tensor(yp, yp, z_sg[:, :], ALU.mult).then_inc(y_ready, 1)
                    if g and p % 4 == 2:
                        if g >= 2:
                            dve.wait_ge(y_normed, 4 * g - 4)
                        first_inverses(inv_y, std_y, S // 2)
                    if g >= 2 and p % 4 == 0:
                        group_norm(g - 2)
            group_norm(SSD_G - 2)

            def y_low(first, end):
                dve.wait_ge(y_normed, end)
                for i in range(first, end):
                    low(y[:, i, :], y_hi[:, i, :], y_lo[:, i, :])

            y_low(0, 4)
            dve.wait_ge(y_ready, 16)
            dve.wait_ge(y_normed, 12)
            inverse(inv_y, std_y)
            group_norm(3)
            y_low(4, 16)
            inverse(inv_s, std_s)
            split(2, lambda i: dve.scalar_tensor_tensor(qa_val[:, i, :], qa_val[:, i, :], vec("qa_g", i), inv_s[:, :],
                                                        ALU.mult, ALU.mult),
                  lambda i: qa_val[:, i, :], lambda i: qn_hi[:, i, :], lambda i: qn_lo[:, i, :])
            inverse(inv_s, std_s)
            split(1, lambda i: dve.scalar_tensor_tensor(kva_val[:, :], kva_val[:, :], vec("kva_g"), inv_s[:, :],
                                                        ALU.mult, ALU.mult),
                  lambda i: kva_val[:, :], lambda i: kn_hi[:, :], lambda i: kn_lo[:, :])

            def gain(name, r0, r1):
                return vecs[r0:r1, VEC[name][0]:VEC[name][0] + 1]

            link(dve.scalar_tensor_tensor(rope[96:P, :], small2[96:P, :], gain("k_g", 96, P), trig[96:P, :], ALU.mult,
                                          ALU.mult))
            link(dve.tensor_copy(rk_diag[64:96, :], rope[96:P, :]))
            link(dve.scalar_tensor_tensor(rope[64:96, :], small2[64:96, :], gain("k_g", 64, 96), trig[64:96, :],
                                          ALU.mult, ALU.mult))
            link(dve.tensor_tensor(rope[64:96, :], rope[64:96, :], rk_diag[64:96, :], ALU.add))

            def head_features(h):
                b = bank[st["head_q"][h]["bank"]]
                dve.wait_ge(head_sq, 2 * h + 1)
                dve.tensor_scalar(q_s[0:64, h % 2, :], b[0:64, :], gain("q_g", 0, 64), None, ALU.mult)
                link(dve.scalar_tensor_tensor(rope[96:P, :], b[96:P, :], gain("q_g", 96, P), trig[96:P, :], ALU.mult,
                                              ALU.mult))
                link(dve.scalar_tensor_tensor(b[64:96, :], b[64:96, :], gain("q_g", 64, 96), trig[64:96, :], ALU.mult,
                                              ALU.mult))
                free(dve.tensor_tensor(q_s[64:96, h % 2, :], b[64:96, :], rope[96:P, :], ALU.add))
                dve.wait_ge(head_sq, 2 * h + 2)
                if h:
                    dve.wait_ge(k_ready, h)
                free(dve.tensor_scalar(rope[0:64, :], bank[st["head_k"][h]["bank"]][0:64, :], gain("k_g", 0, 64), None,
                                       ALU.mult))
                dve.wait_ge(dve_freed, frees[0])

            def head_scales(h):
                r = r_qk[:, h % 2, :]
                dve.wait_ge(std_qk_ready, 2 * h + 2)
                dve.reciprocal(r, r).then_inc(r_qk_ready, 1)
                dve.wait_ge(r_qk_ready, h + 1)
                if h:
                    dve.wait_ge(rk_spread, h)
                dve.tensor_tensor(rk_diag[:, :].rearrange("p (c t) -> p c t", c=NT),
                                  ident[:, :].unsqueeze(1).broadcast_to([P, NT, P]),
                                  r[:, NT:2 * NT].unsqueeze(2).broadcast_to([P, NT, P]),
                                  ALU.mult).then_inc(rk_diag_ready, 1)

            def head_keys(h):
                dve.wait_ge(rk_spread, h + 1)
                dve.tensor_tensor(k_s[:, h % 2, :], rope[0:QK, :], bank[2][0:QK, :], ALU.mult).then_inc(k_ready, 1)

            def head_max(n):
                h, ti = heads[n]
                dve.wait_ge(x_logits, n + 1)
                link(dve.reduce_max(x_cols[:, 0, n:n + 1], bank[4 + n % 2][:, 0:(ti + 1) * P], AX_X))
                dve.tensor_scalar(x_cols[:, 1, n:n + 1], x_cols[:, 0, n:n + 1], r_qk[:, h % 2, ti:ti + 1], -1.0,
                                  ALU.mult, ALU.mult).then_inc(x_max, 1)

            def head_out(n):
                h, ti = heads[n]
                dve.wait_ge(x_probs, n + 1)
                link(dve.reciprocal(x_cols[:, 3, n:n + 1], x_cols[:, 2, n:n + 1]))
                dve.wait_ge(x_sum, n + 1)
                dve.tensor_scalar(o_tok[:, ti, h * VD:(h + 1) * VD], bank[7][:, 0:VD], x_cols[:, 3, n:n + 1],
                                  None, ALU.mult).then_inc(x_out, 1)

            def values_out(half):
                rows_out(st["v"][4 * half:4 * half + 4], lambda i: v_tok[:, i, half * S:(half + 1) * S])

            head_features(0)
            values_out(0)
            head_scales(0)
            values_out(1)
            head_keys(0)
            head_max(0)
            head_max(1)
            head_features(1)
            for n, (h, ti) in enumerate(heads):
                if n + 2 < len(heads):
                    head_max(n + 2)
                if ti == 0 and h + 1 < XH:
                    head_scales(h + 1)
                if ti == 1 and h + 1 < XH:
                    head_keys(h + 1)
                if ti == 3 and h + 2 < XH:
                    head_features(h + 2)
                if ti == 3 and 1 <= h <= KD:
                    dve.wait_ge(act_freed, st["mix_gate"][h - 1]["freed"][1])
                    dve.tensor_tensor(y_ssd[:, h - 1, :], y_ssd[:, h - 1, :], gm[:, h - 1, :],
                                      ALU.mult).then_inc(gates_used, 1)
                if n:
                    head_out(n - 1)
            head_out(len(heads) - 1)
            dve.wait_ge(gates_used, KD)
            for i in range(KD):
                low(bank[6 + i % 2][:, :], o_hi[:, i, :], o_lo[:, i, :])

            def fuse(i):
                t = st["mla_out"][i]
                dve.wait_ge(dense_done, t["full"])
                if i == 0:
                    dve.wait_ge(act_freed, st["mix_gate"][-1]["freed"][1])
                free(dve.tensor_tensor(gm[:, i, :], gm[:, i, :], bank[t["bank"]][:, :], ALU.mult))
                dve.wait_ge(dve_freed, frees[0])
                return dve.tensor_tensor(gm[:, i, :], gm[:, i, :], y_ssd[:, i, :], ALU.add)

            split(KD, fuse, lambda i: gm[:, i, :], lambda i: fused_hi[:, i, :], lambda i: fused_lo[:, i, :])
            for i, t in enumerate(st["mix_out"]):
                dve.wait_ge(dense_done, t["full"])
                free(dve.tensor_tensor(h_res[:, i, :], h_res[:, i, :], bank[t["bank"]][:, :], ALU.add))
            dve.wait_ge(dve_freed, frees[0])
            scales([x3_diag[:, :]])
            dve.wait_ge(norm_spread, 4)
            split(KD, lambda i: dve.scalar_tensor_tensor(val_x[:, i % 2, :], h_res[:, i, :], vec("norm_ffn", i),
                                                         bank[5][:, :], ALU.mult, ALU.mult),
                  lambda i: val_x[:, i % 2, :], lambda i: u3_hi[:, i, :], lambda i: u3_lo[:, i, :])
            s0, v0, h0 = steps[0], vals[0], his[0]

            def step(ins, n):
                ins.then_inc(dve_step, 1)
                dve.wait_ge(dve_step, n + s0)

            def up_tile(g, j, n):
                acc, b = (ffn_g, ffn_v)[j % 2][:, j // 2, :], bank[j]
                dve.wait_ge(act_in, 4 * g + (j + 1))
                step(dve.scalar_tensor_tensor(acc[:, 1:S], b[:, 0:S - 1], up_vec("ffn_conv_w", 12 * g + (3 * j + 1)),
                                              acc[:, 1:S], ALU.mult, ALU.add), n)
                dve.scalar_tensor_tensor(acc[:, 2:S], b[:, 0:S - 2], up_vec("ffn_conv_w", 12 * g + 3 * j),
                                         acc[:, 2:S], ALU.mult, ALU.add).then_inc(dve_freed, 1)

            def up_pair(k, b, n):
                g2, v2 = ffn_g[:, b, :], ffn_v[:, b, :]
                dve.wait_ge(act_sg, k + 1)
                dve.wait_ge(dve_freed, 2 * k + (up_freed + 1))
                step(dve.tensor_tensor(v2, v2, g2, ALU.mult), n)
                dve.tensor_tensor(g2, v2, ffn_sg[:, b, :], ALU.mult).then_inc(val_ready, 1)
                dve.wait_ge(val_ready, k + (v0 + 1))
                dve.wait_ge(hi_ready, k + (h0 + 1))
                hi, lo = (x[:, bass.ds(k, 1), :].rearrange("p a n -> p (a n)") for x in (act_hi, act_lo))
                dve.tensor_tensor(lo, g2, hi.bitcast(F32), ALU.subtract).then_inc(lo_ready, 1)

            for j in range(4):
                up_tile(0, j, (1, 2, 3, 5)[j])
                if j == 2:
                    up_pair(0, 0, 4)
            with dve.Fori(1, UP_LOOPS) as g:
                for j in range(4):
                    up_tile(g, j, 6 * g + (0, 2, 3, 5)[j])
                    if j == 0:
                        up_pair(2 * g - 1, 1, 6 * g + 1)
                    if j == 2:
                        up_pair(2 * g, 0, 6 * g + 4)
            up_pair(FT - 1, 1, 6 * UP_LOOPS)
            steps[0] += 6 * UP_LOOPS
            frees[0] += len(up)
            vals[0] += FT
            his[0] += FT
            for i, t in enumerate(st["down"]):
                dve.wait_ge(dense_done, t["full"])
                free(dve.tensor_tensor(h_res[:, i, :], h_res[:, i, :], bank[t["bank"]][:, :], ALU.add))



def _columns(w, n_k):
    k, n = w.shape
    return w.reshape(n_k, P, n // P, P).transpose(2, 0, 1, 3).reshape(-1, P, P)


def _rows(w, n_k):
    k, n = w.shape
    return w.reshape(n_k, P, n // S, S // P, P).transpose(2, 0, 3, 1, 4).reshape(-1, P, P)


def _chunks(*parts):
    out = []
    for tiles in parts:
        n = -(-len(tiles) // CH) * CH
        t = np.zeros((n, P, P), np.float32)
        t[:len(tiles)] = tiles
        out.append(t)
    t = np.concatenate(out)
    return np.ascontiguousarray(t.reshape(-1, CH, P, P).transpose(0, 2, 1, 3).reshape(-1, P, CH * P))


def _col(v):
    return np.ascontiguousarray(v).reshape(-1, P).T


def _put(rows, *pieces):
    first = pieces[0][1]
    out = np.zeros((P,) + first.shape[1:], np.float32)
    for r, v in pieces:
        out[r:r + len(v)] = v
    return out


def _bucket(dist):
    half = BUCKETS // 2
    large = half + (np.log(np.maximum(dist, 1).astype(np.float32) / np.float32(half))
                    / np.float32(np.log(128 / half)) * np.float32(BUCKETS - half)).astype(np.int32)
    return np.where(dist < half, dist, np.minimum(large, BUCKETS - 1))


def layout(i):
    i = {k: np.asarray(v) for k, v in i.items()}
    bf = mybir.dt.np(BF16)
    a = {}
    w = i["w_in"][0]
    cut = np.cumsum([512, 512, 1024, 1024, 1024, 8, 512, 512, 512, 512, 512, 64, 8])
    mq, mk, mv, mo, mz, mif, aq, ak, av, az, ixq, ixk, ixw = np.split(w, cut[:-1], axis=1)
    small = np.zeros((D, P), np.float32)
    small[:, 0:4], small[:, 32:36], small[:, 64:72] = mif[:, 0:4], mif[:, 4:8], ixw
    oz = np.stack([mo.reshape(D, 8, P), mz.reshape(D, 8, P)], 2).reshape(D, 16 * P)
    parts = [_columns(x, KD) for x in (ixq, np.concatenate([ixk, ixk], 1), small, aq, ak)]
    parts += [_rows(av, KD), _rows(mv, KD), _columns(az, KD), _columns(np.concatenate([mq, mk], 1), KD),
              _columns(oz, KD), _columns(np.concatenate([i["w_out"][0, MH * MV:], i["w_out"][0, :MH * MV]]), 12), _columns(i["w_ple"][0], 2),
              _columns(i["w_ple_gate"][0], KD)]
    w = i["w_in_2"][0]
    cut = np.cumsum([2048, 2048, 512, 512, 32, 256, 128, 32, 2048])
    wz, wx, wb, wc, wdt, wqa, wkva, wkr, wgate = np.split(w, cut[:-1], axis=1)
    small2 = np.zeros((D, P), np.float32)
    small2[:, 0:32], small2[:, 64:96], small2[:, 96:112], small2[:, 112:128] = wdt, wkr, wkr[:, 16:], wkr[:, :16]
    parts += [_columns(x, KD) for x in (small2, wb, wc, wx, wz, wqa, wkva)]
    parts.append(_columns(i["w_ssd_proj_2"][0], 16))
    ukv = i["w_ukv_2"][0].reshape(P, XH, NOPE + VD)
    uq = i["w_uq_2"][0].reshape(2, P, XH, QK)
    wq = np.concatenate([uq, uq[..., 80:96], uq[..., 64:80]], axis=-1).transpose(2, 0, 1, 3)
    wk = np.concatenate([ukv[:, :, :NOPE], np.zeros_like(ukv[:, :, :NOPE])], axis=2).transpose(1, 0, 2)[:, None]
    wqk = np.concatenate([wq, wk], axis=1)
    gates = _columns(wgate, KD).reshape(XH, KD, P, P)
    parts.append(wqk[0:2].reshape(6, P, P))
    parts.append(_rows(np.ascontiguousarray(ukv[:, :, NOPE:]).reshape(P, XH * VD), 1))
    for h in range(XH):
        parts.append(gates[h])
        if h % 2 == 0 and h + 2 < XH:
            parts.append(wqk[h + 2:h + 4].reshape(6, P, P))
    up = i["w_up_2"][0].reshape(D, 2, FT, P).transpose(0, 2, 1, 3).reshape(D, 2 * FT * P)
    parts += [_columns(x, KD) for x in (i["w_mla_proj_2"][0], i["w_o_2"][0], up)]
    parts.append(_columns(i["w_down_2"][0], FT))
    a["weights"] = _chunks(*parts)
    a["x_t"] = np.ascontiguousarray(i["x"][0].T.reshape(KD, P, S).transpose(1, 0, 2))
    a["p_t"] = np.ascontiguousarray(i["p"][0, 0].T.reshape(2, P, S).transpose(1, 0, 2))
    e, r = np.eye(P, dtype=np.float32), np.arange(P)
    tri = np.where(r[None, :] > r[:, None], np.float32(NEG), np.float32(0))
    a["squares_f"] = np.concatenate([e, tri], axis=1)
    a["squares_b"] = np.concatenate([e, tri.T, tri.T, tri.T, tri.T], axis=1).astype(bf)
    a["sel_m"] = np.repeat(np.tile(np.eye(32, dtype=np.float32)[:, :MH], (3, 1)), P, axis=1).astype(bf)
    d = S - 1 - np.arange(HANK)
    buckets = ((_bucket(np.maximum(d, 0))[None] == np.arange(BUCKETS)[:, None]) & (d >= 0)).astype(np.float32)
    a["by_bucket"] = np.concatenate([i["rel_bias"], buckets], axis=1)
    v = {n: np.zeros((P, c), np.float32) for n, (_, c) in VEC.items()}
    v["norm_in"], v["m_norm"] = _col(i["norm_in"][0]), _col(i["m_norm"][0])
    v["conv_w"] = i["conv_w"][0].reshape(4, 8, P).transpose(2, 1, 0).reshape(P, 32)
    v["gate_bias"][0:4, 0], v["gate_bias"][32:36, 0] = i["b_gate"][0, 0:4], i["b_gate"][0, 4:8]
    v["gate_scale"][:] = 1
    v["gate_scale"][64:72] = IH ** -0.5
    v["norm_final"], v["eps"][:] = _col(i["norm_final"]), EPS
    v["eps_q"][:], v["eps2"][:] = QK * EPS, EPS * EPS
    v["norm_mix"] = _col(i["norm_mix_g_2"][0])
    v["ssd_conv_w"] = i["conv_ssd_w_2"][0].reshape(4, 24, P).transpose(2, 1, 0).reshape(P, 96)
    v["ssd_conv_b"], v["ssd_g"] = _col(i["conv_ssd_b_2"][0]), _col(i["ssd_norm_g_2"][0])
    v["dt_bias"][0:32, 0], v["a_log"][0:32, 0] = i["dt_bias_2"][0], i["a_log_2"][0]
    v["d_skip"] = _col(np.repeat(i["d_skip_2"][0], SSD_P))
    v["qa_g"], v["kva_g"] = _col(i["q_a_norm_g_2"][0]), _col(i["kv_a_norm_g_2"][0])
    for name in ("q_g", "k_g"):
        g = i[name[0] + "_norm_g_2"][0]
        v[name][:, 0] = np.concatenate([g, g[80:96], g[64:80]])
    v["gate_b"], v["norm_ffn"] = _col(i["gate_b_2"][0]), _col(i["norm_ffn_g_2"][0])
    v["ffn_conv_w"] = i["conv_ffn_w_2"][0].reshape(3, 2, FT, P).transpose(3, 2, 1, 0).reshape(P, 6 * FT)
    v["ffn_conv_b"] = i["conv_ffn_b_2"][0].reshape(2, FT, P).transpose(2, 1, 0).reshape(P, 2 * FT)
    a["one_hot"] = np.tile(np.eye(SSD_H, dtype=np.float32), (3, 1)).astype(bf)
    inv = 1.0 / (np.float32(10000.0) ** (np.arange(0, ROPE, 2, dtype=np.float32) / np.float32(ROPE)))
    ang = np.arange(S, dtype=np.float32)[None, :] * inv.astype(np.float32)[:, None]
    a["trig"] = np.zeros((P, S), np.float32)
    a["trig"][64:] = np.concatenate([np.cos(ang), np.cos(ang), -np.sin(ang), np.sin(ang)])
    a["tri_b"] = tri.astype(bf)
    a["vecs"] = np.ascontiguousarray(np.concatenate([v[n] for n in VEC], axis=1))
    return a


def kernel(**inputs):
    import concourse.bacc as _bacc
    from concourse.bass_utils import run_bass_kernel_spmd as _run

    arrays = layout(inputs)
    nc = _bacc.Bacc("TRN2", target_bir_lowering=False, num_devices=1)
    aps = {name: nc.dram_tensor(name, v.shape, mybir.dt.from_np(v.dtype), kind="ExternalInput").ap()
           for name, v in arrays.items()}
    out = nc.dram_tensor("out", (P, KD, S), F32, kind="ExternalOutput").ap()
    build(nc, aps, out)
    r = _run(nc, [arrays], core_ids=[0])
    return np.ascontiguousarray(r.results[0]["out"].transpose(1, 0, 2).reshape(1, D, S).transpose(0, 2, 1))
```
